# Optimizing a Trainium2 kernel written in Bass

```python
import math
import jax, jax.numpy as jnp
from jax import lax
import numpy as np

D_MODEL = 2048
BATCH = 1
SEQ = 512
DEPTH = 2

CHUNK = 64
EPS = 1e-6

NUM_BUCKETS = 32
MAX_DISTANCE = 1024
N_ATTN_HEADS = 16

A_HEADS = N_ATTN_HEADS
A_KV_HEADS = 4
A_HEAD_DIM = D_MODEL // 32
A_WIDTH = A_HEADS * A_HEAD_DIM
A_KV_WIDTH = A_KV_HEADS * A_HEAD_DIM
A_WINDOW = 128

B_HEADS = 4
B_QK_DIM = D_MODEL // 16
B_V_DIM = D_MODEL // 8
B_QK_WIDTH = B_HEADS * B_QK_DIM
B_V_WIDTH = B_HEADS * B_V_DIM
B_CONV = 4

C_HEADS = N_ATTN_HEADS
C_HEAD_DIM = D_MODEL // 16
C_WIDTH = C_HEADS * C_HEAD_DIM
C_LATENT = D_MODEL // 4
C_IDX_HEADS = 8
C_IDX_DIM = D_MODEL // 32
C_TOPK_MAX = 256
C_QUERY_BLOCK = 128

EVEN_WIDTHS = (A_WIDTH, A_KV_WIDTH, A_KV_WIDTH, A_WIDTH,
               B_QK_WIDTH, B_QK_WIDTH, B_V_WIDTH, B_HEADS, B_HEADS, B_V_WIDTH, B_V_WIDTH)
EVEN_IN = sum(EVEN_WIDTHS)
EVEN_OUT = A_WIDTH + B_V_WIDTH
ODD_WIDTHS = (C_WIDTH, C_LATENT, C_IDX_HEADS * C_IDX_DIM, C_IDX_DIM, C_IDX_HEADS, C_WIDTH)
ODD_IN = sum(ODD_WIDTHS)

kernel_name = 'hybrid_swa_mlstm_dsa_chunk_causal'

def rms_norm(x, g):
    xf = x.astype(jnp.float32)
    y = xf * lax.rsqrt(jnp.mean(xf * xf, axis=-1, keepdims=True) + EPS)
    return (y * g.astype(jnp.float32)).astype(x.dtype)

def split_cols(h, widths):
    idx = [int(i) for i in np.cumsum(widths)[:-1]]
    return jnp.split(h, idx, axis=-1)

def t5_bucket(rel):
    nb = NUM_BUCKETS // 2
    max_exact = nb // 2
    ret = jnp.where(rel > 0, nb, 0)
    n = jnp.abs(rel)
    large = max_exact + (jnp.log(jnp.maximum(n, 1).astype(jnp.float32) / max_exact)
                         / math.log(MAX_DISTANCE / max_exact) * (nb - max_exact)).astype(jnp.int32)
    large = jnp.minimum(large, nb - 1)
    return ret + jnp.where(n < max_exact, n, large)

def causal_dwconv(x, w, b):
    k = w.shape[0]
    y = lax.conv_general_dilated(x, w[:, None, :].astype(x.dtype), window_strides=(1,),
                                 padding=((k - 1, 0),), dimension_numbers=('NWC', 'WIO', 'NWC'),
                                 feature_group_count=x.shape[-1])
    return y + b

def swa_sink_attention(q, k, v, q_gain, k_gain, sinks, rel_bias):
    bsz, t = q.shape[:2]
    L = CHUNK
    nc = t // L
    P = A_WINDOW // CHUNK - 1
    G = A_HEADS // A_KV_HEADS
    W = (P + 1) * L
    q = rms_norm(q, q_gain)
    k = rms_norm(k, k_gain)
    qc = q.reshape(bsz, nc, L, A_KV_HEADS, G, A_HEAD_DIM)

    def band(z):
        zc = z.reshape(bsz, nc, L, A_KV_HEADS, A_HEAD_DIM)
        zp = jnp.pad(zc, ((0, 0), (P, 0), (0, 0), (0, 0), (0, 0)))
        return jnp.concatenate([zp[:, p:p + nc] for p in range(P + 1)], axis=2)

    kb, vb = band(k), band(v)
    i = jnp.arange(L)
    j = jnp.arange(W)
    rel = j[None, :] - P * L - i[:, None]
    bias = rel_bias[t5_bucket(rel)].transpose(2, 0, 1)
    bias = bias.reshape(A_KV_HEADS, G, L, W).astype(jnp.float32)
    c = jnp.arange(nc)
    valid = (c[:, None] - P + j[None, :] // L) >= 0
    logits = jnp.einsum('bcqhgd,bckhd->bchgqk', qc, kb).astype(jnp.float32) * (A_HEAD_DIM ** -0.5) + bias
    logits = jnp.where(valid[None, :, None, None, None, :], logits, -jnp.inf)
    s = sinks.astype(jnp.float32).reshape(A_KV_HEADS, G)[None, None, :, :, None]
    m = jnp.maximum(logits.max(-1), s)
    e = jnp.exp(logits - m[..., None])
    p = e / (e.sum(-1) + jnp.exp(s - m))[..., None]
    out = jnp.einsum('bchgqk,bckhd->bcqhgd', p.astype(v.dtype), vb)
    return out.reshape(bsz, t, A_WIDTH)

def mlstm_chunkwise(q, k, v, i_pre, f_pre):
    dt = v.dtype
    f32 = jnp.float32
    bsz, t = q.shape[:2]
    L = CHUNK
    nc = t // L

    def heads(z, d):
        return z.astype(f32).reshape(bsz, nc, L, B_HEADS, d).transpose(0, 3, 1, 2, 4)

    q = heads(q, B_QK_DIM) * (B_QK_DIM ** -0.5)
    k = heads(k, B_QK_DIM)
    v = heads(v, B_V_DIM)
    ig = i_pre.astype(f32).reshape(bsz, nc, L, B_HEADS).transpose(0, 3, 1, 2)
    logf = jax.nn.log_sigmoid(f_pre.astype(f32)).reshape(bsz, nc, L, B_HEADS).transpose(0, 3, 1, 2)
    b = jnp.cumsum(logf, axis=-1)
    b_last = b[..., -1]
    g = b_last[..., None] - b + ig
    m_loc = g.max(-1)
    w = jnp.exp(g - m_loc[..., None])
    S = jnp.einsum('bhcs,bhcsv,bhcsk->bhcvk', w, v, k)
    nS = jnp.einsum('bhcs,bhcsk->bhck', w, k)

    def step(carry, inp):
        C, n, m = carry
        s_c, n_c, ml, bl = inp
        m_new = jnp.maximum(bl + m, ml)
        a = jnp.exp(bl + m - m_new)
        bc = jnp.exp(ml - m_new)
        C_new = a[..., None, None] * C + bc[..., None, None] * s_c
        n_new = a[..., None] * n + bc[..., None] * n_c
        return (C_new, n_new, m_new), (C, n, m)

    init = (jnp.zeros((bsz, B_HEADS, B_V_DIM, B_QK_DIM), f32),
            jnp.zeros((bsz, B_HEADS, B_QK_DIM), f32),
            jnp.zeros((bsz, B_HEADS), f32))
    xs = (jnp.moveaxis(S, 2, 0), jnp.moveaxis(nS, 2, 0), jnp.moveaxis(m_loc, 2, 0), jnp.moveaxis(b_last, 2, 0))
    _, (C0, n0, m0) = lax.scan(step, init, xs)
    C0 = jnp.moveaxis(C0, 0, 2)
    n0 = jnp.moveaxis(n0, 0, 2)
    m0 = jnp.moveaxis(m0, 0, 2)
    causal = jnp.tril(jnp.ones((L, L), dtype=bool))
    D = jnp.where(causal, b[..., :, None] - b[..., None, :] + ig[..., None, :], -jnp.inf)
    inter = b + m0[..., None]
    m = jnp.maximum(D.max(-1), inter)
    Pm = jnp.exp(D - m[..., None]) * jnp.einsum('bhctd,bhcsd->bhcts', q, k)
    a = jnp.exp(inter - m)
    num = jnp.einsum('bhcts,bhcsv->bhctv', Pm, v) + a[..., None] * jnp.einsum('bhcvk,bhctk->bhctv', C0, q)
    den = Pm.sum(-1) + a * jnp.einsum('bhck,bhctk->bhct', n0, q)
    h = num / jnp.maximum(jnp.abs(den), jnp.exp(-m))[..., None]
    return h.transpose(0, 2, 3, 1, 4).reshape(bsz, t, B_HEADS, B_V_DIM).astype(dt)

def dsa_attention(q, k, lat, iq, ik, iw, w_uv, rel_bias):
    bsz, t = q.shape[:2]
    qb_len = min(C_QUERY_BLOCK, t)
    nb = t // qb_len
    k_sel = min(C_TOPK_MAX, t // 4)
    k_pos = jnp.arange(t)
    gather = jax.vmap(lambda arr, ind: arr[ind])

    def one_block(args):
        q_b, iq_b, iw_b, t0 = args
        tq = t0 + jnp.arange(qb_len)
        end = (tq // CHUNK + 1) * CHUNK
        sc = jnp.einsum('bqhd,bsd->bqhs', iq_b, ik).astype(jnp.float32) * (C_IDX_DIM ** -0.5)
        score = jnp.einsum('bqhs,bqh->bqs', jax.nn.relu(sc), iw_b.astype(jnp.float32))
        score = jnp.where((k_pos[None, :] < end[:, None])[None], score, -jnp.inf)
        _, idx = lax.top_k(score, k_sel)
        valid = idx < end[None, :, None]
        k_g = gather(k, idx)
        c_g = gather(lat, idx)
        bias = rel_bias[t5_bucket(idx - tq[None, :, None])]
        logits = jnp.einsum('bqhd,bqkd->bqhk', q_b, k_g).astype(jnp.float32) * (C_HEAD_DIM ** -0.5)
        logits = logits + jnp.moveaxis(bias, -1, 2).astype(jnp.float32)
        logits = jnp.where(valid[:, :, None, :], logits, -jnp.inf)
        p = jax.nn.softmax(logits, axis=-1).astype(lat.dtype)
        o = jnp.einsum('bqhk,bqkc->bqhc', p, c_g)
        return jnp.einsum('bqhc,hcd->bqhd', o, w_uv)

    def blocks(z):
        return jnp.moveaxis(z.reshape(bsz, nb, qb_len, *z.shape[2:]), 1, 0)

    xs = (blocks(q), blocks(iq), blocks(iw), jnp.arange(nb, dtype=jnp.int32) * qb_len)
    out = lax.map(one_block, xs)
    return jnp.moveaxis(out, 0, 1).reshape(bsz, t, C_WIDTH)

def even_layer(h, w_in, a_q_norm, a_k_norm, a_sinks, b_conv_w, b_conv_b, b_i_bias, b_f_bias,
               b_out_norm, w_out, rel_bias):
    bsz, t, _ = h.shape
    proj = h @ w_in
    aq, ak, av, az, bq, bk, bv, bi, bf, bo, bz = split_cols(proj, EVEN_WIDTHS)
    a = swa_sink_attention(aq.reshape(bsz, t, A_HEADS, A_HEAD_DIM),
                           ak.reshape(bsz, t, A_KV_HEADS, A_HEAD_DIM),
                           av.reshape(bsz, t, A_KV_HEADS, A_HEAD_DIM),
                           a_q_norm, a_k_norm, a_sinks, rel_bias)
    a = a * jax.nn.silu(az)
    qk = jax.nn.silu(causal_dwconv(jnp.concatenate([bq, bk], axis=-1), b_conv_w, b_conv_b))
    bq, bk = jnp.split(qk, 2, axis=-1)
    hb = mlstm_chunkwise(bq, bk, bv, bi + b_i_bias, bf + b_f_bias)
    hb = rms_norm(hb, b_out_norm.reshape(B_HEADS, B_V_DIM)).reshape(bsz, t, B_V_WIDTH)
    hb = hb * jax.nn.sigmoid(bo) * jax.nn.silu(bz)
    return jnp.concatenate([a, hb], axis=-1) @ w_out

def odd_layer(h, w_in, c_kv_norm, c_w_uk, c_w_uv, c_q_norm, c_k_norm, w_out, rel_bias):
    bsz, t, _ = h.shape
    proj = h @ w_in
    cq, ckv, iq, ik, iw, cz = split_cols(proj, ODD_WIDTHS)
    q = rms_norm(cq.reshape(bsz, t, C_HEADS, C_HEAD_DIM), c_q_norm)
    lat = rms_norm(ckv, c_kv_norm)
    k = rms_norm(lat @ c_w_uk, c_k_norm)
    iq = iq.reshape(bsz, t, C_IDX_HEADS, C_IDX_DIM)
    iw = iw * (C_IDX_HEADS ** -0.5)
    o = dsa_attention(q, k, lat, iq, ik, iw, c_w_uv, rel_bias)
    o = o * jax.nn.silu(cz)
    return o @ w_out

def setup_inputs(seed: int = 0) -> dict:
    key = jax.random.key(seed)
    ks = jax.random.split(key, 24)
    ne = (DEPTH + 1) // 2
    no = DEPTH // 2
    f32 = jnp.float32

    def nrm(k, shape, scale):
        return jax.random.normal(k, shape, f32) * scale

    def gain(k, shape):
        return 1.0 + 0.02 * jax.random.normal(k, shape, f32)

    return {
        'x': nrm(ks[0], (BATCH, SEQ, D_MODEL), 1.0),
        'rel_bias': nrm(ks[1], (NUM_BUCKETS, N_ATTN_HEADS), 0.3),
        'norm_even': gain(ks[2], (ne, D_MODEL)),
        'w_in_even': nrm(ks[3], (ne, D_MODEL, EVEN_IN), D_MODEL ** -0.5),
        'a_q_norm': gain(ks[4], (ne, A_HEAD_DIM)),
        'a_k_norm': gain(ks[5], (ne, A_HEAD_DIM)),
        'a_sinks': nrm(ks[6], (ne, A_HEADS), 0.5),
        'b_conv_w': nrm(ks[7], (ne, B_CONV, 2 * B_QK_WIDTH), B_CONV ** -0.5),
        'b_conv_b': nrm(ks[8], (ne, 2 * B_QK_WIDTH), 0.02),
        'b_i_bias': nrm(ks[9], (ne, B_HEADS), 0.1),
        'b_f_bias': jnp.linspace(3.0, 6.0, B_HEADS, dtype=f32)[None, :] + nrm(ks[10], (ne, B_HEADS), 0.1),
        'b_out_norm': gain(ks[11], (ne, B_V_WIDTH)),
        'w_out_even': nrm(ks[12], (ne, EVEN_OUT, D_MODEL), EVEN_OUT ** -0.5),
        'norm_odd': gain(ks[13], (no, D_MODEL)),
        'w_in_odd': nrm(ks[14], (no, D_MODEL, ODD_IN), D_MODEL ** -0.5),
        'c_kv_norm': gain(ks[15], (no, C_LATENT)),
        'c_w_uk': nrm(ks[16], (no, C_LATENT, C_HEAD_DIM), C_LATENT ** -0.5),
        'c_w_uv': nrm(ks[17], (no, C_HEADS, C_LATENT, C_HEAD_DIM), C_LATENT ** -0.5),
        'c_q_norm': gain(ks[18], (no, C_HEAD_DIM)),
        'c_k_norm': gain(ks[19], (no, C_HEAD_DIM)),
        'w_out_odd': nrm(ks[20], (no, C_WIDTH, D_MODEL), C_WIDTH ** -0.5),
    }

def reference(x, rel_bias, norm_even, w_in_even, a_q_norm, a_k_norm, a_sinks, b_conv_w, b_conv_b,
              b_i_bias, b_f_bias, b_out_norm, w_out_even, norm_odd, w_in_odd, c_kv_norm, c_w_uk,
              c_w_uv, c_q_norm, c_k_norm, w_out_odd):
    for layer in range(DEPTH):
        j = layer // 2
        if layer % 2 == 0:
            h = rms_norm(x, norm_even[j])
            x = x + even_layer(h, w_in_even[j], a_q_norm[j], a_k_norm[j], a_sinks[j], b_conv_w[j],
                               b_conv_b[j], b_i_bias[j], b_f_bias[j], b_out_norm[j], w_out_even[j],
                               rel_bias)
        else:
            h = rms_norm(x, norm_odd[j])
            x = x + odd_layer(h, w_in_odd[j], c_kv_norm[j], c_w_uk[j], c_w_uv[j], c_q_norm[j],
                              c_k_norm[j], w_out_odd[j], rel_bias)
    return x


_drawn_inputs = setup_inputs


def setup_inputs(seed=0):
    import zlib

    import numpy as np

    out = dict(_drawn_inputs(seed))
    spreads = {}
    factors = {'norm_even': 4.534,
     'a_q_norm': 8.0,
     'a_k_norm': 8.0,
     'a_sinks': 8.0,
     'b_conv_b': 8.0,
     'b_i_bias': 200.0,
     'b_out_norm': 7.924,
     'norm_odd': 4.739,
     'c_kv_norm': 8.0,
     'c_q_norm': 8.0,
     'c_k_norm': 8.0}
    for name, (base, spread) in spreads.items():
        noise = np.random.default_rng([zlib.crc32(name.encode()), seed]).standard_normal(out[name].shape)
        drawn = base * np.exp(spread * noise) if base else spread * noise
        out[name] = __import__('jax').numpy.asarray(drawn.astype(out[name].dtype))
    for name, factor in factors.items():
        out[name] = (out[name] * factor).astype(out[name].dtype)
    return out
```

```python
from contextlib import ExitStack

import numpy as np

import concourse.bass as bass
from concourse import mybir

F32 = mybir.dt.float32
F32R = mybir.dt.float32r
BF16 = mybir.dt.bfloat16
BYTES = {F32: 4, F32R: 4, BF16: 2}
ALU = mybir.AluOpType
ACT = mybir.ActivationFunctionType
AX = mybir.AxisListType.X

P = 128
D = 2048
T = 512
KT = D // P
TT = T // P
EPS = 1e-6
NEG = -1e30
TAKEN = -3e38
FUTURE = -1e38

A_DIM, A_PAIRS, A_KV = 64, 8, 4
M_HEADS, M_QK, M_V = 4, 128, 256
C_HEADS, C_DIM, C_LAT, C_IH, C_ID, TOPK = 16, 128, 512, 8, 64, 128
LT = C_LAT // P

K0 = 0
GATES = 4
A0 = 5
M0 = A0 + 2 * A_PAIRS
E0 = M0 + 8 * M_HEADS
IKW = E0 + KT
IQ0 = IKW + 1
CKV = IQ0 + 4
U0 = CKV + LT
O0 = U0 + 4
F0 = O0 + 2 * C_HEADS
NPANEL = F0 + KT

NCOL = 0


def _cols(n):
    global NCOL
    NCOL += n
    return NCOL - n


G_EVEN = _cols(KT)
G_ODD = _cols(KT)
G_AQ = _cols(1)
G_AK = _cols(1)
G_LAT = _cols(LT)
G_CQ = _cols(1)
G_CK = _cols(1)
SINKS = _cols(8 * A_PAIRS)
I_BIAS = _cols(1)
F_BIAS = _cols(1)
M_PAR = _cols(12 * M_HEADS)
IDENT, BLOCK1, ONES, HEAD1, SEL, NCONST = 0, 128, 256, 384, 386, 386 + 512
NREL = 640
NBUCKET = 32


class Panel:

    def __init__(self, base, j=0, per=0):
        self.n = base + per * j
        self.slot = base % 2
        self.fills = base // 2 + (per // 2) * j + 1
        self.primed = not isinstance(self.n, int) or self.n >= 2


class OwnSteps:

    def __init__(self, eng, sem):
        self.eng, self.sem, self.base, self.k = eng, sem, 0, 0

    def mark(self, ins):
        ins.then_inc(self.sem, 1)
        self.k += 1

    def settle(self):
        self.eng.wait_ge(self.sem, self.base + self.k)

    def link(self, ins):
        self.mark(ins)
        self.settle()

    def enter(self, i, first, per):
        self.start = self.base + self.k
        self.base, self.k, self.per = self.start + (i - first) * per, 0, per

    def leave(self, count):
        assert self.k == self.per, (self.k, self.per)
        self.base, self.k = self.start + count * self.per, 0


class Unit:

    def __init__(self, even):
        self.even = even
        if even:
            self.blocks = [(2 * t + h, t, h, 256, 2 + (2 * t + h) // 2, (h % 2) * 256, (2 * t + h) * 256)
                           for t in range(TT) for h in range(2)]
            pv = [(b, s + k * P, t - 1 + k) for b, t, h, w, _, _, s in self.blocks
                  for k in range(2) if t - 1 + k >= 0]
        else:
            place = {0: (3, 384, 0), 1: (4, 0, 128), 2: (3, 0, 384), 3: (2, 0, 768)}
            self.blocks = [(t, t, 0, P * (t + 1), *place[t]) for t in range(TT)]
            pv = [(b, s + k * P, k) for b, t, h, w, _, _, s in self.blocks for k in range(t + 1)]
        self.pv = pv
        self.nb = len(self.blocks)
        self.ow = A_DIM if even else C_DIM
        self.banks = -(-len(pv) // 4)
        self.bw = 256 if even else T
        self.inv_dim = 1.0 / (A_DIM if even else C_DIM)


EVEN, ODD = Unit(True), Unit(False)


def trunk_program(nc, panels, xT, cols_in, const_src, onehot_in, rel_in, wuk_src, outT):
    x1T = nc.dram_tensor("x1T", (KT, P, T), F32, kind="Internal").ap()
    tab_d = nc.dram_tensor("tab_d", (16, NREL), F32, kind="Internal").ap()
    toep_d = nc.dram_tensor("toep_d", (16, P, T), F32, kind="Internal").ap()

    top = [-(-nc.sbuf_base // 64) * 64]

    def fixed(name, shape, dt=F32):
        size = int(np.prod(shape[1:])) * BYTES[dt]
        t = nc.alloc_sbuf_tensor_at(name, shape, dt, offset=top[0])
        top[0] += -(-size // 32) * 32
        return t

    def zone(start):
        at = [start]

        def place(name, shape, dt=F32):
            size = int(np.prod(shape[1:])) * BYTES[dt]
            t = nc.alloc_sbuf_tensor_at(name, shape, dt, offset=at[0])
            at[0] += -(-size // 32) * 32
            assert at[0] <= nc.sbuf_usable_end, (name, at[0])
            return t
        place.at = at
        return place

    xs_at = top[0]
    xs = fixed("xs", [P, KT, T])
    hh = fixed("hh", [P, KT, T], F32R)
    hl = fixed("hl", [P, KT, T], F32R)
    raw = [fixed(f"raw{i}", [P, KT, P]) for i in range(2)]
    wh = [fixed(f"wh{i}", [P, KT, P], F32R) for i in range(2)]
    wl = [fixed(f"wl{i}", [P, KT, P], F32R) for i in range(2)]
    const = fixed("const", [P, NCONST])
    cols = fixed("cols", [P, NCOL])
    identb = fixed("identb", [P, P], BF16)
    rstd = fixed("rstd", [P, T])
    kgain = fixed("kgain", [P, 2])
    nsink = fixed("nsink", [P, 8 * A_PAIRS])
    epsc = fixed("epsc", [P, 1])
    rtq = fixed("rtq", [P, 8])
    rq = fixed("rq", [P, 8])
    negm = fixed("negm", [P, 8])
    sink_arg = fixed("sink_arg", [P, 8])
    sums = fixed("sums", [P, 8])
    esink = fixed("esink", [P, 8])
    rinv = fixed("rinv", [P, 8])
    iwt = fixed("iwt", [P, TT, C_IH])
    v8 = fixed("v8", [P, 8])
    region = top[0]

    za = zone(region)
    kd = za("kd", [P, A_KV, P + T])
    qm = za("qm", [P, 2, T])
    bias_a = za("bias_a", [P, 2, 256])
    sq_a = za("sq_a", [P, T])
    zf_a = za("zf_a", [P, T])
    th_a = za("th_a", [P, T])
    sz_a = za("sz_a", [P, T])
    s_at = za.at[0]
    S_a = za("S_a", [P, 8 * 256])
    pt_at = za.at[0]
    PT_a = za("PT_a", [P, 4 * T])
    os_a = za("os_a", [P, T])
    vA = za("vA", [P, TT, A_KV * A_DIM])
    keep_at = za.at[0]
    wm = za("wm", [P, 2, 256], BF16)
    rows = za("rows", [4, 2, T])
    acol = za("acol", [P, 16])
    hp = za("hp", [P, 12])
    acur = za("acur", [P, TT])
    selcur = za("selcur", [4, P])
    once = za("once", [32, NREL])
    tab = za("tab", [16, NREL])
    rel_sb = za("rel_sb", [NBUCKET, 16])
    zs = zone(s_at)
    ss4 = zs("ss4", [P, 4, T])
    sq4 = zs("sq4", [P, 4, T])
    zs = zone(s_at)
    kf = [zs(f"kf{i}", [P, T]) for i in range(2)]
    vf = [zs(f"vf{i}", [P, T]) for i in range(2)]
    ksq = [zs(f"ksq{i}", [P, T]) for i in range(2)]
    krt = zs("krt", [P, T])
    kn = zs("kn", [P, T])
    zs = zone(s_at)
    gi, gf, gu, gb, ga, g1 = (zs(f"g_{x}", [4, T]) for x in "ifuba1")

    zm = zone(region)
    cx = zm("cx", [P, 3 + T])
    cy = zm("cy", [P, T])
    cth = zm("cth", [P, T])
    qs = zm("qs", [P, T])
    ks = zm("ks", [P, T])
    early_end = region + 4 * (A_KV * (P + T) + 2 * T)
    assert zm.at[0] <= early_end
    zm.at[0] = early_end
    mvf = [zm(f"mvf{i}", [P, T]) for i in range(2)]
    tho = [zm(f"tho{i}", [P, T]) for i in range(2)]
    G = [zm(f"G{i}", [P, T]) for i in range(2)]
    em = zm("em", [P, T])
    E = zm("E", [P, 1280])
    Tm = zm("Tm", [P, 1280])
    hn = [zm(f"hn{i}", [P, T]) for i in range(2)]
    vtm = zm("vtm", [P, TT, M_V])
    assert zm.at[0] <= keep_at
    dd = cy
    ogf, m_th = cx[:, 3:3 + T], cth

    zo = zone(region)
    V = zo("V", [P, TT, C_HEADS * C_DIM])
    kk = zo("kk", [P, T])
    q_c = zo("q_c", [P, T])
    zf_c = zo("zf_c", [P, T])
    s_o = zo.at[0]
    S_c = zo("S_c", [P, 1280])
    pt_o = zo.at[0]
    PT_c = zo("PT_c", [P, 1280])
    os_c = zo("os_c", [P, T])
    bias_c = zo("bias_c", [P, 1, T])
    sq_c = zo("sq_c", [P, T])
    mask_c = zo("mask_c", [P, 1280], BF16)
    th_c = os_c
    zq = zone(s_o)
    kfc = zq("kfc", [P, T])
    zq = zone(pt_o)
    ksqc = zq("ksqc", [P, T])
    krc = zq("krc", [P, T])
    zq = zone(region)
    iq = zq("iq", [P, TT, T])
    ik = zq("ik", [P, T])
    iwf = zq("iwf", [C_IH, T])
    rl = [zq(f"rl{i}", [P, T]) for i in range(2)]
    latsq = zq("latsq", [P, LT, T])
    latr = zq("latr", [P, T])
    zx = zone(xs_at)
    lath = zx("lath", [P, LT, T], F32R)
    latl = zx("latl", [P, LT, T], F32R)
    latf = zx("latf", [P, LT, T])
    sc = zx("sc", [P, 1152])
    wuk = zx("wuk", [P, LT, C_DIM])
    assert zx.at[0] <= xs_at + 4 * KT * T
    zt = zone(region)
    res = [zt(f"res{i}", [P, T]) for i in range(2)]
    yt = [zt(f"yt{i}", [P, T]) for i in range(2)]
    ptmp = zt("ptmp", [P, T])
    ssum = zt("ssum", [P, T])
    rt_tmp = zt("rt_tmp", [P, T])
    SC_AT = {1: 0, 2: 256, 3: 640}
    EOFF = [0, 512, 896, 1152]

    ident = const[:, IDENT:IDENT + P]
    block1 = const[:, BLOCK1:BLOCK1 + P]
    ones = const[:, ONES:ONES + P]
    head1 = const[:, HEAD1:HEAD1 + 2]

    def col(c, n=1):
        return cols[:, c:c + n]

    with ExitStack() as ctx:
        B = [ctx.enter_context(nc.psum_tensor(f"B{i}", [P, T], F32)) for i in range(8)]

        def sem(name):
            return ctx.enter_context(nc.semaphore(name))

        raw_in = [sem("raw_in0"), sem("raw_in1")]
        (hi_done, lo_done, mm_done, evac_done, h_hi, h_lo, const_in, tab_in, tab_mm, tab_sb, tab_out, toep_out,
         x_sq, x_ss, ss_mm, ss_rt, setup, identb_ok, rstd_ok) = map(sem, (
             "hi_done lo_done mm_done evac_done h_hi h_lo const_in tab_in tab_mm tab_sb tab_out toep_out "
             "x_sq x_ss ss_mm ss_rt setup identb_ok rstd_ok").split())
        x_in = [sem(f"x_in{i}") for i in range(4)]
        (ksq_ok, kss_mm, krt_ok, kd_ok, vT_mm, vA_ok, gate_f, gate_u, gate_a, acol_mm, acol_ok) = map(sem, (
            "ksq_ok kss_mm krt_ok kd_ok vT_mm vA_ok gate_f gate_u gate_a acol_mm acol_ok").split())
        (sq_ok, qss_mm, rtq_ok, lg_mm, bias_in, negm_ok, sk_ok, p_ok, pt_mm, pt_ok, pv_mm, os_ok, oT_mm, cat_ok,
         th_ok) = map(sem, ("sq_ok qss_mm rtq_ok lg_mm bias_in negm_ok sk_ok p_ok pt_mm pt_ok pv_mm os_ok oT_mm "
                            "cat_ok th_ok").split())
        (m_par, m_conv, m_cth, m_qk, m_bc, m_st, m_T, m_E, m_sel, m_P, m_vT, m_vA, m_gth, m_num, m_h, m_hsq, m_ss,
         m_rtk, m_cat, m_em) = map(sem, ("m_par m_conv m_cth m_qk m_bc m_st m_T m_E m_sel m_P m_vT m_vA m_gth m_num m_h "
                                   "m_hsq m_ss m_rtk m_cat m_em").split())
        res_in = [sem("res_in0"), sem("res_in1")]
        x1_out = sem("x1_out")
        y_out = [sem("y_out0"), sem("y_out1")]
        (iw_mm, iw_ok, isc_mm, rl_ok, rl_used, lsq_ok, lss_mm, lrt_ok, lat_ok, lath_ok, latl_ok, ck_mm, ckf_ok,
         cksq_ok, ckss_mm, ckrt_ok, kk_ok, mask_ok, x1_ss, wuk_in) = map(sem, (
             "iw_mm iw_ok isc_mm rl_ok rl_used lsq_ok lss_mm lrt_ok lat_ok lath_ok latl_ok ck_mm ckf_ok "
             "cksq_ok ckss_mm ckrt_ok kk_ok mask_ok x1_ss wuk_in").split())
        dve_own, act_own, pool_own = sem("dve_own"), sem("act_own"), sem("pool_own")

        def u_of(u, j):
            return j if u.even else A_PAIRS + j

        def pt_of(u, j):
            return 4 * j if u.even else 4 * A_PAIRS + ODD.banks * j

        block = ctx.enter_context(nc.Block())

        @block.sync
        def _(sp):
            def load(pn):
                if pn.primed:
                    sp.wait_ge(lo_done, pn.n - 1)
                sp.dma_start(raw[pn.slot][:, :, :].rearrange("p k c -> p (k c)"),
                             panels[bass.ds(pn.n, 1), :, :].rearrange("a p n -> p (a n)")).then_inc(raw_in[pn.slot], 16)

            sp.dma_start(const[:, :], const_src).then_inc(const_in, 16)
            sp.dma_start(cols[:, :], cols_in).then_inc(const_in, 16)
            for c in range(4):
                sp.dma_start(xs[:, 4 * c:4 * c + 4, :],
                             xT[4 * c:4 * c + 4, :, :].rearrange("k p n -> p k n")).then_inc(x_in[c], 16)
                if c == 0:
                    load(Panel(0))
            load(Panel(1))
            with sp.Fori(1, NPANEL // 2) as i:
                load(Panel(0, i, 2))
                load(Panel(1, i, 2))

        @block.gpsimd
        def _(pool):
            own = OwnSteps(pool, pool_own)
            pool.dma_start(once[:, :], onehot_in).then_inc(tab_in, 16)
            pool.dma_start(rel_sb[:, :], rel_in).then_inc(tab_in, 16)
            for z in range(2):
                own.mark(pool.memset(wm[:, z, :], NEG))
            own.settle()
            own.mark(pool.memset(wm[0:64, 0, 128:192], 0.0))
            own.mark(pool.memset(wm[64:128, 0, 128:256], 0.0))
            own.mark(pool.memset(wm[0:64, 1, 64:192], 0.0))
            own.mark(pool.memset(wm[64:128, 1, 128:256], 0.0))
            own.settle()
            pool.memset(epsc[:, :], EPS).then_inc(setup, 1)
            for c in range(1, 4):
                pool.wait_ge(x_sq, c + 1)
                pool.tensor_tensor(ss4[:, :, :], ss4[:, :, :], sq4[:, :, :], ALU.add).then_inc(x_ss, 1)
                pool.wait_ge(x_ss, c)
            pool.wait_ge(tab_sb, 1)
            pool.dma_start(tab_d, tab[:, :]).then_inc(tab_out, 16)
            pool.wait_ge(tab_out, 16)
            pool.dma_start(toep_d, bass.AP(tab_d.tensor, P - 1, [[NREL, 16], [-1, P], [1, T]])).then_inc(toep_out, 16)
            pool.wait_ge(toep_out, 16)

            def load_bias_a(j):
                pool.dma_start(bias_a[:, :, :], toep_d[bass.ds(2 * j, 2), :, 256:512].rearrange("a p n -> p a n"))\
                    .then_inc(bias_in, 16)

            load_bias_a(0)
            with pool.Fori(1, A_PAIRS) as j:
                pool.wait_ge(negm_ok, j)
                load_bias_a(j)

            with pool.Fori(1, M_HEADS + 1) as made:
                pool.wait_ge(cat_ok, A_PAIRS)
                pool.wait_ge(m_E, made)
                for s in range(TT):
                    blk = E[:, EOFF[s]:EOFF[s] + P]
                    last = pool.affine_select(out=blk, in_=blk, pattern=[[1, P]], compare_op=ALU.is_ge, fill=0.0,
                                              base=0, channel_multiplier=-1)
                last.then_inc(m_sel, 1)

            def load_res(src, m, s):
                pool.dma_start(res[s][:, :], src[bass.ds(m, 1), :, :].rearrange("a p n -> p (a n)"))\
                    .then_inc(res_in[s], 16)

            pool.wait_ge(m_cat, 2 * M_HEADS)
            own.link(pool.memset(ssum[:, :], 0.0))
            load_res(xT, 0, 0)
            load_res(xT, 1, 1)

            def even_out(i, last=False):
                for s in range(2):
                    m = 2 * i + s
                    pool.wait_ge(evac_done, E0 + m + 1)
                    pool.dma_start(x1T[bass.ds(m, 1), :, :].rearrange("a p n -> p (a n)"),
                                   xs[:, bass.ds(m, 1), :].rearrange("p a n -> p (a n)")).then_inc(x1_out, 16)
                    if not last:
                        load_res(xT, m + 2, s)
                    tile = xs[:, bass.ds(m, 1), :].rearrange("p a n -> p (a n)")
                    own.link(pool.tensor_tensor(ptmp[:, :], tile, tile, ALU.mult))
                    add = pool.tensor_tensor(ssum[:, :], ssum[:, :], ptmp[:, :], ALU.add)
                    add.then_inc(x1_ss, 1) if last and s else own.link(add)

            with pool.Fori(0, KT // 2 - 1) as i:
                own.enter(i, 0, 4)
                even_out(i)
            own.leave(KT // 2 - 1)
            even_out(KT // 2 - 1, last=True)
            pool.wait_ge(x1_out, 16 * KT)
            pool.wait_ge(h_lo, 3 * KT)
            pool.dma_start(wuk[:, :, :], wuk_src).then_inc(wuk_in, 16)

            def load_bias_c(h):
                pool.dma_start(bias_c[:, 0, :], toep_d[bass.ds(h, 1), :, :].rearrange("a p n -> p (a n)"))\
                    .then_inc(bias_in, 16)

            load_bias_c(0)
            with pool.Fori(1, C_HEADS) as h:
                pool.wait_ge(negm_ok, A_PAIRS + h)
                load_bias_c(h)

            pool.wait_ge(pv_mm, A_PAIRS + C_HEADS)
            load_res(x1T, 0, 0)
            load_res(x1T, 1, 1)

            def odd_out(i, last=False):
                for s in range(2):
                    m = 2 * i + s
                    pool.wait_ge(evac_done, F0 + m + 1)
                    pool.dma_start(outT[bass.ds(m, 1), :, :].rearrange("a p n -> p (a n)"), yt[s][:, :])\
                        .then_inc(y_out[s], 16)
                    if not last:
                        load_res(x1T, m + 2, s)

            with pool.Fori(0, KT // 2 - 1) as i:
                odd_out(i)
            odd_out(KT // 2 - 1, last=True)
            pool.wait_ge(y_out[0], 16 * KT // 2)
            pool.wait_ge(y_out[1], 16 * KT // 2)

        @block.tensor
        def _(pe):
            def mm(out, lhsT, rhs, start=True, stop=True):
                return nc.tensor.matmul(out, lhsT, rhs, start=start, stop=stop)

            def main_panel(pn, conv=None, before_last=None):
                pe.wait_ge(lo_done, pn.n + 1)
                if pn.primed:
                    pe.wait_ge(evac_done, pn.n - 1)
                acc, w1, w2 = B[pn.slot], wh[pn.slot], wl[pn.slot]
                for k in range(KT):
                    if k == KT - 1 and before_last:
                        before_last()
                    if conv is not None:
                        pe.wait_ge(h_lo, KT * conv + k + 1)
                    mm(acc[:, :], w1[:, k, :], hh[:, k, :], k == 0, False)
                    mm(acc[:, :], w1[:, k, :], hl[:, k, :], False, False)
                    last = mm(acc[:, :], w2[:, k, :], hh[:, k, :], False, k == KT - 1)
                last.then_inc(mm_done, 1)

            def transpose4(bank, src, rows_=P):
                for t in range(TT):
                    last = nc.tensor.transpose(bank[:, t * P:t * P + rows_], src[:, t * P:(t + 1) * P],
                                               ident[0:rows_, 0:rows_])
                return last

            def logits(u, j):
                q, sq, k = (None, sq_a, kd) if u.even else (q_c, sq_c, kk)
                pe.wait_ge(sq_ok, u_of(u, j) + 1)
                for t in range(TT):
                    w = 2 if u.even else 1
                    last = mm(B[6][:, w * t:w * t + w], sq[:, t * P:(t + 1) * P],
                              head1 if u.even else ones[:, 0:1])
                last.then_inc(qss_mm, 1)
                for b, t, h, w, bank, c, _ in u.blocks:
                    dst = B[bank][:, c:c + w]
                    if u.even:
                        mm(dst, qm[:, h, t * P:(t + 1) * P],
                           kd[:, :, :].rearrange("p g n -> p (g n)")[:, bass.ds((j // 2) * (P + T) + t * P, w)],
                           True, False)
                        mask = wm[:, min(t, 1), :]
                    else:
                        mm(dst, q_c[:, t * P:(t + 1) * P], kk[:, 0:w], True, False)
                        mask = mask_c[:, ODD.blocks[t][6]:ODD.blocks[t][6] + w]
                    last = mm(dst, identb[:, :], mask, False, True)
                last.then_inc(lg_mm, 1)

            def weighted_values(u, j):
                S, PT, OS = (S_a, PT_a, os_a) if u.even else (S_c, PT_c, os_c)
                pe.wait_ge(p_ok, u_of(u, j) + 1)
                n = len(u.pv)
                for i, (b, s, _) in enumerate(u.pv):
                    last = nc.tensor.transpose(B[2 + i // 4][:, (i % 4) * P:(i % 4 + 1) * P], S[:, s:s + P], ident)
                    if i % 4 == 3 or i == n - 1:
                        last.then_inc(pt_mm, 1)
                for i, (b, _, vt) in enumerate(u.pv):
                    if i % 4 == 0:
                        pe.wait_ge(pt_ok, pt_of(u, j) + i // 4 + 1)
                    if u.even:
                        rhs = vA[:, vt, bass.ds((j // 2) * A_DIM, A_DIM)]
                    else:
                        rhs = V[:, vt, bass.ds(j * C_DIM, C_DIM)]
                    last = mm(B[6][:, b * u.ow:(b + 1) * u.ow], PT[:, i * P:(i + 1) * P], rhs,
                              i == 0 or u.pv[i - 1][0] != b, i == n - 1 or u.pv[i + 1][0] != b)
                last.then_inc(pv_mm, 1)

            def outputs(u, j):
                pe.wait_ge(os_ok, u_of(u, j) + 1)
                transpose4(B[7], os_a if u.even else os_c).then_inc(oT_mm, 1)

            pe.wait_ge(const_in, 32)
            pe.wait_ge(tab_in, 32)
            mm(B[2][0:16, 0:512], rel_sb[:, :], once[:, 0:512])
            mm(B[3][0:16, 0:NREL - 512], rel_sb[:, :], once[:, 512:NREL]).then_inc(tab_mm, 1)
            main_panel(Panel(0), conv=0)
            pe.wait_ge(x_ss, 3)
            for k in range(4):
                last = mm(B[7][:, :], ones, ss4[:, k, :], k == 0, k == 3)
            last.then_inc(ss_mm, 1)
            main_panel(Panel(1))
            main_panel(Panel(2))
            for p in range(2):
                if p:
                    main_panel(Panel(3))
                pe.wait_ge(ksq_ok, p + 1)
                mm(B[2 + p][:, :], block1, ksq[p][:, :]).then_inc(kss_mm, 1)
            pe.wait_ge(evac_done, 3)
            transpose4(B[4], vf[0]).then_inc(vT_mm, 1)
            main_panel(Panel(4))
            pe.wait_ge(evac_done, 4)
            transpose4(B[5], vf[1]).then_inc(vT_mm, 1)
            main_panel(Panel(5))
            pe.wait_ge(gate_a, 1)
            for t in range(TT):
                last = nc.tensor.transpose(B[7][:, 4 * t:4 * t + 4], ga[:, t * P:(t + 1) * P], ident[0:4, 0:4])
            last.then_inc(acol_mm, 1)
            main_panel(Panel(6))
            pe.wait_ge(kd_ok, 2)
            pe.wait_ge(setup, 1)
            pe.wait_ge(identb_ok, 1)
            pe.wait_ge(vA_ok, 2)
            logits(EVEN, 0)

            with pe.Fori(1, A_PAIRS) as j:
                main_panel(Panel(A0, j, 2))
                weighted_values(EVEN, j - 1)
                main_panel(Panel(A0 + 1, j, 2))
                pe.wait_ge(acol_ok, 1)
                outputs(EVEN, j - 1)
                logits(EVEN, j)

            def head(h, first=False):
                pn = [Panel(M0 + u, h, 8) for u in range(8)]
                main_panel(pn[0])
                if first:
                    weighted_values(EVEN, A_PAIRS - 1)
                main_panel(pn[1])
                if first:
                    outputs(EVEN, A_PAIRS - 1)
                main_panel(pn[2])
                pe.wait_ge(m_par, h + 1)
                if first:
                    pe.wait_ge(gate_a, 2)
                mm(B[5][:, :], selcur[:, :], rows[:, 0, :])
                mm(B[6][:, :], selcur[:, :], rows[:, 1, :]).then_inc(m_bc, 1)
                pe.wait_ge(m_qk, 2 * h + 2)
                for s, (bank, c) in enumerate([(2, 0), (3, 0), (4, 0), (3, 384)]):
                    last = mm(B[bank][:, c:c + T - s * P], ks[:, s * P:(s + 1) * P], qs[:, s * P:T])
                last.then_inc(m_st, 1)
                main_panel(pn[3])
                if first:
                    pe.wait_ge(cat_ok, A_PAIRS)
                pe.wait_ge(evac_done, pn[2].n + 1)
                transpose4(B[7], mvf[0]).then_inc(m_vT, 1)
                main_panel(pn[4])
                pe.wait_ge(evac_done, pn[3].n + 1)
                pe.wait_ge(m_vA, 2 * h + 1)
                transpose4(B[7], mvf[1]).then_inc(m_vT, 1)
                main_panel(pn[5])
                pe.wait_ge(m_vA, 2 * h + 2)
                pe.wait_ge(m_P, h + 1)
                for v in range(2):
                    for s in range(TT):
                        mm(B[2 + v][:, s * P:T], vtm[:, s, v * P:(v + 1) * P], E[:, EOFF[s]:EOFF[s] + T - s * P],
                           s == 0, s == TT - 1)
                for s in range(TT):
                    last = mm(B[4][:, s * P:T], ones, E[:, EOFF[s]:EOFF[s] + T - s * P], s == 0, s == TT - 1)
                last.then_inc(m_num, 1)
                main_panel(pn[6])
                main_panel(pn[7])
                pe.wait_ge(m_hsq, h + 1)
                for v in range(2):
                    last = mm(B[5][:, :], ones, Tm[:, v * T:(v + 1) * T], v == 0, v == 1)
                last.then_inc(m_ss, 1)

            head(0, first=True)
            with pe.Fori(1, M_HEADS) as h:
                head(h)

            main_panel(Panel(E0), conv=1)
            main_panel(Panel(E0 + 1))
            with pe.Fori(1, KT // 2) as i:
                main_panel(Panel(E0, i, 2))
                main_panel(Panel(E0 + 1, i, 2))

            main_panel(Panel(IKW), conv=2)
            pe.wait_ge(x1_ss, 1)
            mm(B[7][:, :], ones, ssum[:, :]).then_inc(ss_mm, 1)
            main_panel(Panel(IKW + 1))
            main_panel(Panel(IKW + 2))
            pe.wait_ge(evac_done, IKW + 1)
            pe.wait_ge(ss_rt, 2)
            for t in range(TT):
                last = nc.tensor.transpose(B[7][:, C_IH * t:C_IH * (t + 1)], iwf[:, t * P:(t + 1) * P],
                                           ident[0:C_IH, 0:C_IH])
            last.then_inc(iw_mm, 1)
            main_panel(Panel(IKW + 3))
            main_panel(Panel(IKW + 4))
            done = 0

            def index_scores(t):
                nonlocal done
                pe.wait_ge(evac_done, IQ0 + 4)
                w = P * (t + 1)
                for h in range(C_IH):
                    if done >= 4:
                        pe.wait_ge(rl_ok, done - 3)
                    r = slice(64 * (h % 2), 64 * (h % 2) + 64)
                    mm(B[2 + done % 4][:, 0:w], iq[r, h // 2, t * P:(t + 1) * P], ik[r, 0:w]).then_inc(isc_mm, 1)
                    done += 1

            main_panel(Panel(CKV))
            index_scores(1)
            main_panel(Panel(CKV + 1))
            index_scores(2)
            main_panel(Panel(CKV + 2))
            main_panel(Panel(CKV + 3))
            pe.wait_ge(lsq_ok, LT)
            for c in range(LT):
                last = mm(B[6][:, :], ones, latsq[:, c, :], c == 0, c == LT - 1)
            last.then_inc(lss_mm, 1)
            index_scores(3)

            for g in range(4):
                pn = Panel(U0 + g)
                pe.wait_ge(lo_done, pn.n + 1)
                if g == 0:
                    pe.wait_ge(latl_ok, LT)
                    pe.wait_ge(evac_done, U0)
                    pe.wait_ge(rl_ok, 3 * C_IH)
                if g >= 2:
                    pe.wait_ge(evac_done, pn.n - 1)
                w1 = wh[pn.slot][:, :, :].rearrange("p (c a) n -> p c (a n)", c=LT)
                w2 = wl[pn.slot][:, :, :].rearrange("p (c a) n -> p c (a n)", c=LT)
                for t in range(TT):
                    dst = B[4 * (g % 2) + t][:, :]
                    tok = slice(t * P, (t + 1) * P)
                    for c in range(LT):
                        mm(dst, lath[:, c, tok], w1[:, c, :], c == 0, False)
                        mm(dst, lath[:, c, tok], w2[:, c, :], False, False)
                        last = mm(dst, latl[:, c, tok], w1[:, c, :], False, c == LT - 1)
                last.then_inc(mm_done, 1)
            pe.wait_ge(wuk_in, 16)
            pe.wait_ge(evac_done, U0 + 3)
            for c in range(LT):
                last = mm(B[2][:, :], wuk[:, c, :], latf[:, c, :], c == 0, c == LT - 1)
            last.then_inc(ck_mm, 1)
            main_panel(Panel(O0))
            pe.wait_ge(cksq_ok, 1)
            mm(B[3][:, :], ones, ksqc[:, :]).then_inc(ckss_mm, 1)
            main_panel(Panel(O0 + 1))
            pe.wait_ge(evac_done, O0)
            pe.wait_ge(kk_ok, 1)
            pe.wait_ge(mask_ok, 1)
            logits(ODD, 0)

            with pe.Fori(1, C_HEADS) as j:
                main_panel(Panel(O0, j, 2))
                weighted_values(ODD, j - 1)
                main_panel(Panel(O0 + 1, j, 2))
                outputs(ODD, j - 1)
                logits(ODD, j)

            def last_unit():
                weighted_values(ODD, C_HEADS - 1)
                outputs(ODD, C_HEADS - 1)

            main_panel(Panel(F0), conv=3, before_last=last_unit)
            main_panel(Panel(F0 + 1))
            with pe.Fori(1, KT // 2) as i:
                main_panel(Panel(F0, i, 2))
                main_panel(Panel(F0 + 1, i, 2))

        @block.scalar
        def _(act):
            own = OwnSteps(act, act_own)
            A = nc.scalar.activation

            def split_hi(pn):
                act.wait_ge(raw_in[pn.slot], 16 * pn.fills)
                if pn.primed:
                    act.wait_ge(mm_done, pn.n - 1)
                A(wh[pn.slot][:, :, :], raw[pn.slot][:, :, :], ACT.Copy).then_inc(hi_done, 1)

            def act_hi(k, gain=None):
                A(hh[:, k, :], xs[:, k, :], ACT.Copy, scale=col(gain + k) if gain is not None else 1.0)\
                    .then_inc(h_hi, 1)

            def after_q(u, j, first=False, lookahead=True):
                pn = Panel(A0 if u.even else O0, j, 2)
                act.wait_ge(mm_done, pn.n + 1)
                split_hi(Panel((A0 if u.even else O0) + 2, j, 2))
                act.wait_ge(evac_done, pn.n + 1)
                if u.even:
                    A(sq_a[0:64, :], qm[0:64, 0, :], ACT.Square)
                    A(sq_a[64:128, :], qm[64:128, 1, :], ACT.Square).then_inc(sq_ok, 1)
                else:
                    A(sq_c[:, :], q_c[:, :], ACT.Square).then_inc(sq_ok, 1)
                if not first:
                    move_blocks(u, j - 1)

            def move_blocks(u, j):
                PT = PT_a if u.even else PT_c
                for i in range(u.banks):
                    act.wait_ge(pt_mm, pt_of(u, j) + i + 1)
                    w = min(T, P * len(u.pv) - i * T)
                    A(PT[:, i * T:i * T + w], B[2 + i][:, 0:w], ACT.Copy).then_inc(pt_ok, 1)

            def after_z(u, j):
                base = (A0 if u.even else O0) + 1
                S, zf, th = (S_a, zf_a, th_a) if u.even else (S_c, zf_c, th_c)
                act.wait_ge(mm_done, Panel(base, j, 2).n + 1)
                split_hi(Panel(base + 2, j, 2))
                n = 8 if u.even else 4
                act.wait_ge(qss_mm, u_of(u, j) + 1)
                A(rtq[:, 0:n], B[6][:, 0:n], ACT.Sqrt, bias=epsc[:, :], scale=u.inv_dim).then_inc(rtq_ok, 1)
                act.wait_ge(evac_done, Panel(base, j, 2).n + 1)
                A(th[:, :], zf[:, :], ACT.Tanh, scale=0.5).then_inc(th_ok, 1)
                act.wait_ge(negm_ok, u_of(u, j) + 1)
                for b, t, h, w, _, _, s in u.blocks:
                    last = A(S[:, s:s + w], S[:, s:s + w], ACT.Exp, bias=negm[:, b:b + 1],
                             accum_out=sums[:, b:b + 1])
                if u.even:
                    act.wait_ge(sk_ok, j + 1)
                    last = A(esink[:, :], sink_arg[:, :], ACT.Exp)
                last.then_inc(p_ok, 1)

            act.wait_ge(const_in, 32)
            A(identb[:, :], ident, ACT.Copy).then_inc(identb_ok, 1)
            for c in range(4):
                act.wait_ge(x_in[c], 16)
                for k in range(4 * c, 4 * c + 4):
                    act_hi(k, G_EVEN)
                if c > 1:
                    act.wait_ge(x_ss, c - 1)
                A((sq4 if c else ss4)[:, :, :], xs[:, 4 * c:4 * c + 4, :], ACT.Square).then_inc(x_sq, 1)
                if c == 0:
                    split_hi(Panel(0))
            split_hi(Panel(1))
            act.wait_ge(tab_mm, 1)
            A(tab[:, 0:512], B[2][0:16, :], ACT.Copy)
            A(tab[:, 512:NREL], B[3][0:16, 0:NREL - 512], ACT.Copy).then_inc(tab_sb, 1)
            act.wait_ge(ss_mm, 1)
            act.wait_ge(setup, 1)
            A(krt[:, :], B[7][:, :], ACT.Sqrt, bias=epsc[:, :], scale=1.0 / D).then_inc(ss_rt, 1)
            for p in range(2):
                split_hi(Panel(2 + p))
                act.wait_ge(evac_done, p + 1)
                A(ksq[p][:, :], kf[p][:, :], ACT.Square).then_inc(ksq_ok, 1)
            for p in range(2):
                split_hi(Panel(4 + p))
                act.wait_ge(kss_mm, p + 1)
                if p:
                    act.wait_ge(kd_ok, 1)
                A(krt[:, :], B[2 + p][:, :], ACT.Sqrt, bias=epsc[:, :], scale=1.0 / A_DIM).then_inc(krt_ok, 1)
                act.wait_ge(vT_mm, p + 1)
                A(vA[:, :, p * P:(p + 1) * P], B[4 + p][:, :].rearrange("p (t d) -> p t d", t=TT),
                  ACT.Copy).then_inc(vA_ok, 1)
            split_hi(Panel(6))
            act.wait_ge(gate_f, 1)
            own.link(A(gu[:, :], gf[:, :], ACT.Abs))
            own.link(A(gu[:, :], gu[:, :], ACT.Exp, scale=-1.0))
            A(gu[:, :], gu[:, :], ACT.Ln, bias=ones[0:4, 0:1]).then_inc(gate_u, 1)
            after_q(EVEN, 0, first=True)
            act.wait_ge(acol_mm, 1)
            A(acol[:, :].rearrange("p (h t) -> p t h", t=TT), B[7][:, 0:16].rearrange("p (t h) -> p t h", t=TT),
              ACT.Copy).then_inc(acol_ok, 1)
            after_z(EVEN, 0)

            with act.Fori(1, A_PAIRS) as j:
                after_q(EVEN, j)
                after_z(EVEN, j)

            def head(h, first=False):
                pn = [Panel(M0 + u, h, 8) for u in range(10)]

                def ahead(u):
                    act.wait_ge(mm_done, pn[u].n + 1)
                    split_hi(pn[u + 2])

                for u in range(2):
                    ahead(u)
                    if first and u == 0:
                        move_blocks(EVEN, A_PAIRS - 1)
                    act.wait_ge(m_conv, 2 * h + u + 1)
                    A(cth[:, :], cy[:, :], ACT.Tanh, scale=0.5).then_inc(m_cth, 1)
                ahead(2)
                act.wait_ge(m_bc, h + 1)
                A(em[:, :], B[6][:, :], ACT.Exp, scale=-1.0).then_inc(m_em, 1)
                act.wait_ge(m_T, h + 1)
                for s in range(TT):
                    c = slice(EOFF[s], EOFF[s] + T - s * P)
                    last = A(E[:, c], Tm[:, c], ACT.Exp, scale=-1.0)
                last.then_inc(m_E, 1)
                for v in range(2):
                    ahead(3 + v)
                    if v:
                        act.wait_ge(evac_done, pn[4].n + 1)
                        A(tho[0][:, :], ogf[:, :], ACT.Tanh, scale=0.5).then_inc(m_gth, 1)
                    act.wait_ge(m_vT, 2 * h + v + 1)
                    A(vtm[:, :, v * P:(v + 1) * P], B[7][:, :].rearrange("p (t d) -> p t d", t=TT),
                      ACT.Copy).then_inc(m_vA, 1)
                ahead(5)
                act.wait_ge(evac_done, pn[5].n + 1)
                A(tho[1][:, :], ogf[:, :], ACT.Tanh, scale=0.5).then_inc(m_gth, 1)
                ahead(6)
                act.wait_ge(evac_done, pn[6].n + 1)
                A(m_th[:, :], ogf[:, :], ACT.Tanh, scale=0.5).then_inc(m_gth, 1)
                act.wait_ge(m_h, h + 1)
                for v in range(2):
                    last = A(Tm[:, v * T:(v + 1) * T], hn[v][:, :], ACT.Square)
                last.then_inc(m_hsq, 1)
                ahead(7)
                act.wait_ge(evac_done, pn[7].n + 1)
                A(m_th[:, :], ogf[:, :], ACT.Tanh, scale=0.5).then_inc(m_gth, 1)
                act.wait_ge(m_ss, h + 1)
                A(em[:, :], B[5][:, :], ACT.Sqrt, bias=epsc[:, :], scale=1.0 / M_V).then_inc(m_rtk, 1)

            head(0, first=True)
            with act.Fori(1, M_HEADS) as h:
                head(h)

            act.wait_ge(mm_done, E0)
            act.wait_ge(cat_ok, A_PAIRS)
            for k in range(KT):
                if k >= 8:
                    act.wait_ge(m_cat, k - 7)
                act_hi(k)
            with act.Fori(0, KT // 2) as i:
                for s in range(2):
                    act.wait_ge(mm_done, E0 + 2 * i + s + 1)
                    split_hi(Panel(E0 + 2 + s, i, 2))

            for k in range(KT):
                act.wait_ge(evac_done, E0 + k + 1)
                act_hi(k, G_ODD)

            def ahead(n):
                act.wait_ge(mm_done, n + 1)
                split_hi(Panel(n + 2))

            act.wait_ge(ss_mm, 2)
            A(rt_tmp[:, :], B[7][:, :], ACT.Sqrt, bias=epsc[:, :], scale=1.0 / D).then_inc(ss_rt, 1)
            for n in range(IKW, IKW + 3):
                ahead(n)
            act.wait_ge(iw_mm, 1)
            A(iwt[:, :, :].rearrange("p t h -> p (t h)"), B[7][:, 0:TT * C_IH], ACT.Copy,
              scale=float(C_IH) ** -0.5).then_inc(iw_ok, 1)
            for n in range(IKW + 3, CKV):
                ahead(n)
            done = 0

            def relu_scores(t):
                nonlocal done
                for h in range(C_IH):
                    act.wait_ge(isc_mm, done + 1)
                    if done >= 2:
                        act.wait_ge(rl_used, done - 1)
                    A(rl[done % 2][:, 0:P * (t + 1)], B[2 + done % 4][:, 0:P * (t + 1)], ACT.Relu,
                      scale=float(C_ID) ** -0.5).then_inc(rl_ok, 1)
                    done += 1

            for c in range(LT):
                ahead(CKV + c)
                act.wait_ge(evac_done, CKV + c + 1)
                A(latsq[:, c, :], latf[:, c, :], ACT.Square).then_inc(lsq_ok, 1)
                if c < 2:
                    relu_scores(c + 1)
            act.wait_ge(lss_mm, 1)
            A(latr[:, :], B[6][:, :], ACT.Sqrt, bias=epsc[:, :], scale=1.0 / C_LAT).then_inc(lrt_ok, 1)
            for c in range(LT):
                act.wait_ge(lat_ok, c + 1)
                A(lath[:, c, :], latf[:, c, :], ACT.Copy).then_inc(lath_ok, 1)
            relu_scores(3)
            for g in range(4):
                ahead(U0 + g)
            act.wait_ge(ckf_ok, 1)
            A(ksqc[:, :], kfc[:, :], ACT.Square).then_inc(cksq_ok, 1)
            after_q(ODD, 0, first=True)
            act.wait_ge(ckss_mm, 1)
            A(krc[:, :], B[3][:, :], ACT.Sqrt, bias=epsc[:, :], scale=1.0 / C_DIM).then_inc(ckrt_ok, 1)
            after_z(ODD, 0)
            with act.Fori(1, C_HEADS) as j:
                after_q(ODD, j)
                after_z(ODD, j)

            for k in range(KT - 1):
                act.wait_ge(cat_ok, A_PAIRS + k + 1)
                act_hi(k)
            move_blocks(ODD, C_HEADS - 1)
            act.wait_ge(cat_ok, A_PAIRS + KT)
            act_hi(KT - 1)
            with act.Fori(0, KT // 2 - 1) as i:
                for s in range(2):
                    act.wait_ge(mm_done, F0 + 2 * i + s + 1)
                    split_hi(Panel(F0 + 2 + s, i, 2))

        @block.vector
        def _(dve):
            own = OwnSteps(dve, dve_own)
            V_ = nc.vector

            def split_lo(pn):
                dve.wait_ge(hi_done, pn.n + 1)
                V_.tensor_tensor(wl[pn.slot][:, :, :], raw[pn.slot][:, :, :], wh[pn.slot][:, :, :].bitcast(F32),
                                 ALU.subtract).then_inc(lo_done, 1)

            def evac(pn, out, rows_=slice(0, P), out_rows=None):
                dve.wait_ge(mm_done, pn.n + 1)
                return V_.tensor_tensor(out, B[pn.slot][rows_, :], rstd[rows_, :], ALU.mult)

            def act_lo(k, phase, gain=None):
                dve.wait_ge(h_hi, KT * phase + k + 1)
                hi = hh[:, k, :].bitcast(F32)
                if gain is None:
                    ins = V_.tensor_tensor(hl[:, k, :], xs[:, k, :], hi, ALU.subtract)
                else:
                    ins = V_.scalar_tensor_tensor(hl[:, k, :], xs[:, k, :], col(gain + k), hi, ALU.mult, ALU.subtract)
                ins.then_inc(h_lo, 1)

            def after_q(u, j, first=False):
                base = A0 if u.even else O0
                pn = Panel(base, j, 2)
                if u.even:
                    evac(pn, qm[0:64, 0, :], slice(0, 64))
                    evac(pn, qm[64:128, 1, :], slice(64, 128)).then_inc(evac_done, 1)
                else:
                    evac(pn, q_c[:, :]).then_inc(evac_done, 1)
                split_lo(Panel(base + 2, j, 2))
                if not first:
                    normalise(u, j - 1)

            def normalise(u, j):
                n, OS = u.nb, os_a if u.even else os_c
                dve.wait_ge(p_ok, u_of(u, j) + 1)
                tot = sums
                if u.even:
                    own.link(V_.tensor_tensor(esink[:, 0:n], sums[:, 0:n], esink[:, 0:n], ALU.add))
                    tot = esink
                own.link(V_.reciprocal(rinv[:, 0:n], tot[:, 0:n]))
                dve.wait_ge(pv_mm, u_of(u, j) + 1)
                V_.tensor_tensor(OS[:, :].rearrange("p (b d) -> p b d", b=n),
                                 B[6][:, :].rearrange("p (b d) -> p b d", b=n),
                                 rinv[:, 0:n].unsqueeze(2).to_broadcast([P, n, u.ow]), ALU.mult).then_inc(os_ok, 1)

            def gate_out(u, j):
                dve.wait_ge(oT_mm, u_of(u, j) + 1)
                V_.scalar_tensor_tensor(xs[:, bass.ds(j, 1), :].rearrange("p a n -> p (a n)"), B[7][:, :], 0.5,
                                        (sz_a if u.even else zf_c)[:, :], ALU.mult, ALU.mult).then_inc(cat_ok, 1)

            def after_z(u, j, first=False):
                base = (A0 if u.even else O0) + 1
                S, th, bias = (S_a, th_a, bias_a) if u.even else (S_c, th_c, bias_c)
                zf, sz = (zf_a, sz_a) if u.even else (zf_c, zf_c)
                pn = Panel(base, j, 2)
                if u.even:
                    evac(pn, zf[:, :]).then_inc(evac_done, 1)
                    split_lo(Panel(base + 2, j, 2))
                    if not first:
                        gate_out(u, j - 1)
                else:
                    split_lo(Panel(base + 2, j, 2))
                    if not first:
                        gate_out(u, j - 1)
                        dve.wait_ge(cat_ok, u_of(u, j))
                    evac(pn, zf[:, :]).then_inc(evac_done, 1)
                n = u.nb
                dve.wait_ge(rtq_ok, u_of(u, j) + 1)
                own.link(V_.reciprocal(rq[:, 0:n], rtq[:, 0:n]))
                dve.wait_ge(lg_mm, u_of(u, j) + 1)
                dve.wait_ge(bias_in, 16 * (u_of(u, j) + 1))
                for b, t, h, w, bank, c, s in u.blocks:
                    own.mark(V_.scalar_tensor_tensor(S[:, s:s + w], B[bank][:, c:c + w], rq[:, b:b + 1],
                                                     bias[:, h, u.bw - w:u.bw], ALU.mult, ALU.add))
                own.settle()
                if u.even:
                    own.link(V_.tensor_reduce(negm[:, :], S[:, :].rearrange("p (b n) -> p b n", b=n), AX, ALU.max,
                                              negate=True))
                    ns = nsink[:, bass.ds(8 * j, 8)]
                    V_.tensor_tensor(negm[:, :], negm[:, :], ns, ALU.min).then_inc(negm_ok, 1)
                    dve.wait_ge(negm_ok, j + 1)
                    V_.tensor_tensor(sink_arg[:, :], negm[:, :], ns, ALU.subtract).then_inc(sk_ok, 1)
                else:
                    for b, t, h, w, bank, c, s in u.blocks:
                        last = V_.tensor_reduce(negm[:, b:b + 1], S[:, s:s + w], AX, ALU.max, negate=True)
                    last.then_inc(negm_ok, 1)
                dve.wait_ge(th_ok, u_of(u, j) + 1)
                own.link(V_.scalar_tensor_tensor(sz[:, :], th[:, :], 1.0, zf[:, :], ALU.add, ALU.mult))

            dve.wait_ge(const_in, 32)
            own.mark(V_.memset(qm[0:64, 1, :], 0.0))
            own.mark(V_.memset(qm[64:128, 0, :], 0.0))
            own.mark(V_.memset(kd[:, :, 0:P], 0.0))
            own.mark(V_.scalar_tensor_tensor(kgain[:, 0:1], col(G_AQ), float(A_DIM) ** -0.5, col(G_AK),
                                             ALU.mult, ALU.mult))
            own.mark(V_.scalar_tensor_tensor(kgain[:, 1:2], col(G_CQ), float(C_DIM) ** -0.5, col(G_CK),
                                             ALU.mult, ALU.mult))
            own.link(V_.tensor_scalar(nsink[:, :], col(SINKS, 8 * A_PAIRS), -1.0, None, ALU.mult))
            for k in range(KT):
                act_lo(k, 0, G_EVEN)
                if k == 3:
                    split_lo(Panel(0))
            split_lo(Panel(1))
            dve.wait_ge(ss_rt, 1)
            own.link(V_.reciprocal(rstd[:, :], krt[:, :]))
            for p in range(2):
                evac(Panel(p), kf[p][:, :]).then_inc(evac_done, 1)
                split_lo(Panel(2 + p))
            for p in range(2):
                evac(Panel(2 + p), vf[p][:, :]).then_inc(evac_done, 1)
                split_lo(Panel(4 + p))
                dve.wait_ge(krt_ok, p + 1)
                own.link(V_.reciprocal(kn[:, :], krt[:, :]))
                own.link(V_.scalar_tensor_tensor(kn[:, :], kf[p][:, :], kgain[:, 0:1], kn[:, :], ALU.mult, ALU.mult))
                for a in range(2):
                    for b in range(2):
                        last = V_.tensor_copy(kd[64 * b:64 * b + 64, 2 * p + a, P:P + T], kn[64 * a:64 * a + 64, :])
                        own.mark(last) if (a, b) != (1, 1) else last.then_inc(kd_ok, 1)
                dve.wait_ge(kd_ok, p + 1)
            dve.wait_ge(vT_mm, 2)
            dve.wait_ge(identb_ok, 1)
            own.mark(evac(Panel(GATES), gi[:, :], slice(0, 4)))
            evac(Panel(GATES), gf[:, :], slice(32, 36)).then_inc(evac_done, 1)
            split_lo(Panel(6))
            dve.wait_ge(evac_done, GATES + 1)
            own.mark(V_.memset(g1[:, :], 1.0))
            own.mark(V_.tensor_scalar(gi[:, :], gi[:, :], cols[0:4, I_BIAS:I_BIAS + 1], None, ALU.add))
            V_.tensor_scalar(gf[:, :], gf[:, :], cols[0:4, F_BIAS:F_BIAS + 1], None, ALU.add).then_inc(gate_f, 1)
            dve.wait_ge(gate_f, 1)
            dve.wait_ge(gate_u, 1)
            own.link(V_.scalar_tensor_tensor(gf[:, :], gf[:, :], 0.0, gu[:, :], ALU.min, ALU.subtract))
            own.link(V_.tensor_tensor_scan(gb[:, :], g1[:, :], gf[:, :], 0.0, ALU.mult, ALU.add))
            V_.tensor_tensor(ga[:, :], gi[:, :], gb[:, :], ALU.subtract).then_inc(gate_a, 1)
            dve.wait_ge(gate_a, 1)
            own.link(V_.tensor_tensor_scan(rows[:, 0, :], ga[:, :], ga[:, :], 0.0, ALU.max, ALU.max))
            V_.tensor_tensor(rows[:, 1, :], gb[:, :], rows[:, 0, :], ALU.add).then_inc(gate_a, 1)
            after_q(EVEN, 0, first=True)
            dve.wait_ge(acol_mm, 1)
            after_z(EVEN, 0, first=True)

            with dve.Fori(1, A_PAIRS) as j:
                own.enter(j, 1, EVEN_STEPS)
                after_q(EVEN, j)
                after_z(EVEN, j)
            own.leave(A_PAIRS - 1)

            def head(h, first=False):
                pn = [Panel(M0 + u, h, 8) for u in range(10)]
                if first:
                    dve.wait_ge(acol_ok, 1)
                own.mark(V_.tensor_copy(hp[:, :], cols[:, bass.ds(M_PAR + 12 * h, 12)]))
                own.mark(V_.tensor_copy(acur[:, :], acol[:, bass.ds(TT * h, TT)]))
                V_.tensor_copy(selcur[:, :], const[0:4, bass.ds(SEL + P * h, P)]).then_inc(m_par, 1)
                if first:
                    own.mark(V_.memset(cx[:, 0:3], 0.0))
                own.settle()
                for u, dst in ((0, qs), (1, ks)):
                    evac(pn[u], cx[:, 3:3 + T]).then_inc(evac_done, 1)
                    split_lo(pn[u + 2])
                    if first:
                        normalise(EVEN, A_PAIRS - 1) if u == 0 else gate_out(EVEN, A_PAIRS - 1)
                    dve.wait_ge(evac_done, pn[u].n + 1)
                    own.link(V_.tensor_scalar(cy[:, :], cx[:, 3:3 + T], hp[:, 4 * u + 3:4 * u + 4],
                                              hp[:, 8 + u:9 + u], ALU.mult, ALU.add))
                    for tap in range(3):
                        ins = V_.scalar_tensor_tensor(cy[:, :], cx[:, tap:tap + T], hp[:, 4 * u + tap:4 * u + tap + 1],
                                                      cy[:, :], ALU.mult, ALU.add)
                        own.link(ins) if tap < 2 else ins.then_inc(m_conv, 1)
                    dve.wait_ge(m_cth, 2 * h + u + 1)
                    V_.scalar_tensor_tensor(dst[:, :], cth[:, :], 1.0, cy[:, :], ALU.add, ALU.mult).then_inc(m_qk, 1)
                evac(pn[2], mvf[0][:, :]).then_inc(evac_done, 1)
                split_lo(pn[4])
                dve.wait_ge(m_bc, h + 1)
                for s in range(TT):
                    ins = V_.tensor_scalar(Tm[:, EOFF[s]:EOFF[s] + T - s * P], B[5][:, s * P:T], acur[:, s:s + 1], 0.0,
                                           ALU.subtract, ALU.max)
                ins.then_inc(m_T, 1)
                evac(pn[3], mvf[1][:, :]).then_inc(evac_done, 1)
                split_lo(pn[5])
                dve.wait_ge(m_st, h + 1)
                dve.wait_ge(m_sel, h + 1)
                for s, (bank, c) in enumerate([(2, 0), (3, 0), (4, 0), (3, 384)]):
                    w = T - s * P
                    e = E[:, EOFF[s]:EOFF[s] + w]
                    ins = V_.scalar_tensor_tensor(e, B[bank][:, c:c + w], 0.25 * float(M_QK) ** -0.5, e,
                                                  ALU.mult, ALU.mult)
                ins.then_inc(m_P, 1)
                for v in range(2):
                    if v:
                        dve.wait_ge(m_gth, 4 * h + 1)
                    evac(pn[4 + v], ogf[:, :]).then_inc(evac_done, 1)
                    split_lo(pn[6 + v])
                for v in range(2):
                    if v == 0:
                        dve.wait_ge(m_gth, 4 * h + 2)
                    evac(pn[6 + v], ogf[:, :]).then_inc(evac_done, 1)
                    split_lo(pn[8 + v])
                    dve.wait_ge(m_gth, 4 * h + 3 + v)
                    dve.wait_ge(evac_done, pn[6 + v].n + 1)
                    own.link(V_.scalar_tensor_tensor(G[v][:, :], m_th[:, :], 1.0, ogf[:, :], ALU.add, ALU.mult))
                    own.link(V_.scalar_tensor_tensor(G[v][:, :], tho[v][:, :], 1.0, G[v][:, :], ALU.add, ALU.mult))
                    if v == 0:
                        dve.wait_ge(m_num, h + 1)
                        dve.wait_ge(m_em, h + 1)
                        own.link(V_.tensor_tensor(dd[:, :], B[4][:, :], em[:, :], ALU.max))
                        own.link(V_.scalar_tensor_tensor(dd[:, :], B[4][:, :], -1.0, dd[:, :], ALU.mult, ALU.max))
                        own.link(V_.reciprocal(dd[:, :], dd[:, :]))
                        for w in range(2):
                            ins = V_.tensor_tensor(hn[w][:, :], B[2 + w][:, :], dd[:, :], ALU.mult)
                            own.mark(ins) if w == 0 else ins.then_inc(m_h, 1)
                dve.wait_ge(m_rtk, h + 1)
                own.link(V_.reciprocal(dd[:, :], em[:, :]))
                for v in range(2):
                    own.link(V_.scalar_tensor_tensor(hn[v][:, :], hn[v][:, :], hp[:, 10 + v:11 + v], dd[:, :],
                                                     ALU.mult, ALU.mult))
                    V_.scalar_tensor_tensor(xs[:, bass.ds(A_PAIRS + 2 * h + v, 1), :].rearrange("p a n -> p (a n)"),
                                            hn[v][:, :], 0.25, G[v][:, :], ALU.mult, ALU.mult).then_inc(m_cat, 1)

            head(0, first=True)
            with dve.Fori(1, M_HEADS) as h:
                own.enter(h, 1, HEAD_STEPS)
                head(h)
            own.leave(M_HEADS - 1)

            for k in range(KT):
                act_lo(k, 1)
            with dve.Fori(0, KT // 2) as i:
                for s in range(2):
                    pn = Panel(E0 + s, i, 2)
                    dve.wait_ge(mm_done, pn.n + 1)
                    dve.wait_ge(res_in[s], 16 * i + 16)
                    V_.tensor_tensor(xs[:, bass.ds(2 * i + s, 1), :].rearrange("p a n -> p (a n)"), B[pn.slot][:, :],
                                     res[s][:, :], ALU.add).then_inc(evac_done, 1)
                    split_lo(Panel(E0 + 2 + s, i, 2))

            for k in range(KT):
                act_lo(k, 2, G_ODD)
            dve.wait_ge(ss_rt, 2)
            V_.reciprocal(rstd[:, :], rt_tmp[:, :]).then_inc(rstd_ok, 1)
            dve.wait_ge(rstd_ok, 1)
            own.mark(evac(Panel(IKW), ik[0:64, :], slice(0, 64)))
            own.mark(evac(Panel(IKW), ik[64:128, :], slice(0, 64)))
            evac(Panel(IKW), iwf[:, :], slice(64, 72)).then_inc(evac_done, 1)
            split_lo(Panel(IKW + 2))
            for p in range(4):
                evac(Panel(IQ0 + p), iq[:, p, :]).then_inc(evac_done, 1)
                split_lo(Panel(IQ0 + p + 2))
            dve.wait_ge(iw_ok, 1)
            done = 0

            def add_scores(t):
                nonlocal done
                w, at = P * (t + 1), SC_AT[t]
                dst = sc[:, at:at + w]
                for h in range(C_IH):
                    dve.wait_ge(rl_ok, done + 1)
                    src = rl[done % 2][:, 0:w]
                    if h == 0:
                        V_.tensor_scalar(dst, src, iwt[:, t, h:h + 1], None, ALU.mult).then_inc(rl_used, 1)
                    else:
                        V_.scalar_tensor_tensor(dst, src, iwt[:, t, h:h + 1], dst, ALU.mult, ALU.add)\
                            .then_inc(rl_used, 1)
                    done += 1
                    dve.wait_ge(rl_used, done)
                own.link(V_.memset(sc[0:64, at + w - 64:at + w], FUTURE))

            def take(t, rounds):
                w, at = P * (t + 1), SC_AT[t]
                dst = sc[:, at:at + w]
                first = own.base + own.k + 1
                with dve.Fori(first, first + 2 * rounds, 2) as found:
                    V_.max(v8[:, :], dst).then_inc(dve_own, 1)
                    dve.wait_ge(rl_used, C_IH * t)
                    dve.wait_ge(dve_own, found)
                    V_.match_replace(dst, v8[:, :], dst, TAKEN).then_inc(dve_own, 1)
                    dve.wait_ge(dve_own, found + 1)
                own.k += 2 * rounds

            def make_mask(t):
                w, at = P * (t + 1), SC_AT[t]
                c = ODD.blocks[t][6]
                return V_.tensor_scalar(mask_c[:, c:c + w], sc[:, at:at + w], TAKEN * 0.9, NEG, ALU.is_gt, ALU.mult)

            for c in range(LT):
                if c == 0:
                    dve.wait_ge(x1_out, 16 * KT)
                    dve.wait_ge(h_lo, 3 * KT)
                evac(Panel(CKV + c), latf[:, c, :]).then_inc(evac_done, 1)
                split_lo(Panel(CKV + c + 2))
                if c < 2:
                    add_scores(c + 1)
                if c == 1:
                    take(1, 8)
            dve.wait_ge(lrt_ok, 1)
            own.link(V_.reciprocal(latr[:, :], latr[:, :]))
            for c in range(LT):
                V_.scalar_tensor_tensor(latf[:, c, :], latf[:, c, :], col(G_LAT + c), latr[:, :], ALU.mult, ALU.mult)\
                    .then_inc(lat_ok, 1)
            for c in range(LT):
                dve.wait_ge(lath_ok, c + 1)
                V_.tensor_tensor(latl[:, c, :], latf[:, c, :], lath[:, c, :].bitcast(F32), ALU.subtract)\
                    .then_inc(latl_ok, 1)
            add_scores(3)
            rounds = {0: [(1, 8), (2, 4)], 1: [(2, 8)], 2: [(2, 4), (3, 6)], 3: [(3, 10)]}
            for g in range(4):
                dve.wait_ge(mm_done, U0 + g + 1)
                for t in range(TT):
                    ins = V_.tensor_copy(V[:, t, g * T:(g + 1) * T], B[4 * (g % 2) + t][:, :])
                ins.then_inc(evac_done, 1)
                split_lo(Panel(U0 + g + 2))
                if g == 3:
                    dve.wait_ge(ck_mm, 1)
                    V_.tensor_copy(kfc[:, :], B[2][:, :]).then_inc(ckf_ok, 1)
                for t, r in rounds[g]:
                    take(t, r)
            own.mark(V_.memset(mask_c[:, 0:P], 0.0))
            own.settle()
            own.mark(V_.memset(mask_c[0:64, 64:128], NEG))
            for t in range(1, TT):
                ins = make_mask(t)
                own.mark(ins) if t < TT - 1 else ins.then_inc(mask_ok, 1)
            after_q(ODD, 0, first=True)
            dve.wait_ge(ckrt_ok, 1)
            own.link(V_.reciprocal(krc[:, :], krc[:, :]))
            V_.scalar_tensor_tensor(kk[:, :], kfc[:, :], kgain[:, 1:2], krc[:, :], ALU.mult, ALU.mult)\
                .then_inc(kk_ok, 1)
            after_z(ODD, 0, first=True)
            with dve.Fori(1, C_HEADS) as j:
                own.enter(j, 1, ODD_STEPS)
                after_q(ODD, j)
                after_z(ODD, j)
            own.leave(C_HEADS - 1)

            for k in range(KT - 1):
                act_lo(k, 3)
            normalise(ODD, C_HEADS - 1)
            gate_out(ODD, C_HEADS - 1)
            act_lo(KT - 1, 3)

            def odd_out(i, last=False):
                for s in range(2):
                    pn = Panel(F0 + s, i, 2)
                    dve.wait_ge(mm_done, pn.n + 1)
                    dve.wait_ge(res_in[s], 16 * (KT // 2) + 16 * i + 16)
                    if not isinstance(i, int) or i:
                        dve.wait_ge(y_out[s], 16 * i)
                    V_.tensor_tensor(yt[s][:, :], B[pn.slot][:, :], res[s][:, :], ALU.add).then_inc(evac_done, 1)
                    if not last:
                        split_lo(Panel(F0 + 2 + s, i, 2))

            odd_out(0)
            with dve.Fori(1, KT // 2 - 1) as i:
                odd_out(i)
            odd_out(KT // 2 - 1, last=True)


EVEN_STEPS = 2 + 1 + 8 + 1 + 1
ODD_STEPS = 1 + 1 + 4 + 1
HEAD_STEPS = 2 + 2 * 3 + 2 * 2 + 4 + 1 + 2


def buckets():
    rel = np.arange(NREL) - (T - 1)
    half, exact = NBUCKET // 2, NBUCKET // 4
    n = np.abs(rel)
    large = exact + (np.log(np.maximum(n, 1).astype(np.float32) / np.float32(exact))
                     / np.float32(np.log(1024 / exact)) * np.float32(half - exact)).astype(np.int32)
    return np.where(rel > 0, half, 0) + np.where(n < exact, n, np.minimum(large, half - 1))


def kernel(**inputs):
    import concourse.bacc as _bacc
    from concourse.bass_utils import run_bass_kernel_spmd as _run

    a = {k: np.asarray(v) for k, v in inputs.items()}
    f32 = np.float32

    def columns(w, c, n=P):
        return w[:, c:c + n].reshape(KT, P, n).transpose(1, 0, 2)

    we, wo = a["w_in_even"][0], a["w_in_odd"][0]
    panels = np.zeros((NPANEL, P, KT * P), f32)

    def put(n, block):
        panels[n].reshape(P, KT, P)[:, :, :block.shape[2]] = block

    for i in range(4):
        put(K0 + i, columns(we, 1024 + P * i))
    put(GATES, columns(we, 4608, 4))
    panels[GATES].reshape(P, KT, P)[:, :, 32:36] = columns(we, 4612, 4)
    for j in range(A_PAIRS):
        put(A0 + 2 * j, columns(we, P * j))
        put(A0 + 2 * j + 1, columns(we, 1536 + P * j))
    for h in range(M_HEADS):
        for u, c in enumerate([2560 + P * h, 3072 + P * h, 3584 + 256 * h, 3712 + 256 * h, 4616 + 256 * h,
                               4744 + 256 * h, 5640 + 256 * h, 5768 + 256 * h]):
            put(M0 + 8 * h + u, columns(we, c))
    iq_c = 2048 + 512
    ik_c = iq_c + C_IH * C_ID
    cz_c = ik_c + C_ID + C_IH
    put(IKW, columns(wo, ik_c, C_ID + C_IH))
    for i in range(4):
        put(IQ0 + i, columns(wo, iq_c + P * i))
        put(CKV + i, columns(wo, 2048 + P * i))
        uv = a["c_w_uv"][0][4 * i:4 * i + 4].reshape(4, LT, P, C_DIM)
        panels[U0 + i] = uv.transpose(2, 1, 0, 3).reshape(P, KT * P)
    for h in range(C_HEADS):
        put(O0 + 2 * h, columns(wo, P * h))
        put(O0 + 2 * h + 1, columns(wo, cz_c + P * h))
    for m in range(KT):
        put(E0 + m, columns(a["w_out_even"][0], P * m))
        put(F0 + m, columns(a["w_out_odd"][0], P * m))

    cols = np.zeros((P, NCOL), f32)
    cols[:, G_EVEN:G_EVEN + KT] = a["norm_even"][0].reshape(KT, P).T
    cols[:, G_ODD:G_ODD + KT] = a["norm_odd"][0].reshape(KT, P).T
    cols[:, G_AQ] = np.concatenate([a["a_q_norm"][0]] * 2)
    cols[:, G_AK] = np.concatenate([a["a_k_norm"][0]] * 2)
    cols[:, G_LAT:G_LAT + LT] = a["c_kv_norm"][0].reshape(LT, P).T
    cols[:, G_CQ] = a["c_q_norm"][0]
    cols[:, G_CK] = a["c_k_norm"][0]
    sinks = np.broadcast_to(a["a_sinks"][0].reshape(A_PAIRS, 1, 2), (A_PAIRS, TT, 2))
    cols[:, SINKS:SINKS + 8 * A_PAIRS] = sinks.reshape(1, -1)
    cols[0:4, I_BIAS] = a["b_i_bias"][0]
    cols[0:4, F_BIAS] = a["b_f_bias"][0]
    cw, cb = a["b_conv_w"][0], a["b_conv_b"][0]
    for h in range(M_HEADS):
        c = M_PAR + 12 * h
        for u in range(2):
            ch = slice(512 * u + P * h, 512 * u + P * h + P)
            cols[:, c + 4 * u:c + 4 * u + 4] = cw[:, ch].T
            cols[:, c + 8 + u] = cb[ch]
            cols[:, c + 10 + u] = a["b_out_norm"][0][256 * h + P * u:256 * h + P * u + P]

    const = np.zeros((P, NCONST), f32)
    const[:, IDENT:IDENT + P] = np.eye(P)
    const[0:64, BLOCK1:BLOCK1 + 64] = 1
    const[64:128, BLOCK1 + 64:BLOCK1 + 128] = 1
    const[:, ONES:ONES + P] = 1
    const[0:64, HEAD1] = 1
    const[64:128, HEAD1 + 1] = 1
    for h in range(4):
        const[h, SEL + P * h:SEL + P * h + P] = 1
    onehot = np.zeros((NBUCKET, NREL), f32)
    onehot[buckets()[:NREL - 1], np.arange(NREL - 1)] = 1

    arrays = {
        "panels": panels,
        "xT": np.ascontiguousarray(a["x"][0].T).reshape(KT, P, T),
        "cols_in": cols, "const_src": const, "onehot_in": onehot, "rel_in": np.ascontiguousarray(a["rel_bias"]),
        "wuk_src": np.ascontiguousarray(a["c_w_uk"][0].reshape(LT, P, C_DIM).transpose(1, 0, 2)),
    }
    nc = _bacc.Bacc("TRN2", target_bir_lowering=False, num_devices=1)
    t = {k: nc.dram_tensor(k, v.shape, F32, kind="ExternalInput").ap() for k, v in arrays.items()}
    outT = nc.dram_tensor("outT", (KT, P, T), F32, kind="ExternalOutput").ap()
    trunk_program(nc, t["panels"], t["xT"], t["cols_in"], t["const_src"], t["onehot_in"], t["rel_in"], t["wuk_src"],
                  outT)
    r = _run(nc, [arrays], core_ids=[0])
    got = r.results[0]["outT"].reshape(D, T)
    return np.ascontiguousarray(got.T).reshape(1, T, D)
```

```python
from contextlib import ExitStack

import numpy as np

import concourse.bass as bass
from concourse import mybir

F32 = mybir.dt.float32
F32R = mybir.dt.float32r
BF16 = mybir.dt.bfloat16
BYTES = {F32: 4, F32R: 4, BF16: 2}
ALU = mybir.AluOpType
ACT = mybir.ActivationFunctionType
AX = mybir.AxisListType.X

P = 128
D = 2048
T = 512
KT = D // P
TT = T // P
EPS = 1e-6
NEG = -1e30
POOL_TILES = range(6, 14)
LO_BEFORE = [0, KT, 2 * KT - len(POOL_TILES), 3 * KT - len(POOL_TILES)]
UNROLL = 4
TAKEN = -3e38
FUTURE = -1e38

A_DIM, A_PAIRS, A_KV = 64, 8, 4
M_HEADS, M_QK, M_V = 4, 128, 256
C_HEADS, C_DIM, C_LAT, C_IH, C_ID, TOPK = 16, 128, 512, 8, 64, 128
LT = C_LAT // P

K0 = 0
GATES = 4
A0 = 5
M0 = A0 + 2 * A_PAIRS
E0 = M0 + 8 * M_HEADS
IKW = E0 + KT
IQ0 = IKW + 1
CKV = IQ0 + 4
Q0 = CKV + LT
U0 = Q0 + 1
O0 = U0 + 3
F0 = O0 + 2 * C_HEADS
NPANEL = F0 + KT

NCOL = 0


def _cols(n):
    global NCOL
    NCOL += n
    return NCOL - n


G_EVEN = _cols(KT)
G_ODD = _cols(KT)
G_AQ = _cols(1)
G_AK = _cols(1)
G_LAT = _cols(LT)
G_CQ = _cols(1)
G_CK = _cols(1)
SINKS = _cols(8 * A_PAIRS)
I_BIAS = _cols(1)
F_BIAS = _cols(1)
M_PAR = _cols(12 * M_HEADS)
IDENT, BLOCK1, ONES, HEAD1, NCONST = 0, 128, 256, 384, 386
NREL = 640
NBUCKET = 32


class Panel:

    def __init__(self, base, j=0, per=0):
        self.n = base + per * j
        self.slot = base % 2
        self.fills = base // 2 + (per // 2) * j + 1
        self.primed = not isinstance(self.n, int) or self.n >= 2


class OwnSteps:

    def __init__(self, eng, sem):
        self.eng, self.sem, self.base, self.k = eng, sem, 0, 0

    def mark(self, ins):
        ins.then_inc(self.sem, 1)
        self.k += 1

    def settle(self):
        self.eng.wait_ge(self.sem, self.base + self.k)

    def link(self, ins):
        self.mark(ins)
        self.settle()

    def enter(self, i, first, per):
        self.start = self.base + self.k
        self.base, self.k, self.per = self.start + (i - first) * per, 0, per

    def leave(self, count):
        assert self.k == self.per, (self.k, self.per)
        self.base, self.k = self.start + count * self.per, 0


class Unit:

    def __init__(self, even):
        self.even = even
        if even:
            self.blocks = [(2 * t + h, t, h, 256 if t else P, 2 + t, h * 256, (2 * t + h) * 256)
                           for t in range(TT) for h in range(2)]
            pv = [(b, s + k * P, t + 1 - w // P + k) for b, t, h, w, _, _, s in self.blocks for k in range(w // P)]
        else:
            place = {0: (3, 384, 0), 1: (4, 0, 128), 2: (3, 0, 384), 3: (2, 0, 768)}
            self.blocks = [(t, t, 0, P * (t + 1), *place[t]) for t in range(TT)]
            pv = [(b, s + k * P, k) for b, t, h, w, _, _, s in self.blocks for k in range(t + 1)]
        self.pv = pv
        self.nb = len(self.blocks)
        self.ow = A_DIM if even else C_DIM
        self.banks = -(-len(pv) // 4)
        self.bw = 256 if even else T
        self.inv_dim = 1.0 / (A_DIM if even else C_DIM)


EVEN, ODD = Unit(True), Unit(False)


def trunk_program(nc, panels, xT, cols_in, const_src, onehot_in, rel_in, wuk_src, outT):
    x1T = nc.dram_tensor("x1T", (KT, P, T), F32, kind="Internal").ap()
    tab_d = nc.dram_tensor("tab_d", (16, NREL), F32, kind="Internal").ap()
    toep_d = nc.dram_tensor("toep_d", (16, P, T), F32, kind="Internal").ap()

    top = [-(-nc.sbuf_base // 64) * 64]

    def fixed(name, shape, dt=F32):
        size = int(np.prod(shape[1:])) * BYTES[dt]
        t = nc.alloc_sbuf_tensor_at(name, shape, dt, offset=top[0])
        top[0] += -(-size // 32) * 32
        return t

    def zone(start):
        at = [start]

        def place(name, shape, dt=F32):
            size = int(np.prod(shape[1:])) * BYTES[dt]
            t = nc.alloc_sbuf_tensor_at(name, shape, dt, offset=at[0])
            at[0] += -(-size // 32) * 32
            assert at[0] <= nc.sbuf_usable_end, (name, at[0])
            return t
        place.at = at
        return place

    xs_at = top[0]
    xs = fixed("xs", [P, KT, T])
    hh = fixed("hh", [P, KT, T], F32R)
    hl = fixed("hl", [P, KT, T], F32R)
    raw = [fixed(f"raw{i}", [P, KT, P]) for i in range(2)]
    wh = [fixed(f"wh{i}", [P, KT, P], F32R) for i in range(2)]
    wl = [fixed(f"wl{i}", [P, KT, P], F32R) for i in range(2)]
    const = fixed("const", [P, NCONST])
    cols = fixed("cols", [P, NCOL])
    rstd = fixed("rstd", [P, T])
    kgain = fixed("kgain", [P, 2])
    nsink = fixed("nsink", [P, 8 * A_PAIRS])
    epsc = fixed("epsc", [P, 1])
    rtq = fixed("rtq", [P, 8])
    rq = fixed("rq", [P, 8])
    negm = fixed("negm", [P, 8])
    sink_arg = fixed("sink_arg", [P, 8])
    sums = fixed("sums", [P, 8])
    esink = fixed("esink", [P, 8])
    rinv = fixed("rinv", [P, 8])
    iwt = fixed("iwt", [P, TT, C_IH])
    v8 = fixed("v8", [P, 8])
    region = top[0]

    za = zone(region)
    kd = za("kd", [P, A_KV, T])
    qm = za("qm", [P, 2, T])
    sq_a = za("sq_a", [P, T])
    bias_a = za("bias_a", [P, 2, 256])
    zf_a = za("zf_a", [P, T])
    th_a = za("th_a", [P, T])
    sz_a = za("sz_a", [P, T])
    s_at = za.at[0]
    S_a = za("S_a", [P, 8 * 256])
    pt_at = za.at[0]
    PT_a = za("PT_a", [P, 4 * T])
    os_a = za("os_a", [P, T])
    vA = za("vA", [P, TT, A_KV * A_DIM])
    za.at[0] += 2048
    keep_at = za.at[0]
    wm = za("wm", [P, 256])
    rows = za("rows", [4, 2, T])
    acol = za("acol", [P, 16])
    hp = za("hp", [P, 12])
    acur = za("acur", [P, TT])
    selcur = za("selcur", [4, P])
    once = za("once", [32, NREL])
    tab = za("tab", [16, NREL])
    rel_sb = za("rel_sb", [NBUCKET, 16])
    zs = zone(s_at)
    ss4 = zs("ss4", [P, 4, T])
    sq4 = zs("sq4", [P, 4, T])
    sqx = zone(region)("sqx", [P, 4, T])
    zs = zone(s_at)
    kf = [zs(f"kf{i}", [P, T]) for i in range(2)]
    vf = [zs(f"vf{i}", [P, T]) for i in range(2)]
    ksq = [zs(f"ksq{i}", [P, T]) for i in range(2)]
    krt = zs("krt", [P, T])
    kn = zs("kn", [P, T])
    zs = zone(s_at)
    gi, gf, gu, gb, ga, g1 = (zs(f"g_{x}", [4, T]) for x in "ifuba1")

    zm = zone(region)
    cx = zm("cx", [P, 3 + T])
    cy = zm("cy", [P, T])
    cth = zm("cth", [P, T])
    qs = zm("qs", [P, T])
    ks = zm("ks", [P, T])
    early_end = region + 4 * (A_KV * T + 3 * T)
    assert zm.at[0] <= early_end
    zm.at[0] = early_end
    mvf = [zm(f"mvf{i}", [P, T]) for i in range(2)]
    tho = [zm(f"tho{i}", [P, T]) for i in range(2)]
    G = [zm(f"G{i}", [P, T]) for i in range(2)]
    em = zm("em", [P, T])
    E = zm("E", [P, 1280])
    Tm = zm("Tm", [P, 1280])
    hn = [zm(f"hn{i}", [P, T]) for i in range(2)]
    vtm = zm("vtm", [P, TT, M_V])
    assert zm.at[0] <= keep_at
    dd = cy
    ogf, m_th = cx[:, 3:3 + T], cth

    zo = zone(region)
    V = zo("V", [P, TT, C_HEADS * C_DIM])
    kk = zo("kk", [P, T])
    q_c = zo("q_c", [P, T])
    zf_c = zo("zf_c", [P, T])
    s_o = zo.at[0]
    S_c = zo("S_c", [P, 1280])
    pt_o = zo.at[0]
    PT_c = zo("PT_c", [P, 1280])
    os_c = zo("os_c", [P, T])
    bias_c = zo("bias_c", [P, 1280])
    sq_c = PT_c[:, 0:T]
    mask_c = zo("mask_c", [P, 1280], BF16)
    th_c = os_c
    zq = zone(s_o)
    kfc = zq("kfc", [P, T])
    ksqc = zq("ksqc", [P, T])
    zq = zone(pt_o + 4 * T)
    krc = zq("krc", [P, T])
    zq = zone(region)
    iq = zq("iq", [P, TT, T])
    ik = zq("ik", [P, T])
    iwf = zq("iwf", [C_IH, T])
    rl = [zq(f"rl{i}", [P, T]) for i in range(4)]
    latsq = zq("latsq", [P, LT, T])
    latr = zq("latr", [P, T])
    assert zq.at[0] <= region + 4 * TT * C_HEADS * C_DIM
    zx = zone(xs_at)
    lath = zx("lath", [P, LT, T], F32R)
    latl = zx("latl", [P, LT, T], F32R)
    latf = zx("latf", [P, LT, T])
    sc = zx("sc", [P, 1152])
    wuk = zx("wuk", [P, LT, C_DIM])
    assert zx.at[0] <= xs_at + 4 * KT * T
    zt = zone(region)
    res = [zt(f"res{i}", [P, T]) for i in range(2)]
    yt = [zt(f"yt{i}", [P, T]) for i in range(2)]
    ptmp = zt("ptmp", [P, T])
    ssum = zt("ssum", [P, T])
    rt_tmp = zt("rt_tmp", [P, T])
    SC_AT = {1: 0, 2: 256, 3: 640}
    EOFF = [0, 512, 896, 1152]

    ident = const[:, IDENT:IDENT + P]
    block1 = const[:, BLOCK1:BLOCK1 + P]
    ones = const[:, ONES:ONES + P]
    head1 = const[:, HEAD1:HEAD1 + 2]

    def col(c, n=1):
        return cols[:, c:c + n]

    with ExitStack() as ctx:
        B = [ctx.enter_context(nc.psum_tensor(f"B{i}", [P, T], F32)) for i in range(8)]

        def sem(name):
            return ctx.enter_context(nc.semaphore(name))

        raw_in = [sem("raw_in0"), sem("raw_in1")]
        (hi_done, lo_done, mm_done, evac_done, h_hi, h_lo, const_in, tab_in, tab_mm, tab_sb, tab_out, toep_out,
         x_sq, x_ss, ss_mm, ss_rt, setup, rstd_ok, cols_ok, x_sqp, h_lo2, bias_ok) = map(sem, (
             "hi_done lo_done mm_done evac_done h_hi h_lo const_in tab_in tab_mm tab_sb tab_out toep_out "
             "x_sq x_ss ss_mm ss_rt setup rstd_ok cols_ok x_sqp h_lo2 bias_ok").split())
        x_in = [sem(f"x_in{i}") for i in range(4)]
        (ksq_ok, kss_mm, krt_ok, kd_ok, vT_mm, vA_ok, gate_f, gate_u, gate_a, acol_mm, acol_ok) = map(sem, (
            "ksq_ok kss_mm krt_ok kd_ok vT_mm vA_ok gate_f gate_u gate_a acol_mm acol_ok").split())
        (sq_ok, qss_mm, rtq_ok, lg_mm, bias_in, negm_ok, sk_ok, p_ok, pt_mm, pt_ok, pv_mm, os_ok, oT_mm, cat_ok,
         th_ok) = map(sem, ("sq_ok qss_mm rtq_ok lg_mm bias_in negm_ok sk_ok p_ok pt_mm pt_ok pv_mm os_ok oT_mm "
                            "cat_ok th_ok").split())
        (m_par, m_conv, m_cth, m_qk, m_bc, m_st, m_T, m_E, m_sel, m_P, m_vT, m_vA, m_gth, m_num, m_h, m_hsq, m_ss,
         m_rtk, m_cat, m_em) = map(sem, ("m_par m_conv m_cth m_qk m_bc m_st m_T m_E m_sel m_P m_vT m_vA m_gth m_num m_h "
                                   "m_hsq m_ss m_rtk m_cat m_em").split())
        res_in = [sem("res_in0"), sem("res_in1")]
        x1_out = sem("x1_out")
        y_out = [sem("y_out0"), sem("y_out1")]
        (iw_mm, iw_ok, isc_mm, rl_ok, rl_used, rl_used3, lsq_ok, lss_mm, lrt_ok, lat_ok, lath_ok, latl_ok, ck_mm,
         cksq_ok, ckss_mm, ckrt_ok, kk_ok, mask_ok, x1_ss, wuk_in) = map(sem, (
             "iw_mm iw_ok isc_mm rl_ok rl_used rl_used3 lsq_ok lss_mm lrt_ok lat_ok lath_ok latl_ok ck_mm "
             "cksq_ok ckss_mm ckrt_ok kk_ok mask_ok x1_ss wuk_in").split())
        found8 = [sem(f"found8_{r}") for r in range(UNROLL)]
        taken8 = [sem(f"taken8_{r}") for r in range(UNROLL)]
        dve_own, act_own, pool_own = sem("dve_own"), sem("act_own"), sem("pool_own")

        def u_of(u, j):
            return j if u.even else A_PAIRS + j

        def pt_of(u, j):
            return 4 * j if u.even else 4 * A_PAIRS + ODD.banks * j

        block = ctx.enter_context(nc.Block())

        @block.sync
        def _(sp):
            def load(pn):
                if pn.primed:
                    sp.wait_ge(lo_done, pn.n - 1)
                sp.dma_start(raw[pn.slot][:, :, :].rearrange("p k c -> p (k c)"),
                             panels[bass.ds(pn.n, 1), :, :].rearrange("a p n -> p (a n)")).then_inc(raw_in[pn.slot], 16)

            sp.dma_start(cols[:, :], cols_in).then_inc(cols_ok, 16)
            for c in range(4):
                sp.dma_start(xs[:, 4 * c:4 * c + 4, :],
                             xT[4 * c:4 * c + 4, :, :].rearrange("k p n -> p k n")).then_inc(x_in[c], 16)
                if c < 2:
                    load(Panel(c))
            sp.dma_start(const[:, :], const_src).then_inc(const_in, 16)
            with sp.Fori(1, NPANEL // 2) as i:
                load(Panel(0, i, 2))
                load(Panel(1, i, 2))

        @block.gpsimd
        def _(pool):
            own = OwnSteps(pool, pool_own)
            pool.memset(epsc[:, :], EPS).then_inc(setup, 1)
            for c, sq in ((0, ss4), (1, sq4)):
                pool.wait_ge(x_in[c], 16)
                own.mark(pool.tensor_tensor(sq[:, :, :], xs[:, 4 * c:4 * c + 4, :], xs[:, 4 * c:4 * c + 4, :],
                                            ALU.mult))
            own.settle()
            pool.tensor_tensor(ss4[:, :, :], ss4[:, :, :], sq4[:, :, :], ALU.add).then_inc(x_sqp, 1)
            pool.dma_start(once[:, :], onehot_in).then_inc(tab_in, 16)
            pool.dma_start(rel_sb[:, :], rel_in).then_inc(tab_in, 16)
            own.link(pool.memset(wm[:, :], NEG))
            own.mark(pool.memset(wm[0:64, 64:192], 0.0))
            own.link(pool.memset(wm[64:128, 128:256], 0.0))
            pool.wait_ge(tab_sb, 1)
            pool.dma_start(tab_d, tab[:, :]).then_inc(tab_out, 16)
            pool.wait_ge(tab_out, 16)
            pool.dma_start(toep_d, bass.AP(tab_d.tensor, P - 1, [[NREL, 16], [-1, P], [1, T]])).then_inc(toep_out, 16)
            pool.wait_ge(toep_out, 16)

            def load_bias_a(j):
                pool.dma_start(bias_a[:, :, :], toep_d[bass.ds(2 * j, 2), :, 256:512].rearrange("a p n -> p a n"))\
                    .then_inc(bias_in, 16)

            def mask_bias_a(unit):
                pool.wait_ge(bias_in, 16 * unit)
                pool.tensor_tensor(bias_a[:, :, :], bias_a[:, :, :], wm[:, :].unsqueeze(1).to_broadcast([P, 2, 256]),
                                   ALU.add).then_inc(bias_ok, 1)

            load_bias_a(0)
            mask_bias_a(1)
            with pool.Fori(1, A_PAIRS) as j:
                pool.wait_ge(negm_ok, j)
                load_bias_a(j)
                mask_bias_a(j + 1)

            with pool.Fori(1, M_HEADS + 1) as made:
                pool.wait_ge(cat_ok, A_PAIRS)
                pool.wait_ge(m_E, made)
                for s in range(TT):
                    blk = E[:, EOFF[s]:EOFF[s] + P]
                    last = pool.affine_select(out=blk, in_=blk, pattern=[[1, P]], compare_op=ALU.is_ge, fill=0.0,
                                              base=0, channel_multiplier=-1)
                last.then_inc(m_sel, 1)

            def act_lo2(phase):
                for i, k in enumerate(POOL_TILES):
                    pool.wait_ge(h_hi, KT * phase + k + 1)
                    pool.tensor_tensor(hl[:, k, :], xs[:, k, :], hh[:, k, :].bitcast(F32), ALU.subtract)\
                        .then_inc(h_lo2, 1)

            act_lo2(1)

            def load_res(src, m, s):
                pool.dma_start(res[s][:, :], src[bass.ds(m, 1), :, :].rearrange("a p n -> p (a n)"))\
                    .then_inc(res_in[s], 16)

            pool.wait_ge(m_cat, 2 * M_HEADS)
            own.link(pool.memset(ssum[:, :], 0.0))
            load_res(xT, 0, 0)
            load_res(xT, 1, 1)

            def even_out(i, last=False):
                for s in range(2):
                    m = 2 * i + s
                    pool.wait_ge(evac_done, E0 + m + 1)
                    pool.dma_start(x1T[bass.ds(m, 1), :, :].rearrange("a p n -> p (a n)"),
                                   xs[:, bass.ds(m, 1), :].rearrange("p a n -> p (a n)")).then_inc(x1_out, 16)
                    if not last:
                        load_res(xT, m + 2, s)
                    tile = xs[:, bass.ds(m, 1), :].rearrange("p a n -> p (a n)")
                    own.link(pool.tensor_tensor(ptmp[:, :], tile, tile, ALU.mult))
                    add = pool.tensor_tensor(ssum[:, :], ssum[:, :], ptmp[:, :], ALU.add)
                    add.then_inc(x1_ss, 1) if last and s else own.link(add)

            with pool.Fori(0, KT // 2 - 1) as i:
                own.enter(i, 0, 4)
                even_out(i)
            own.leave(KT // 2 - 1)
            even_out(KT // 2 - 1, last=True)
            pool.wait_ge(x1_out, 16 * KT)
            pool.wait_ge(h_lo, LO_BEFORE[3])
            pool.dma_start(wuk[:, :, :], wuk_src).then_inc(wuk_in, 16)

            def load_bias_c(h):
                for b, t, _, w, _, _, c in ODD.blocks:
                    pool.dma_start(bias_c[:, c:c + w], toep_d[bass.ds(h, 1), :, T - w:T].rearrange("a p n -> p (a n)"))\
                        .then_inc(bias_in, 16)

            def mask_bias_c(h):
                pool.wait_ge(bias_in, 16 * A_PAIRS + 64 * h + 64)
                pool.tensor_tensor(bias_c[:, :], bias_c[:, :], mask_c[:, :], ALU.add).then_inc(bias_ok, 1)

            load_bias_c(0)
            pool.wait_ge(iw_ok, 1)
            t = TT - 1
            dst = sc[:, SC_AT[t]:SC_AT[t] + T]
            for h in range(C_IH):
                pool.wait_ge(rl_ok, C_IH * 2 + h + 1)
                r = rl[h % 4][:, :]
                if h == 0:
                    pool.tensor_scalar(dst, r, iwt[:, t, h:h + 1], None, ALU.mult).then_inc(rl_used3, 1)
                else:
                    own.link(pool.tensor_scalar(r, r, iwt[:, t, h:h + 1], None, ALU.mult))
                    pool.tensor_tensor(dst, dst, r, ALU.add).then_inc(rl_used3, 1)
                pool.wait_ge(rl_used3, h + 1)
            pool.wait_ge(lo_done, U0)
            for n in range(U0, O0 + 3):
                pool.wait_ge(hi_done, n + 1)
                pool.tensor_tensor(wl[n % 2][:, :, :], raw[n % 2][:, :, :], wh[n % 2][:, :, :].bitcast(F32),
                                   ALU.subtract).then_inc(lo_done, 1)
            pool.wait_ge(mask_ok, 1)
            mask_bias_c(0)
            with pool.Fori(1, C_HEADS) as h:
                pool.wait_ge(negm_ok, A_PAIRS + h)
                load_bias_c(h)
                mask_bias_c(h)
            act_lo2(3)

            pool.wait_ge(pv_mm, A_PAIRS + C_HEADS)
            load_res(x1T, 0, 0)
            load_res(x1T, 1, 1)

            def odd_out(i, last=False):
                for s in range(2):
                    m = 2 * i + s
                    pool.wait_ge(evac_done, F0 + m + 1)
                    pool.dma_start(outT[bass.ds(m, 1), :, :].rearrange("a p n -> p (a n)"), yt[s][:, :])\
                        .then_inc(y_out[s], 16)
                    if not last:
                        load_res(x1T, m + 2, s)

            with pool.Fori(0, KT // 2 - 1) as i:
                odd_out(i)
            odd_out(KT // 2 - 1, last=True)
            pool.wait_ge(y_out[0], 16 * KT // 2)
            pool.wait_ge(y_out[1], 16 * KT // 2)

        @block.tensor
        def _(pe):
            def mm(out, lhsT, rhs, start=True, stop=True):
                return nc.tensor.matmul(out, lhsT, rhs, start=start, stop=stop)

            def wait_tile(phase, k):
                if phase in (1, 3) and k in POOL_TILES:
                    pe.wait_ge(h_lo2, len(POOL_TILES) * (phase // 2) + POOL_TILES.index(k) + 1)
                else:
                    mine = k if phase in (0, 2) or k < POOL_TILES[0] else k - len(POOL_TILES)
                    pe.wait_ge(h_lo, LO_BEFORE[phase] + mine + 1)

            def main_panel(pn, conv=None, between=None, tiles=range(KT)):
                if tiles[0] == 0:
                    pe.wait_ge(lo_done, pn.n + 1)
                    if pn.primed:
                        pe.wait_ge(evac_done, pn.n - 1)
                acc, w1, w2 = B[pn.slot], wh[pn.slot], wl[pn.slot]
                for k in tiles:
                    if between and k in between:
                        between[k]()
                    if conv is not None:
                        wait_tile(conv, k)
                    mm(acc[:, :], w1[:, k, :], hh[:, k, :], k == 0, False)
                    mm(acc[:, :], w1[:, k, :], hl[:, k, :], False, False)
                    last = mm(acc[:, :], w2[:, k, :], hh[:, k, :], False, k == KT - 1)
                if tiles[-1] == KT - 1:
                    last.then_inc(mm_done, 1)

            def transpose4(bank, src, rows_=P):
                for t in range(TT):
                    last = nc.tensor.transpose(bank[:, t * P:t * P + rows_], src[:, t * P:(t + 1) * P],
                                               ident[0:rows_, 0:rows_])
                return last

            def logits(u, j):
                q, sq, k = (None, sq_a, kd) if u.even else (q_c, sq_c, kk)
                pe.wait_ge(sq_ok, u_of(u, j) + 1)
                for t in range(TT):
                    w = 2 if u.even else 1
                    last = mm(B[6][:, w * t:w * t + w], sq[:, t * P:(t + 1) * P],
                              head1 if u.even else ones[:, 0:1])
                last.then_inc(qss_mm, 1)
                for b, t, h, w, bank, c, _ in u.blocks:
                    dst = B[bank][:, c:c + w]
                    if u.even:
                        last = mm(dst, qm[:, h, t * P:(t + 1) * P],
                                  kd[:, :, :].rearrange("p g n -> p (g n)")[:, bass.ds((j // 2) * T + (t + 1) * P - w, w)])
                    else:
                        last = mm(dst, q_c[:, t * P:(t + 1) * P], kk[:, 0:w])
                last.then_inc(lg_mm, 1)

            def transpose_weights(u, j):
                S = S_a if u.even else S_c
                pe.wait_ge(p_ok, u_of(u, j) + 1)
                n = len(u.pv)
                for i, (b, s, _) in enumerate(u.pv):
                    last = nc.tensor.transpose(B[2 + i // 4][:, (i % 4) * P:(i % 4 + 1) * P], S[:, s:s + P], ident)
                    if i % 4 == 3 or i == n - 1:
                        last.then_inc(pt_mm, 1)

            def weighted_values(u, j):
                PT, n = PT_a if u.even else PT_c, len(u.pv)
                for i, (b, _, vt) in enumerate(u.pv):
                    if i % 4 == 0:
                        pe.wait_ge(pt_ok, pt_of(u, j) + i // 4 + 1)
                    if u.even:
                        rhs = vA[:, vt, bass.ds((j // 2) * A_DIM, A_DIM)]
                    else:
                        rhs = V[:, vt, bass.ds(j * C_DIM, C_DIM)]
                    last = mm(B[6][:, b * u.ow:(b + 1) * u.ow], PT[:, i * P:(i + 1) * P], rhs,
                              i == 0 or u.pv[i - 1][0] != b, i == n - 1 or u.pv[i + 1][0] != b)
                last.then_inc(pv_mm, 1)

            def rest_of_unit(u, j):
                return {0: lambda: transpose_weights(u, j), 6: lambda: weighted_values(u, j),
                        12: lambda: outputs(u, j)}

            def outputs(u, j):
                pe.wait_ge(os_ok, u_of(u, j) + 1)
                transpose4(B[7], os_a if u.even else os_c).then_inc(oT_mm, 1)

            def sum_squares():
                pe.wait_ge(tab_in, 32)
                mm(B[2][0:16, 0:512], rel_sb[:, :], once[:, 0:512])
                mm(B[3][0:16, 0:NREL - 512], rel_sb[:, :], once[:, 512:NREL]).then_inc(tab_mm, 1)
                pe.wait_ge(const_in, 16)
                pe.wait_ge(x_ss, 2)
                for k in range(4):
                    last = mm(B[7][:, :], ones, ss4[:, k, :], k == 0, k == 3)
                last.then_inc(ss_mm, 1)

            main_panel(Panel(0), conv=0)
            main_panel(Panel(1), between={8: sum_squares})
            main_panel(Panel(2))
            for p in range(2):
                if p:
                    main_panel(Panel(3))
                if p == 0:
                    pe.wait_ge(tab_sb, 1)
                pe.wait_ge(ksq_ok, p + 1)
                mm(B[2 + p][:, :], block1, ksq[p][:, :]).then_inc(kss_mm, 1)
            pe.wait_ge(evac_done, 3)
            transpose4(B[4], vf[0]).then_inc(vT_mm, 1)
            main_panel(Panel(4))
            pe.wait_ge(evac_done, 4)
            transpose4(B[5], vf[1]).then_inc(vT_mm, 1)
            def gate_columns():
                pe.wait_ge(gate_a, 1)
                for t in range(TT):
                    last = nc.tensor.transpose(B[7][:, 4 * t:4 * t + 4], ga[:, t * P:(t + 1) * P], ident[0:4, 0:4])
                last.then_inc(acol_mm, 1)

            main_panel(Panel(5))
            main_panel(Panel(6), between={8: gate_columns})
            pe.wait_ge(kd_ok, 2)
            pe.wait_ge(vA_ok, 2)
            logits(EVEN, 0)

            def unit(u, base, j):
                main_panel(Panel(base, j, 2))
                main_panel(Panel(base + 1, j, 2), between=rest_of_unit(u, j - 1))
                logits(u, j)

            pe.wait_ge(acol_ok, 1)
            with pe.Fori(1, A_PAIRS) as j:
                unit(EVEN, A0, j)

            def head(h, first=False):
                pn = [Panel(M0 + u, h, 8) for u in range(8)]
                main_panel(pn[0])
                main_panel(pn[1], between=rest_of_unit(EVEN, A_PAIRS - 1) if first else None)
                main_panel(pn[2])
                pe.wait_ge(m_par, h + 1)
                if first:
                    pe.wait_ge(gate_a, 2)
                mm(B[5][:, :], selcur[:, :], rows[:, 0, :])
                mm(B[6][:, :], selcur[:, :], rows[:, 1, :]).then_inc(m_bc, 1)
                pe.wait_ge(m_qk, 2 * h + 2)
                for s, (bank, c) in enumerate([(2, 0), (3, 0), (4, 0), (3, 384)]):
                    last = mm(B[bank][:, c:c + T - s * P], ks[:, s * P:(s + 1) * P], qs[:, s * P:T])
                last.then_inc(m_st, 1)
                main_panel(pn[3])
                if first:
                    pe.wait_ge(cat_ok, A_PAIRS)
                pe.wait_ge(evac_done, pn[2].n + 1)
                transpose4(B[7], mvf[0]).then_inc(m_vT, 1)
                main_panel(pn[4])
                pe.wait_ge(evac_done, pn[3].n + 1)
                pe.wait_ge(m_vA, 2 * h + 1)
                transpose4(B[7], mvf[1]).then_inc(m_vT, 1)
                main_panel(pn[5])
                pe.wait_ge(m_vA, 2 * h + 2)
                pe.wait_ge(m_P, h + 1)
                for v in range(2):
                    for s in range(TT):
                        mm(B[2 + v][:, s * P:T], vtm[:, s, v * P:(v + 1) * P], E[:, EOFF[s]:EOFF[s] + T - s * P],
                           s == 0, s == TT - 1)
                for s in range(TT):
                    last = mm(B[4][:, s * P:T], ones, E[:, EOFF[s]:EOFF[s] + T - s * P], s == 0, s == TT - 1)
                last.then_inc(m_num, 1)
                main_panel(pn[6])

                def head_squares():
                    pe.wait_ge(m_hsq, h + 1)
                    for v in range(2):
                        last = mm(B[5][:, :], ones, Tm[:, v * T:(v + 1) * T], v == 0, v == 1)
                    last.then_inc(m_ss, 1)

                main_panel(pn[7], between={2: head_squares})

            head(0, first=True)
            with pe.Fori(1, M_HEADS) as h:
                head(h)

            main_panel(Panel(E0), conv=1)
            main_panel(Panel(E0 + 1))
            with pe.Fori(1, KT // 2) as i:
                main_panel(Panel(E0, i, 2))
                main_panel(Panel(E0 + 1, i, 2))

            main_panel(Panel(IKW), conv=2)
            pe.wait_ge(x1_ss, 1)
            mm(B[7][:, :], ones, ssum[:, :]).then_inc(ss_mm, 1)
            main_panel(Panel(IKW + 1))
            main_panel(Panel(IKW + 2))
            pe.wait_ge(evac_done, IKW + 1)
            pe.wait_ge(ss_rt, 2)
            for t in range(TT):
                last = nc.tensor.transpose(B[7][:, C_IH * t:C_IH * (t + 1)], iwf[:, t * P:(t + 1) * P],
                                           ident[0:C_IH, 0:C_IH])
            last.then_inc(iw_mm, 1)
            main_panel(Panel(IKW + 3))
            main_panel(Panel(IKW + 4))
            done = 0

            def index_scores(t, half):
                nonlocal done
                pe.wait_ge(evac_done, IQ0 + 4)
                w = P * (t + 1)
                for h in range(4 * half, 4 * half + 4):
                    if done >= 4:
                        pe.wait_ge(rl_ok, done - 3)
                    r = slice(64 * (h % 2), 64 * (h % 2) + 64)
                    mm(B[2 + done % 4][:, 0:w], iq[r, h // 2, t * P:(t + 1) * P], ik[r, 0:w]).then_inc(isc_mm, 1)
                    done += 1

            for c in range(3):
                main_panel(Panel(CKV + c), between={5: lambda: index_scores(c + 1, 0),
                                                    11: lambda: index_scores(c + 1, 1)})
            main_panel(Panel(CKV + 3))
            pe.wait_ge(lsq_ok, LT)
            for c in range(LT):
                last = mm(B[6][:, :], ones, latsq[:, c, :], c == 0, c == LT - 1)
            last.then_inc(lss_mm, 1)
            main_panel(Panel(Q0))
            pe.wait_ge(wuk_in, 16)
            pe.wait_ge(lat_ok, LT)
            for c in range(LT):
                last = mm(B[6][:, :], wuk[:, c, :], latf[:, c, :], c == 0, c == LT - 1)
            last.then_inc(ck_mm, 1)

            for g in range(4):
                pn = Panel(U0 + g)
                pe.wait_ge(lo_done, pn.n + 1)
                if g == 0:
                    pe.wait_ge(latl_ok, LT)
                    pe.wait_ge(evac_done, U0)
                    pe.wait_ge(rl_ok, 3 * C_IH)
                if g == 1:
                    pe.wait_ge(cksq_ok, 1)
                    mm(B[7][:, :], ones, ksqc[:, :]).then_inc(ckss_mm, 1)
                if g >= 2:
                    pe.wait_ge(evac_done, pn.n - 1)
                w1 = wh[pn.slot][:, :, :].rearrange("p (c a) n -> p c (a n)", c=LT)
                w2 = wl[pn.slot][:, :, :].rearrange("p (c a) n -> p c (a n)", c=LT)
                for t in range(TT):
                    if (g, t) == (1, 3):
                        pe.wait_ge(ckrt_ok, 1)
                    dst = B[4 * (g % 2) + t][:, :]
                    tok = slice(t * P, (t + 1) * P)
                    for c in range(LT):
                        mm(dst, lath[:, c, tok], w1[:, c, :], c == 0, False)
                        mm(dst, lath[:, c, tok], w2[:, c, :], False, False)
                        last = mm(dst, latl[:, c, tok], w1[:, c, :], False, c == LT - 1)
                last.then_inc(mm_done, 1)
            main_panel(Panel(O0 + 1))
            pe.wait_ge(evac_done, O0 + 1)
            pe.wait_ge(kk_ok, 1)
            logits(ODD, 0)

            with pe.Fori(1, C_HEADS) as j:
                unit(ODD, O0, j)

            main_panel(Panel(F0), conv=3, tiles=range(KT - 1))
            main_panel(Panel(F0 + 1), tiles=range(KT - 1), between=rest_of_unit(ODD, C_HEADS - 1))
            main_panel(Panel(F0), conv=3, tiles=[KT - 1])
            main_panel(Panel(F0 + 1), tiles=[KT - 1])
            with pe.Fori(1, KT // 2) as i:
                main_panel(Panel(F0, i, 2))
                main_panel(Panel(F0 + 1, i, 2))

        @block.scalar
        def _(act):
            own = OwnSteps(act, act_own)
            A = nc.scalar.activation

            def split_hi(pn):
                act.wait_ge(raw_in[pn.slot], 16 * pn.fills)
                if pn.primed:
                    act.wait_ge(mm_done, pn.n - 1)
                A(wh[pn.slot][:, :, :], raw[pn.slot][:, :, :], ACT.Copy).then_inc(hi_done, 1)

            def act_hi(k, gain=None):
                A(hh[:, k, :], xs[:, k, :], ACT.Copy, scale=col(gain + k) if gain is not None else 1.0)\
                    .then_inc(h_hi, 1)

            def after_q(u, j, first=False, lookahead=True):
                pn = Panel(A0 if u.even else O0, j, 2)
                act.wait_ge(mm_done, pn.n + 1)
                if not first:
                    move_blocks(u, j - 1)
                split_hi(Panel((A0 if u.even else O0) + 2, j, 2))
                act.wait_ge(evac_done, pn.n + 1)
                if u.even:
                    A(sq_a[0:64, :], qm[0:64, 0, :], ACT.Square)
                    A(sq_a[64:128, :], qm[64:128, 1, :], ACT.Square).then_inc(sq_ok, 1)
                else:
                    act.wait_ge(pv_mm, u_of(u, j))
                    A(sq_c, q_c[:, :], ACT.Square).then_inc(sq_ok, 1)

            def move_blocks(u, j):
                PT = PT_a if u.even else PT_c
                for i in range(u.banks):
                    act.wait_ge(pt_mm, pt_of(u, j) + i + 1)
                    w = min(T, P * len(u.pv) - i * T)
                    A(PT[:, i * T:i * T + w], B[2 + i][:, 0:w], ACT.Copy).then_inc(pt_ok, 1)

            def after_z(u, j, last=False):
                base = (A0 if u.even else O0) + 1
                S, zf, th = (S_a, zf_a, th_a) if u.even else (S_c, zf_c, th_c)
                n = 8 if u.even else 4
                act.wait_ge(qss_mm, u_of(u, j) + 1)
                A(rtq[:, 0:n], B[6][:, 0:n], ACT.Sqrt, bias=epsc[:, :], scale=u.inv_dim).then_inc(rtq_ok, 1)
                if not last:
                    split_hi(Panel(base + 2, j, 2))
                else:
                    for k in range(8):
                        act.wait_ge(cat_ok, A_PAIRS + k + 1)
                        act_hi(k)
                act.wait_ge(evac_done, Panel(base, j, 2).n + 1)
                A(th[:, :], zf[:, :], ACT.Tanh, scale=0.5).then_inc(th_ok, 1)
                act.wait_ge(negm_ok, u_of(u, j) + 1)
                for b, t, h, w, _, _, s in u.blocks:
                    ins = A(S[:, s:s + w], S[:, s:s + w], ACT.Exp, bias=negm[:, b:b + 1],
                            accum_out=sums[:, b:b + 1])
                if u.even:
                    act.wait_ge(sk_ok, j + 1)
                    ins = A(esink[:, :], sink_arg[:, :], ACT.Exp)
                ins.then_inc(p_ok, 1)

            act.wait_ge(cols_ok, 16)
            for c in range(4):
                act.wait_ge(x_in[c], 16)
                for k in range(4 * c, 4 * c + 4):
                    act_hi(k, G_EVEN)
                if c < 2:
                    split_hi(Panel(c))
            A(sqx[:, :, :], xs[:, 8:12, :], ACT.Square).then_inc(x_sq, 1)
            act.wait_ge(x_sqp, 1)
            A(sq4[:, :, :], xs[:, 12:16, :], ACT.Square).then_inc(x_sq, 1)
            act.wait_ge(tab_mm, 1)
            A(tab[:, 0:512], B[2][0:16, :], ACT.Copy)
            A(tab[:, 512:NREL], B[3][0:16, 0:NREL - 512], ACT.Copy).then_inc(tab_sb, 1)
            act.wait_ge(ss_mm, 1)
            act.wait_ge(setup, 1)
            A(krt[:, :], B[7][:, :], ACT.Sqrt, bias=epsc[:, :], scale=1.0 / D).then_inc(ss_rt, 1)
            for p in range(2):
                split_hi(Panel(2 + p))
                act.wait_ge(evac_done, p + 1)
                A(ksq[p][:, :], kf[p][:, :], ACT.Square).then_inc(ksq_ok, 1)
            for p in range(2):
                split_hi(Panel(4 + p))
                act.wait_ge(kss_mm, p + 1)
                if p:
                    act.wait_ge(kd_ok, 1)
                A(krt[:, :], B[2 + p][:, :], ACT.Sqrt, bias=epsc[:, :], scale=1.0 / A_DIM).then_inc(krt_ok, 1)
                act.wait_ge(vT_mm, p + 1)
                A(vA[:, :, p * P:(p + 1) * P], B[4 + p][:, :].rearrange("p (t d) -> p t d", t=TT),
                  ACT.Copy).then_inc(vA_ok, 1)
            split_hi(Panel(6))
            act.wait_ge(gate_f, 1)
            own.link(A(gu[:, :], gf[:, :], ACT.Abs))
            own.link(A(gu[:, :], gu[:, :], ACT.Exp, scale=-1.0))
            A(gu[:, :], gu[:, :], ACT.Ln, bias=ones[0:4, 0:1]).then_inc(gate_u, 1)
            after_q(EVEN, 0, first=True)
            act.wait_ge(acol_mm, 1)
            A(acol[:, :].rearrange("p (h t) -> p t h", t=TT), B[7][:, 0:16].rearrange("p (t h) -> p t h", t=TT),
              ACT.Copy).then_inc(acol_ok, 1)
            after_z(EVEN, 0)

            with act.Fori(1, A_PAIRS) as j:
                after_q(EVEN, j)
                after_z(EVEN, j)

            def head(h, first=False, last=False):
                pn = [Panel(M0 + u, h, 8) for u in range(10)]

                def ahead(u):
                    act.wait_ge(mm_done, pn[u].n + 1)
                    split_hi(pn[u + 2])

                for u in range(2):
                    ahead(u)
                    if first and u == 0:
                        move_blocks(EVEN, A_PAIRS - 1)
                    act.wait_ge(m_conv, 2 * h + u + 1)
                    A(cth[:, :], cy[:, :], ACT.Tanh, scale=0.5).then_inc(m_cth, 1)
                ahead(2)
                act.wait_ge(m_bc, h + 1)
                A(em[:, :], B[6][:, :], ACT.Exp, scale=-1.0).then_inc(m_em, 1)
                act.wait_ge(m_T, h + 1)
                for s in range(TT):
                    c = slice(EOFF[s], EOFF[s] + T - s * P)
                    ins = A(E[:, c], Tm[:, c], ACT.Exp, scale=-1.0)
                ins.then_inc(m_E, 1)
                for v in range(2):
                    ahead(3 + v)
                    if v:
                        act.wait_ge(evac_done, pn[4].n + 1)
                        A(tho[0][:, :], ogf[:, :], ACT.Tanh, scale=0.5).then_inc(m_gth, 1)
                    act.wait_ge(m_vT, 2 * h + v + 1)
                    A(vtm[:, :, v * P:(v + 1) * P], B[7][:, :].rearrange("p (t d) -> p t d", t=TT),
                      ACT.Copy).then_inc(m_vA, 1)
                ahead(5)
                act.wait_ge(evac_done, pn[5].n + 1)
                A(tho[1][:, :], ogf[:, :], ACT.Tanh, scale=0.5).then_inc(m_gth, 1)
                act.wait_ge(m_h, h + 1)
                for v in range(2):
                    ins = A(Tm[:, v * T:(v + 1) * T], hn[v][:, :], ACT.Square)
                ins.then_inc(m_hsq, 1)
                ahead(6)
                act.wait_ge(evac_done, pn[6].n + 1)
                A(m_th[:, :], ogf[:, :], ACT.Tanh, scale=0.5).then_inc(m_gth, 1)
                act.wait_ge(m_ss, h + 1)
                A(em[:, :], B[5][:, :], ACT.Sqrt, bias=epsc[:, :], scale=1.0 / M_V).then_inc(m_rtk, 1)
                if not last:
                    ahead(7)
                else:
                    act.wait_ge(mm_done, E0)
                    for k in range(KT - 2):
                        if k >= 8:
                            act.wait_ge(m_cat, k - 7)
                        act_hi(k)
                        if k == 2:
                            act.wait_ge(evac_done, pn[7].n + 1)
                            A(m_th[:, :], ogf[:, :], ACT.Tanh, scale=0.5).then_inc(m_gth, 1)
                    return
                act.wait_ge(evac_done, pn[7].n + 1)
                A(m_th[:, :], ogf[:, :], ACT.Tanh, scale=0.5).then_inc(m_gth, 1)

            head(0, first=True)
            with act.Fori(1, M_HEADS - 1) as h:
                head(h)
            head(M_HEADS - 1, last=True)

            for k in range(KT - 2, KT):
                act.wait_ge(m_cat, k - 7)
                act_hi(k)
            split_hi(Panel(E0 + 1))
            with act.Fori(0, KT // 2 - 1) as i:
                for s in range(2):
                    act.wait_ge(mm_done, E0 + 2 * i + s + 1)
                    split_hi(Panel(E0 + 2 + s, i, 2))
            split_hi(Panel(IKW))

            act.wait_ge(mm_done, IKW)
            for k in range(KT):
                act.wait_ge(evac_done, E0 + k + 1)
                act_hi(k, G_ODD)
            split_hi(Panel(IKW + 1))

            def ahead(n):
                act.wait_ge(mm_done, n + 1)
                split_hi(Panel(n + 2))

            act.wait_ge(ss_mm, 2)
            A(rt_tmp[:, :], B[7][:, :], ACT.Sqrt, bias=epsc[:, :], scale=1.0 / D).then_inc(ss_rt, 1)
            for n in range(IKW, IKW + 3):
                ahead(n)
            act.wait_ge(iw_mm, 1)
            A(iwt[:, :, :].rearrange("p t h -> p (t h)"), B[7][:, 0:TT * C_IH], ACT.Copy,
              scale=float(C_IH) ** -0.5).then_inc(iw_ok, 1)
            for n in range(IKW + 3, CKV):
                ahead(n)
            done = 0

            def relu_scores(t):
                nonlocal done
                for h in range(C_IH):
                    act.wait_ge(isc_mm, done + 1)
                    if done >= 2 * C_IH + 4:
                        act.wait_ge(rl_used3, h - 3)
                    elif done >= 4:
                        act.wait_ge(rl_used, done - 3)
                    A(rl[done % 4][:, 0:P * (t + 1)], B[2 + done % 4][:, 0:P * (t + 1)], ACT.Relu,
                      scale=float(C_ID) ** -0.5).then_inc(rl_ok, 1)
                    done += 1

            relu_scores(1)
            for c in range(LT):
                ahead(CKV + c)
                act.wait_ge(evac_done, CKV + c + 1)
                A(latsq[:, c, :], latf[:, c, :], ACT.Square).then_inc(lsq_ok, 1)
                if c < 2:
                    relu_scores(c + 2)
            act.wait_ge(lss_mm, 1)
            A(latr[:, :], B[6][:, :], ACT.Sqrt, bias=epsc[:, :], scale=1.0 / C_LAT).then_inc(lrt_ok, 1)
            for c in range(LT):
                act.wait_ge(lat_ok, c + 1)
                A(lath[:, c, :], latf[:, c, :], ACT.Copy).then_inc(lath_ok, 1)
            act.wait_ge(ck_mm, 1)
            A(kfc[:, :], B[6][:, :], ACT.Copy)
            A(ksqc[:, :], B[6][:, :], ACT.Square).then_inc(cksq_ok, 1)
            ahead(Q0)
            act.wait_ge(evac_done, Q0 + 1)
            A(sq_c, q_c[:, :], ACT.Square).then_inc(sq_ok, 1)
            for g in range(4):
                if g == 1:
                    act.wait_ge(ckss_mm, 1)
                    A(krc[:, :], B[7][:, :], ACT.Sqrt, bias=epsc[:, :], scale=1.0 / C_DIM).then_inc(ckrt_ok, 1)
                ahead(U0 + g)
                if g == 0:
                    act.wait_ge(rl_used3, C_IH)
                for t in range(TT):
                    ins = A(V[:, t, g * T:(g + 1) * T], B[4 * (g % 2) + t][:, :], ACT.Copy)
                ins.then_inc(evac_done, 1)
            after_z(ODD, 0)
            with act.Fori(1, C_HEADS - 1) as j:
                after_q(ODD, j)
                after_z(ODD, j)
            after_q(ODD, C_HEADS - 1)
            after_z(ODD, C_HEADS - 1, last=True)

            for k in range(8, KT - 1):
                act.wait_ge(cat_ok, A_PAIRS + k + 1)
                act_hi(k)
            split_hi(Panel(F0 + 1))
            move_blocks(ODD, C_HEADS - 1)
            act.wait_ge(cat_ok, A_PAIRS + KT)
            act_hi(KT - 1)
            with act.Fori(0, KT // 2 - 1) as i:
                for s in range(2):
                    act.wait_ge(mm_done, F0 + 2 * i + s + 1)
                    split_hi(Panel(F0 + 2 + s, i, 2))

        @block.vector
        def _(dve):
            own = OwnSteps(dve, dve_own)
            V_ = nc.vector

            def split_lo(pn):
                dve.wait_ge(hi_done, pn.n + 1)
                V_.tensor_tensor(wl[pn.slot][:, :, :], raw[pn.slot][:, :, :], wh[pn.slot][:, :, :].bitcast(F32),
                                 ALU.subtract).then_inc(lo_done, 1)

            def evac(pn, out, rows_=slice(0, P), out_rows=None):
                dve.wait_ge(mm_done, pn.n + 1)
                return V_.tensor_tensor(out, B[pn.slot][rows_, :], rstd[rows_, :], ALU.mult)

            def act_lo(k, phase, gain=None):
                if phase in (1, 3) and k in POOL_TILES:
                    return
                dve.wait_ge(h_hi, KT * phase + k + 1)
                hi = hh[:, k, :].bitcast(F32)
                if gain is None:
                    ins = V_.tensor_tensor(hl[:, k, :], xs[:, k, :], hi, ALU.subtract)
                else:
                    ins = V_.scalar_tensor_tensor(hl[:, k, :], xs[:, k, :], col(gain + k), hi, ALU.mult, ALU.subtract)
                ins.then_inc(h_lo, 1)

            def after_q(u, j, first=False):
                base = A0 if u.even else O0
                pn = Panel(base, j, 2)
                if u.even:
                    evac(pn, qm[0:64, 0, :], slice(0, 64))
                    evac(pn, qm[64:128, 1, :], slice(64, 128)).then_inc(evac_done, 1)
                else:
                    evac(pn, q_c[:, :]).then_inc(evac_done, 1)
                split_lo(Panel(base + 2, j, 2))
                if not first:
                    normalise(u, j - 1)

            def normalise(u, j):
                n, OS = u.nb, os_a if u.even else os_c
                dve.wait_ge(p_ok, u_of(u, j) + 1)
                tot = sums
                if u.even:
                    own.link(V_.tensor_tensor(esink[:, 0:n], sums[:, 0:n], esink[:, 0:n], ALU.add))
                    tot = esink
                own.link(V_.reciprocal(rinv[:, 0:n], tot[:, 0:n]))
                dve.wait_ge(pv_mm, u_of(u, j) + 1)
                V_.tensor_tensor(OS[:, :].rearrange("p (b d) -> p b d", b=n),
                                 B[6][:, :].rearrange("p (b d) -> p b d", b=n),
                                 rinv[:, 0:n].unsqueeze(2).to_broadcast([P, n, u.ow]), ALU.mult).then_inc(os_ok, 1)

            def gate_out(u, j):
                dve.wait_ge(oT_mm, u_of(u, j) + 1)
                V_.scalar_tensor_tensor(xs[:, bass.ds(j, 1), :].rearrange("p a n -> p (a n)"), B[7][:, :], 0.5,
                                        (sz_a if u.even else zf_c)[:, :], ALU.mult, ALU.mult).then_inc(cat_ok, 1)

            def after_z(u, j, first=False, last=False):
                base = (A0 if u.even else O0) + 1
                S, th = (S_a, th_a) if u.even else (S_c, th_c)
                zf, sz = (zf_a, sz_a) if u.even else (zf_c, zf_c)
                n = u.nb
                if not first:
                    gate_out(u, j - 1)
                    if not u.even:
                        dve.wait_ge(cat_ok, u_of(u, j))
                evac(Panel(base, j, 2), zf[:, :]).then_inc(evac_done, 1)
                if last:
                    for k in range(POOL_TILES[0]):
                        act_lo(k, 3)
                dve.wait_ge(rtq_ok, u_of(u, j) + 1)
                own.link(V_.reciprocal(rq[:, 0:n], rtq[:, 0:n]))
                dve.wait_ge(lg_mm, u_of(u, j) + 1)
                dve.wait_ge(bias_ok, u_of(u, j) + 1)
                for b, t, h, w, bank, c, s in u.blocks:
                    own.mark(V_.scalar_tensor_tensor(S[:, s:s + w], B[bank][:, c:c + w], rq[:, b:b + 1],
                                                     bias_a[:, h, 256 - w:256] if u.even else bias_c[:, s:s + w],
                                                     ALU.mult, ALU.add))
                own.settle()
                if u.even:
                    by_block = S[:, :].rearrange("p (b n) -> p b n", b=n)
                    own.mark(V_.tensor_reduce(negm[:, 0:2], by_block[:, 0:2, 0:P], AX, ALU.max, negate=True))
                    own.link(V_.tensor_reduce(negm[:, 2:8], by_block[:, 2:8, :], AX, ALU.max, negate=True))
                    ns = nsink[:, bass.ds(8 * j, 8)]
                    V_.tensor_tensor(negm[:, :], negm[:, :], ns, ALU.min).then_inc(negm_ok, 1)
                    dve.wait_ge(negm_ok, j + 1)
                    V_.tensor_tensor(sink_arg[:, :], negm[:, :], ns, ALU.subtract).then_inc(sk_ok, 1)
                else:
                    for b, t, h, w, bank, c, s in u.blocks:
                        ins = V_.tensor_reduce(negm[:, b:b + 1], S[:, s:s + w], AX, ALU.max, negate=True)
                    ins.then_inc(negm_ok, 1)
                if not last:
                    split_lo(Panel(base + 2, j, 2))
                dve.wait_ge(th_ok, u_of(u, j) + 1)
                own.link(V_.scalar_tensor_tensor(sz[:, :], th[:, :], 1.0, zf[:, :], ALU.add, ALU.mult))

            dve.wait_ge(cols_ok, 16)
            own.mark(V_.memset(qm[0:64, 1, :], 0.0))
            own.mark(V_.memset(qm[64:128, 0, :], 0.0))
            own.mark(V_.scalar_tensor_tensor(kgain[:, 0:1], col(G_AQ), float(A_DIM) ** -0.5, col(G_AK),
                                             ALU.mult, ALU.mult))
            own.mark(V_.scalar_tensor_tensor(kgain[:, 1:2], col(G_CQ), float(C_DIM) ** -0.5, col(G_CK),
                                             ALU.mult, ALU.mult))
            own.link(V_.tensor_scalar(nsink[:, :], col(SINKS, 8 * A_PAIRS), -1.0, None, ALU.mult))
            for k in range(KT):
                act_lo(k, 0, G_EVEN)
                if k in (3, 11):
                    split_lo(Panel(k // 8))
            dve.wait_ge(x_sqp, 1)
            for c, sq in enumerate((sqx, sq4)):
                dve.wait_ge(x_sq, c + 1)
                V_.tensor_tensor(ss4[:, :, :], ss4[:, :, :], sq[:, :, :], ALU.add).then_inc(x_ss, 1)
                dve.wait_ge(x_ss, c + 1)
            dve.wait_ge(ss_rt, 1)
            own.link(V_.reciprocal(rstd[:, :], krt[:, :]))
            for p in range(2):
                evac(Panel(p), kf[p][:, :]).then_inc(evac_done, 1)
                split_lo(Panel(2 + p))
            for p in range(2):
                evac(Panel(2 + p), vf[p][:, :]).then_inc(evac_done, 1)
                split_lo(Panel(4 + p))
                dve.wait_ge(krt_ok, p + 1)
                own.link(V_.reciprocal(kn[:, :], krt[:, :]))
                own.link(V_.scalar_tensor_tensor(kn[:, :], kf[p][:, :], kgain[:, 0:1], kn[:, :], ALU.mult, ALU.mult))
                for a in range(2):
                    for b in range(2):
                        last = V_.tensor_copy(kd[64 * b:64 * b + 64, 2 * p + a, :], kn[64 * a:64 * a + 64, :])
                        own.mark(last) if (a, b) != (1, 1) else last.then_inc(kd_ok, 1)
                dve.wait_ge(kd_ok, p + 1)
            dve.wait_ge(vT_mm, 2)
            own.mark(evac(Panel(GATES), gi[:, :], slice(0, 4)))
            evac(Panel(GATES), gf[:, :], slice(32, 36)).then_inc(evac_done, 1)
            split_lo(Panel(6))
            dve.wait_ge(evac_done, GATES + 1)
            own.mark(V_.memset(g1[:, :], 1.0))
            own.mark(V_.tensor_scalar(gi[:, :], gi[:, :], cols[0:4, I_BIAS:I_BIAS + 1], None, ALU.add))
            V_.tensor_scalar(gf[:, :], gf[:, :], cols[0:4, F_BIAS:F_BIAS + 1], None, ALU.add).then_inc(gate_f, 1)
            dve.wait_ge(gate_f, 1)
            dve.wait_ge(gate_u, 1)
            own.link(V_.scalar_tensor_tensor(gf[:, :], gf[:, :], 0.0, gu[:, :], ALU.min, ALU.subtract))
            own.link(V_.tensor_tensor_scan(gb[:, :], g1[:, :], gf[:, :], 0.0, ALU.mult, ALU.add))
            V_.tensor_tensor(ga[:, :], gi[:, :], gb[:, :], ALU.subtract).then_inc(gate_a, 1)
            dve.wait_ge(gate_a, 1)
            own.link(V_.tensor_tensor_scan(rows[:, 0, :], ga[:, :], ga[:, :], 0.0, ALU.max, ALU.max))
            V_.tensor_tensor(rows[:, 1, :], gb[:, :], rows[:, 0, :], ALU.add).then_inc(gate_a, 1)
            after_q(EVEN, 0, first=True)
            dve.wait_ge(acol_mm, 1)
            after_z(EVEN, 0, first=True)

            with dve.Fori(1, A_PAIRS) as j:
                own.enter(j, 1, EVEN_STEPS)
                after_q(EVEN, j)
                after_z(EVEN, j)
            own.leave(A_PAIRS - 1)

            def head(h, first=False, last=False):
                pn = [Panel(M0 + u, h, 8) for u in range(10)]
                if first:
                    dve.wait_ge(acol_ok, 1)
                own.mark(V_.tensor_copy(hp[:, :], cols[:, bass.ds(M_PAR + 12 * h, 12)]))
                own.mark(V_.tensor_copy(acur[:, :], acol[:, bass.ds(TT * h, TT)]))
                V_.tensor_copy(selcur[:, :], const[0:4, bass.ds(IDENT + h, 1)].to_broadcast([4, P])).then_inc(m_par, 1)
                if first:
                    own.mark(V_.memset(cx[:, 0:3], 0.0))
                own.settle()
                for u, dst in ((0, qs), (1, ks)):
                    evac(pn[u], cx[:, 3:3 + T]).then_inc(evac_done, 1)
                    split_lo(pn[u + 2])
                    if first and u == 1:
                        gate_out(EVEN, A_PAIRS - 1)
                    dve.wait_ge(evac_done, pn[u].n + 1)
                    own.link(V_.tensor_scalar(cy[:, :], cx[:, 3:3 + T], hp[:, 4 * u + 3:4 * u + 4],
                                              hp[:, 8 + u:9 + u], ALU.mult, ALU.add))
                    for tap in range(3):
                        ins = V_.scalar_tensor_tensor(cy[:, :], cx[:, tap:tap + T], hp[:, 4 * u + tap:4 * u + tap + 1],
                                                      cy[:, :], ALU.mult, ALU.add)
                        own.link(ins) if tap < 2 else ins.then_inc(m_conv, 1)
                    dve.wait_ge(m_cth, 2 * h + u + 1)
                    V_.scalar_tensor_tensor(dst[:, :], cth[:, :], 1.0, cy[:, :], ALU.add, ALU.mult).then_inc(m_qk, 1)
                    if first and u == 0:
                        normalise(EVEN, A_PAIRS - 1)
                evac(pn[2], mvf[0][:, :]).then_inc(evac_done, 1)
                split_lo(pn[4])
                dve.wait_ge(m_bc, h + 1)
                for s in range(TT):
                    ins = V_.tensor_scalar(Tm[:, EOFF[s]:EOFF[s] + T - s * P], B[5][:, s * P:T], acur[:, s:s + 1], 0.0,
                                           ALU.subtract, ALU.max)
                ins.then_inc(m_T, 1)
                evac(pn[3], mvf[1][:, :]).then_inc(evac_done, 1)
                split_lo(pn[5])
                dve.wait_ge(m_st, h + 1)
                dve.wait_ge(m_sel, h + 1)
                for s, (bank, c) in enumerate([(2, 0), (3, 0), (4, 0), (3, 384)]):
                    w = T - s * P
                    e = E[:, EOFF[s]:EOFF[s] + w]
                    ins = V_.scalar_tensor_tensor(e, B[bank][:, c:c + w], 0.25 * float(M_QK) ** -0.5, e,
                                                  ALU.mult, ALU.mult)
                ins.then_inc(m_P, 1)
                for v in range(2):
                    if v:
                        dve.wait_ge(m_gth, 4 * h + 1)
                    evac(pn[4 + v], ogf[:, :]).then_inc(evac_done, 1)
                    split_lo(pn[6 + v])
                dve.wait_ge(m_num, h + 1)
                dve.wait_ge(m_em, h + 1)
                own.link(V_.tensor_tensor(dd[:, :], B[4][:, :], em[:, :], ALU.max))
                own.link(V_.scalar_tensor_tensor(dd[:, :], B[4][:, :], -1.0, dd[:, :], ALU.mult, ALU.max))
                own.link(V_.reciprocal(dd[:, :], dd[:, :]))
                for w in range(2):
                    ins = V_.tensor_tensor(hn[w][:, :], B[2 + w][:, :], dd[:, :], ALU.mult)
                    own.mark(ins) if w == 0 else ins.then_inc(m_h, 1)
                for v in range(2):
                    if v == 0:
                        dve.wait_ge(m_gth, 4 * h + 2)
                    evac(pn[6 + v], ogf[:, :]).then_inc(evac_done, 1)
                    if last and v:
                        for k in range(6):
                            act_lo(k, 1)
                    else:
                        split_lo(pn[8 + v])
                    dve.wait_ge(m_gth, 4 * h + 3 + v)
                    dve.wait_ge(evac_done, pn[6 + v].n + 1)
                    own.link(V_.scalar_tensor_tensor(G[v][:, :], m_th[:, :], 1.0, ogf[:, :], ALU.add, ALU.mult))
                    own.link(V_.scalar_tensor_tensor(G[v][:, :], tho[v][:, :], 1.0, G[v][:, :], ALU.add, ALU.mult))
                    if v == 0:
                        dve.wait_ge(m_rtk, h + 1)
                        own.link(V_.reciprocal(dd[:, :], em[:, :]))
                        for w in range(2):
                            own.link(V_.scalar_tensor_tensor(hn[w][:, :], hn[w][:, :], hp[:, 10 + w:11 + w], dd[:, :],
                                                             ALU.mult, ALU.mult))
                    V_.scalar_tensor_tensor(xs[:, bass.ds(A_PAIRS + 2 * h + v, 1), :].rearrange("p a n -> p (a n)"),
                                            hn[v][:, :], 0.25, G[v][:, :], ALU.mult, ALU.mult).then_inc(m_cat, 1)

            head(0, first=True)
            with dve.Fori(1, M_HEADS - 1) as h:
                own.enter(h, 1, HEAD_STEPS)
                head(h)
            own.leave(M_HEADS - 2)
            head(M_HEADS - 1, last=True)

            for k in range(6, KT):
                act_lo(k, 1)
            split_lo(Panel(E0 + 1))

            def even_out(i, last=False):
                for s in range(2):
                    pn = Panel(E0 + s, i, 2)
                    dve.wait_ge(mm_done, pn.n + 1)
                    dve.wait_ge(res_in[s], 16 * i + 16)
                    V_.tensor_tensor(xs[:, bass.ds(2 * i + s, 1), :].rearrange("p a n -> p (a n)"), B[pn.slot][:, :],
                                     res[s][:, :], ALU.add).then_inc(evac_done, 1)
                    if not (last and s):
                        split_lo(Panel(E0 + 2 + s, i, 2))

            with dve.Fori(0, KT // 2 - 1) as i:
                even_out(i)
            even_out(KT // 2 - 1, last=True)

            for k in range(KT):
                act_lo(k, 2, G_ODD)
            split_lo(Panel(IKW + 1))
            dve.wait_ge(ss_rt, 2)
            V_.reciprocal(rstd[:, :], rt_tmp[:, :]).then_inc(rstd_ok, 1)
            dve.wait_ge(rstd_ok, 1)
            own.mark(evac(Panel(IKW), ik[0:64, :], slice(0, 64)))
            own.mark(evac(Panel(IKW), ik[64:128, :], slice(0, 64)))
            evac(Panel(IKW), iwf[:, :], slice(64, 72)).then_inc(evac_done, 1)
            split_lo(Panel(IKW + 2))
            for p in range(4):
                evac(Panel(IQ0 + p), iq[:, p, :]).then_inc(evac_done, 1)
                split_lo(Panel(IQ0 + p + 2))
            def add_scores(t):
                w, at = P * (t + 1), SC_AT[t]
                dst = sc[:, at:at + w]
                for h in range(C_IH):
                    done = C_IH * (t - 1) + h
                    dve.wait_ge(rl_ok, done + 1)
                    src = rl[done % 4][:, 0:w]
                    if h == 0:
                        V_.tensor_scalar(dst, src, iwt[:, t, h:h + 1], None, ALU.mult).then_inc(rl_used, 1)
                    else:
                        V_.scalar_tensor_tensor(dst, src, iwt[:, t, h:h + 1], dst, ALU.mult, ALU.add)\
                            .then_inc(rl_used, 1)
                    dve.wait_ge(rl_used, done + 1)

            def take(t, rounds):
                w, at = P * (t + 1), SC_AT[t]
                dst = sc[:, at:at + w]
                nonlocal bodies
                own.settle()
                with dve.Fori(bodies + 1, bodies + 1 + rounds // UNROLL) as n:
                    for r in range(UNROLL):
                        if r:
                            dve.wait_ge(*scored[t])
                            dve.wait_ge(taken8[r - 1], n)
                        V_.max(v8[:, :], dst).then_inc(found8[r], 1)
                        dve.wait_ge(*scored[t])
                        dve.wait_ge(found8[r], n)
                        V_.match_replace(dst, v8[:, :], dst, TAKEN).then_inc(taken8[r], 1)
                    dve.wait_ge(taken8[UNROLL - 1], n)
                bodies += rounds // UNROLL

            bodies = 0
            scored = {1: (rl_used, C_IH), 2: (rl_used, 2 * C_IH), 3: (rl_used3, C_IH)}

            def hide_future(t):
                end = SC_AT[t] + P * (t + 1)
                dve.wait_ge(*scored[t])
                own.link(V_.memset(sc[0:64, end - 64:end], FUTURE))

            def make_mask(t):
                w, at = P * (t + 1), SC_AT[t]
                c = ODD.blocks[t][6]
                return V_.tensor_scalar(mask_c[:, c:c + w], sc[:, at:at + w], TAKEN * 0.9, NEG, ALU.is_gt, ALU.mult)

            dve.wait_ge(iw_ok, 1)
            dve.wait_ge(x1_out, 16 * KT)
            dve.wait_ge(h_lo, LO_BEFORE[3])
            add_scores(1)
            hide_future(1)
            for c in range(LT):
                evac(Panel(CKV + c), latf[:, c, :]).then_inc(evac_done, 1)
                if c < 3:
                    split_lo(Panel(CKV + c + 2))
                if c < 3:
                    take(1, 4)
                if c == 0:
                    add_scores(2)
                    hide_future(2)
            take(1, 4)
            dve.wait_ge(lrt_ok, 1)
            own.link(V_.reciprocal(latr[:, :], latr[:, :]))
            for c in range(LT):
                V_.scalar_tensor_tensor(latf[:, c, :], latf[:, c, :], col(G_LAT + c), latr[:, :], ALU.mult, ALU.mult)\
                    .then_inc(lat_ok, 1)
            for c in range(LT):
                dve.wait_ge(lath_ok, c + 1)
                V_.tensor_tensor(latl[:, c, :], latf[:, c, :], lath[:, c, :].bitcast(F32), ALU.subtract)\
                    .then_inc(latl_ok, 1)
            evac(Panel(Q0), q_c[:, :]).then_inc(evac_done, 1)
            take(2, 16)
            dve.wait_ge(ckrt_ok, 1)
            own.link(V_.reciprocal(krc[:, :], krc[:, :]))
            V_.scalar_tensor_tensor(kk[:, :], kfc[:, :], kgain[:, 1:2], krc[:, :], ALU.mult, ALU.mult)\
                .then_inc(kk_ok, 1)
            hide_future(3)
            take(3, 16)
            own.mark(V_.memset(mask_c[:, 0:P], 0.0))
            own.settle()
            own.mark(V_.memset(mask_c[0:64, 64:128], NEG))
            for t in range(1, TT):
                ins = make_mask(t)
                own.mark(ins) if t < TT - 1 else ins.then_inc(mask_ok, 1)
            dve.wait_ge(evac_done, O0 + 1)
            dve.wait_ge(lo_done, O0 + 3)
            after_z(ODD, 0, first=True)
            with dve.Fori(1, C_HEADS - 1) as j:
                own.enter(j, 1, ODD_STEPS)
                after_q(ODD, j)
                after_z(ODD, j)
            own.leave(C_HEADS - 2)
            after_q(ODD, C_HEADS - 1)
            after_z(ODD, C_HEADS - 1, last=True)

            act_lo(KT - 2, 3)
            split_lo(Panel(F0 + 1))
            normalise(ODD, C_HEADS - 1)
            gate_out(ODD, C_HEADS - 1)
            act_lo(KT - 1, 3)

            def odd_out(i, last=False):
                for s in range(2):
                    pn = Panel(F0 + s, i, 2)
                    dve.wait_ge(mm_done, pn.n + 1)
                    dve.wait_ge(res_in[s], 16 * (KT // 2) + 16 * i + 16)
                    if not isinstance(i, int) or i:
                        dve.wait_ge(y_out[s], 16 * i)
                    V_.tensor_tensor(yt[s][:, :], B[pn.slot][:, :], res[s][:, :], ALU.add).then_inc(evac_done, 1)
                    if not last:
                        split_lo(Panel(F0 + 2 + s, i, 2))

            odd_out(0)
            with dve.Fori(1, KT // 2 - 1) as i:
                odd_out(i)
            odd_out(KT // 2 - 1, last=True)


EVEN_STEPS = 2 + 1 + 8 + 2 + 1
ODD_STEPS = 1 + 1 + 4 + 1
HEAD_STEPS = 2 + 2 * 3 + 2 * 2 + 4 + 1 + 2


def buckets():
    rel = np.arange(NREL) - (T - 1)
    half, exact = NBUCKET // 2, NBUCKET // 4
    n = np.abs(rel)
    large = exact + (np.log(np.maximum(n, 1).astype(np.float32) / np.float32(exact))
                     / np.float32(np.log(1024 / exact)) * np.float32(half - exact)).astype(np.int32)
    return np.where(rel > 0, half, 0) + np.where(n < exact, n, np.minimum(large, half - 1))


def kernel(**inputs):
    import concourse.bacc as _bacc
    from concourse.bass_utils import run_bass_kernel_spmd as _run

    a = {k: np.asarray(v) for k, v in inputs.items()}
    f32 = np.float32

    def columns(w, c, n=P):
        return w[:, c:c + n].reshape(KT, P, n).transpose(1, 0, 2)

    we, wo = a["w_in_even"][0], a["w_in_odd"][0]
    panels = np.zeros((NPANEL, P, KT * P), f32)

    def put(n, block):
        panels[n].reshape(P, KT, P)[:, :, :block.shape[2]] = block

    for i in range(4):
        put(K0 + i, columns(we, 1024 + P * i))
    put(GATES, columns(we, 4608, 4))
    panels[GATES].reshape(P, KT, P)[:, :, 32:36] = columns(we, 4612, 4)
    for j in range(A_PAIRS):
        put(A0 + 2 * j, columns(we, P * j))
        put(A0 + 2 * j + 1, columns(we, 1536 + P * j))
    for h in range(M_HEADS):
        for u, c in enumerate([2560 + P * h, 3072 + P * h, 3584 + 256 * h, 3712 + 256 * h, 4616 + 256 * h,
                               4744 + 256 * h, 5640 + 256 * h, 5768 + 256 * h]):
            put(M0 + 8 * h + u, columns(we, c))
    iq_c = 2048 + 512
    ik_c = iq_c + C_IH * C_ID
    cz_c = ik_c + C_ID + C_IH
    put(IKW, columns(wo, ik_c, C_ID + C_IH))
    for i in range(4):
        put(IQ0 + i, columns(wo, iq_c + P * i))
        put(CKV + i, columns(wo, 2048 + P * i))
        uv = a["c_w_uv"][0][4 * i:4 * i + 4].reshape(4, LT, P, C_DIM)
        panels[U0 + i] = uv.transpose(2, 1, 0, 3).reshape(P, KT * P)
    for h in range(C_HEADS):
        put(O0 + 2 * h if h else Q0, columns(wo, P * h))
        put(O0 + 2 * h + 1, columns(wo, cz_c + P * h))
    for m in range(KT):
        put(E0 + m, columns(a["w_out_even"][0], P * m))
        put(F0 + m, columns(a["w_out_odd"][0], P * m))

    cols = np.zeros((P, NCOL), f32)
    cols[:, G_EVEN:G_EVEN + KT] = a["norm_even"][0].reshape(KT, P).T
    cols[:, G_ODD:G_ODD + KT] = a["norm_odd"][0].reshape(KT, P).T
    cols[:, G_AQ] = np.concatenate([a["a_q_norm"][0]] * 2)
    cols[:, G_AK] = np.concatenate([a["a_k_norm"][0]] * 2)
    cols[:, G_LAT:G_LAT + LT] = a["c_kv_norm"][0].reshape(LT, P).T
    cols[:, G_CQ] = a["c_q_norm"][0]
    cols[:, G_CK] = a["c_k_norm"][0]
    sinks = np.broadcast_to(a["a_sinks"][0].reshape(A_PAIRS, 1, 2), (A_PAIRS, TT, 2))
    cols[:, SINKS:SINKS + 8 * A_PAIRS] = sinks.reshape(1, -1)
    cols[0:4, I_BIAS] = a["b_i_bias"][0]
    cols[0:4, F_BIAS] = a["b_f_bias"][0]
    cw, cb = a["b_conv_w"][0], a["b_conv_b"][0]
    for h in range(M_HEADS):
        c = M_PAR + 12 * h
        for u in range(2):
            ch = slice(512 * u + P * h, 512 * u + P * h + P)
            cols[:, c + 4 * u:c + 4 * u + 4] = cw[:, ch].T
            cols[:, c + 8 + u] = cb[ch]
            cols[:, c + 10 + u] = a["b_out_norm"][0][256 * h + P * u:256 * h + P * u + P]

    const = np.zeros((P, NCONST), f32)
    const[:, IDENT:IDENT + P] = np.eye(P)
    const[0:64, BLOCK1:BLOCK1 + 64] = 1
    const[64:128, BLOCK1 + 64:BLOCK1 + 128] = 1
    const[:, ONES:ONES + P] = 1
    const[0:64, HEAD1] = 1
    const[64:128, HEAD1 + 1] = 1
    onehot = np.zeros((NBUCKET, NREL), f32)
    onehot[buckets()[:NREL - 1], np.arange(NREL - 1)] = 1

    arrays = {
        "panels": panels,
        "xT": np.ascontiguousarray(a["x"][0].T).reshape(KT, P, T),
        "cols_in": cols, "const_src": const, "onehot_in": onehot, "rel_in": np.ascontiguousarray(a["rel_bias"]),
        "wuk_src": np.ascontiguousarray(a["c_w_uk"][0].reshape(LT, P, C_DIM).transpose(1, 0, 2)),
    }
    nc = _bacc.Bacc("TRN2", target_bir_lowering=False, num_devices=1)
    t = {k: nc.dram_tensor(k, v.shape, F32, kind="ExternalInput").ap() for k, v in arrays.items()}
    outT = nc.dram_tensor("outT", (KT, P, T), F32, kind="ExternalOutput").ap()
    trunk_program(nc, t["panels"], t["xT"], t["cols_in"], t["const_src"], t["onehot_in"], t["rel_in"], t["wuk_src"],
                  outT)
    r = _run(nc, [arrays], core_ids=[0])
    got = r.results[0]["outT"].reshape(D, T)
    return np.ascontiguousarray(got.T).reshape(1, T, D)
```

```python
from contextlib import ExitStack

import numpy as np

import concourse.bass as bass
from concourse import mybir

F32 = mybir.dt.float32
F32R = mybir.dt.float32r
BF16 = mybir.dt.bfloat16
BYTES = {F32: 4, F32R: 4, BF16: 2}
ALU = mybir.AluOpType
ACT = mybir.ActivationFunctionType
AX = mybir.AxisListType.X

P = 128
D = 2048
T = 512
KT = D // P
TT = T // P
EPS = 1e-6
NEG = -1e30
POOL_TILES = range(6, 14)
MIX_ORDER = [0, 6, 1, 7, 2, 8, 3, 9, 4, 10, 5, 11, 12, 13, 14, 15]
LO_BEFORE = [0, KT, 2 * KT - len(POOL_TILES), 3 * KT - len(POOL_TILES)]
UNROLL = 4
TAKEN = -3e38
FUTURE = -1e38

A_DIM, A_PAIRS, A_KV = 64, 8, 4
M_HEADS, M_QK, M_V = 4, 128, 256
C_HEADS, C_DIM, C_LAT, C_IH, C_ID, TOPK = 16, 128, 512, 8, 64, 128
LT = C_LAT // P

K0 = 0
GATES = 4
A0 = 5
M0 = A0 + 2 * A_PAIRS
E0 = M0 + 8 * M_HEADS
IKW = E0 + KT
IQ0 = IKW + 1
CKV = IQ0 + 4
Q0 = CKV + LT
U0 = Q0 + 1
O0 = U0 + 3
F0 = O0 + 2 * C_HEADS
NPANEL = F0 + KT

NCOL = 0


def _cols(n):
    global NCOL
    NCOL += n
    return NCOL - n


G_EVEN = _cols(KT)
G_ODD = _cols(KT)
G_AQ = _cols(1)
G_AK = _cols(1)
G_LAT = _cols(LT)
G_CQ = _cols(1)
G_CK = _cols(1)
SINKS = _cols(8 * A_PAIRS)
I_BIAS = _cols(1)
F_BIAS = _cols(1)
M_PAR = _cols(12 * M_HEADS)
IDENT, HEAD1, NCONST = 0, 128, 130
NREL = 640
NBUCKET = 32


class Panel:

    def __init__(self, base, j=0, per=0):
        self.n = base + per * j
        self.slot = base % 2
        self.fills = base // 2 + (per // 2) * j + 1
        self.primed = not isinstance(self.n, int) or self.n >= 2


class OwnSteps:

    def __init__(self, eng, sem):
        self.eng, self.sem, self.base, self.k = eng, sem, 0, 0

    def mark(self, ins):
        ins.then_inc(self.sem, 1)
        self.k += 1

    def settle(self):
        self.eng.wait_ge(self.sem, self.base + self.k)

    def link(self, ins):
        self.mark(ins)
        self.settle()

    def enter(self, i, first, per):
        self.start = self.base + self.k
        self.base, self.k, self.per = self.start + (i - first) * per, 0, per

    def leave(self, count):
        assert self.k == self.per, (self.k, self.per)
        self.base, self.k = self.start + count * self.per, 0


class Unit:

    def __init__(self, even):
        self.even = even
        if even:
            self.blocks = [(2 * t + h, t, h, 256 if t else P, 2 + t, h * 256, (2 * t + h) * 256)
                           for t in range(TT) for h in range(2)]
            pv = [(b, s + k * P, t + 1 - w // P + k) for b, t, h, w, _, _, s in self.blocks for k in range(w // P)]
        else:
            place = {0: (3, 384, 0), 1: (4, 0, 128), 2: (3, 0, 384), 3: (2, 0, 768)}
            self.blocks = [(t, t, 0, P * (t + 1), *place[t]) for t in range(TT)]
            pv = [(b, s + k * P, k) for b, t, h, w, _, _, s in self.blocks for k in range(t + 1)]
        self.pv = pv
        self.nb = len(self.blocks)
        self.ow = A_DIM if even else C_DIM
        self.banks = -(-len(pv) // 4)
        self.inv_dim = 1.0 / (A_DIM if even else C_DIM)


EVEN, ODD = Unit(True), Unit(False)


def trunk_program(nc, panels, xT, cols_in, const_src, onehot_in, rel_in, wuk_src, outT):
    x1T = nc.dram_tensor("x1T", (KT, P, T), F32, kind="Internal").ap()
    tab_d = nc.dram_tensor("tab_d", (16, NREL), F32, kind="Internal").ap()
    toep_d = nc.dram_tensor("toep_d", (16, P, T), F32, kind="Internal").ap()

    top = [-(-nc.sbuf_base // 64) * 64]

    def fixed(name, shape, dt=F32):
        size = int(np.prod(shape[1:])) * BYTES[dt]
        t = nc.alloc_sbuf_tensor_at(name, shape, dt, offset=top[0])
        top[0] += -(-size // 32) * 32
        return t

    def zone(start):
        at = [start]

        def place(name, shape, dt=F32):
            size = int(np.prod(shape[1:])) * BYTES[dt]
            t = nc.alloc_sbuf_tensor_at(name, shape, dt, offset=at[0])
            at[0] += -(-size // 32) * 32
            assert at[0] <= nc.sbuf_usable_end, (name, at[0])
            return t
        place.at = at
        return place

    xs_at = top[0]
    xs = fixed("xs", [P, KT, T])
    hh = fixed("hh", [P, KT, T], F32R)
    hl = fixed("hl", [P, KT, T], F32R)
    raw = [fixed(f"raw{i}", [P, KT, P]) for i in range(2)]
    wh = [fixed(f"wh{i}", [P, KT, P], F32R) for i in range(2)]
    wl = [fixed(f"wl{i}", [P, KT, P], F32R) for i in range(2)]
    const = fixed("const", [P, NCONST])
    cols = fixed("cols", [P, NCOL])
    ones_r = fixed("ones_r", [P, P], F32R)
    rstd = fixed("rstd", [P, T])
    kgain = fixed("kgain", [P, 2])
    nsink = fixed("nsink", [P, 8 * A_PAIRS])
    epsc = fixed("epsc", [P, 1])
    rtq = fixed("rtq", [P, 8])
    rq = fixed("rq", [P, 8])
    negm = fixed("negm", [P, 8])
    sink_arg = fixed("sink_arg", [P, 8])
    sums = fixed("sums", [P, 8])
    esink = fixed("esink", [P, 8])
    rinv = fixed("rinv", [P, 8])
    iwt = fixed("iwt", [P, TT, C_IH])
    v8 = fixed("v8", [P, 8])
    region = top[0]

    za = zone(region)
    kh = za("kh", [P, A_KV, T], F32R)
    kl = za("kl", [P, A_KV, T], F32R)
    qst_at = za.at[0]
    qst = za("qst", [P, 2, T], F32R)
    qf = za("qf", [P, T])
    bias_a = za("bias_a", [P, 2, 256])
    zf_a = za("zf_a", [P, T])
    th_a = za("th_a", [P, T])
    s_at = za.at[0]
    S_a = za("S_a", [P, 8 * 256])
    pt_at = za.at[0]
    PT_a = za("PT_a", [P, 4 * T])
    sq_a = PT_a[:, 0:T]
    os_a = za("os_a", [P, T])
    vA = za("vA", [P, TT, A_KV * A_DIM])
    keep_at = za.at[0]
    wm = za("wm", [P, 256], BF16)
    rows_h = za("rows_h", [4, 2, T], F32R)
    rows_l = za("rows_l", [4, 2, T], F32R)
    acol = za("acol", [P, 16])
    hp = za("hp", [P, 12])
    acur = za("acur", [P, TT])
    selcur = za("selcur", [4, P], F32R)
    block1 = th_a[:, 0:P]
    zs = zone(qst_at)
    once = zs("once", [32, NREL])
    tab = zs("tab", [16, NREL])
    rel_sb = zs("rel_sb", [NBUCKET, 16])
    zs = zone(s_at)
    ss4 = zs("ss4", [P, 4, T])
    sq4 = zs("sq4", [P, 4, T])
    sqx = zone(region)("sqx", [P, 4, T])
    zs = zone(s_at)
    kf = [zs(f"kf{i}", [P, T]) for i in range(2)]
    vf = [zs(f"vf{i}", [P, T]) for i in range(2)]
    ksq = [zs(f"ksq{i}", [P, T]) for i in range(2)]
    krt = zs("krt", [P, T])
    kn = zs("kn", [P, T])
    zs = zone(s_at)
    gi, gf, gu, gb, g1, ga = (zs(f"g_{x}", [4, T]) for x in "ifub1a")
    rows = zs("rows", [4, 2, T])

    zm = zone(region)
    cx = zm("cx", [P, 3 + T])
    cy = zm("cy", [P, T])
    cth = zm("cth", [P, T])
    qs = zm("qs", [P, T])
    ks = zm("ks", [P, T])
    assert zm.at[0] <= region + 4 * (2 * A_KV * T)
    mvf = [zm(f"mvf{i}", [P, T]) for i in range(2)]
    tho = [zm(f"tho{i}", [P, T]) for i in range(2)]
    G = [zm(f"G{i}", [P, T]) for i in range(2)]
    em = zm("em", [P, T])
    e_at = zm.at[0]
    E = zm("E", [P, 1280])
    tm_at = zm.at[0]
    Tm = zm("Tm", [P, 1280])
    hn = [zm(f"hn{i}", [P, T]) for i in range(2)]
    vth = zm("vth", [P, TT, M_V], F32R)
    vtl = zm("vtl", [P, TT, M_V], F32R)
    assert zm.at[0] <= keep_at
    Eh = zone(tm_at)("Eh", [P, 1280], F32R)
    El = zone(e_at)("El", [P, 1280], F32R)
    dd = cy
    ogf, m_th = cx[:, 3:3 + T], cth

    zo = zone(region)
    V = zo("V", [P, TT, C_HEADS * C_DIM])
    kkh = zo("kkh", [P, T], F32R)
    kk_at = zo.at[0]
    kk = zo("kk", [P, T])
    q_c = zo("q_c", [P, T])
    zf_c = zo("zf_c", [P, T])
    s_o = zo.at[0]
    S_c = zo("S_c", [P, 1280])
    zh = zone(s_o)
    qch = zh("qch", [P, T], F32R)
    qcl = zh("qcl", [P, T], F32R)
    kkl = zone(kk_at)("kkl", [P, T], F32R)
    pt_o = zo.at[0]
    PT_c = zo("PT_c", [P, 1280])
    os_c = zo("os_c", [P, T])
    bias_c = zo("bias_c", [P, 1280])
    sq_c = PT_c[:, 0:T]
    mask_c = zo("mask_c", [P, 1280], BF16)
    th_c = os_c
    zq = zone(s_o)
    kfc = zq("kfc", [P, T])
    ksqc = zq("ksqc", [P, T])
    zq = zone(pt_o + 4 * T)
    krc = zq("krc", [P, T])
    zq = zone(region)
    iqst = zq("iqst", [P, C_IH, T], F32R)
    ikh = zq("ikh", [P, T], F32R)
    ikl = zq("ikl", [P, T], F32R)
    ik = zq("ik", [P, T])
    iwf = zq("iwf", [C_IH, T])
    rl = [zq(f"rl{i}", [P, T]) for i in range(4)]
    iqf = rl[0:2]
    assert zq.at[0] <= region + 4 * TT * C_HEADS * C_DIM
    zq = zone(s_o)
    latsq = zq("latsq", [P, LT, T])
    latr = os_c
    zx = zone(xs_at)
    lath = zx("lath", [P, LT, T], F32R)
    latl = zx("latl", [P, LT, T], F32R)
    latf = zx("latf", [P, LT, T])
    sc = zx("sc", [P, 1152])
    wuk = zx("wuk", [P, LT, C_DIM])
    assert zx.at[0] <= xs_at + 4 * KT * T
    zt = zone(region)
    res = [zt(f"res{i}", [P, T]) for i in range(2)]
    yt = [zt(f"yt{i}", [P, T]) for i in range(2)]
    ptmp = zt("ptmp", [P, T])
    ssum = zt("ssum", [P, T])
    rt_tmp = zt("rt_tmp", [P, T])
    SC_AT = {1: 0, 2: 256, 3: 640}
    EOFF = [0, 512, 896, 1152]

    ident = const[:, IDENT:IDENT + P]
    ones = ones_r[:, :].bitcast(F32)
    head1 = const[:, HEAD1:HEAD1 + 2]

    def col(c, n=1):
        return cols[:, c:c + n]

    with ExitStack() as ctx:
        B = [ctx.enter_context(nc.psum_tensor(f"B{i}", [P, T], F32)) for i in range(8)]

        def sem(name):
            return ctx.enter_context(nc.semaphore(name))

        raw_in = [sem("raw_in0"), sem("raw_in1")]
        hi_done, lo_done, mm_done, evac_done = map(sem, "hi_done lo_done mm_done evac_done".split())
        h_hi, h_lo, h_lo2 = map(sem, "h_hi h_lo h_lo2".split())
        (cols_ok, const_in, setup, tab_in, tab_mm, tab_sb, tab_out, toep_out) = map(sem, (
            "cols_ok const_in setup tab_in tab_mm tab_sb tab_out toep_out").split())
        x_sq, x_sqp, x_ss, ss_mm, ss_rt, rstd_ok = map(sem, "x_sq x_sqp x_ss ss_mm ss_rt rstd_ok".split())
        (q_hi, q_lo, kn_ok, kh_ok, kk_made, iq_hi, iq_lo, rows_hi, rows_lo) = map(sem, (
            "q_hi q_lo kn_ok kh_ok kk_made iq_hi iq_lo rows_hi rows_lo").split())
        bias_ok = sem("bias_ok")
        m_hsum, m_vL, m_Eh, m_El = map(sem, "m_hsum m_vL m_Eh m_El".split())
        x_in = [sem(f"x_in{i}") for i in range(4)]
        (ksq_ok, kss_mm, krt_ok, kd_ok, vT_mm, vA_ok, gate_f, gate_u, gate_a, acol_mm, acol_ok) = map(sem, (
            "ksq_ok kss_mm krt_ok kd_ok vT_mm vA_ok gate_f gate_u gate_a acol_mm acol_ok").split())
        (sq_ok, qss_mm, rtq_ok, lg_mm, bias_in, negm_ok, sk_ok, p_ok, pt_mm, pt_ok, pv_mm, os_ok, oT_mm, cat_ok,
         th_ok) = map(sem, ("sq_ok qss_mm rtq_ok lg_mm bias_in negm_ok sk_ok p_ok pt_mm pt_ok pv_mm os_ok oT_mm "
                            "cat_ok th_ok").split())
        (m_par, m_conv, m_cth, m_qk, m_bc, m_st, m_T, m_E, m_sel, m_P, m_vT, m_vA, m_gth, m_num, m_h, m_hsq, m_ss,
         m_rtk, m_cat, m_em) = map(sem, ("m_par m_conv m_cth m_qk m_bc m_st m_T m_E m_sel m_P m_vT m_vA m_gth m_num m_h "
                                   "m_hsq m_ss m_rtk m_cat m_em").split())
        res_in = [sem("res_in0"), sem("res_in1")]
        x1_out = sem("x1_out")
        y_out = [sem("y_out0"), sem("y_out1")]
        (iw_mm, iw_ok, isc_mm, rl_ok, rl_used, rl_used3, lsq_ok, lss_mm, lrt_ok, lat_ok, lath_ok, latl_ok, ck_mm,
         cksq_ok, ckss_mm, ckrt_ok, kk_ok, mask_ok, x1_ss, wuk_in) = map(sem, (
             "iw_mm iw_ok isc_mm rl_ok rl_used rl_used3 lsq_ok lss_mm lrt_ok lat_ok lath_ok latl_ok ck_mm "
             "cksq_ok ckss_mm ckrt_ok kk_ok mask_ok x1_ss wuk_in").split())
        found8 = [sem(f"found8_{r}") for r in range(UNROLL)]
        taken8 = [sem(f"taken8_{r}") for r in range(UNROLL)]
        dve_own, act_own, pool_own = sem("dve_own"), sem("act_own"), sem("pool_own")

        def u_of(u, j):
            return j if u.even else A_PAIRS + j

        def pt_of(u, j):
            return 4 * j if u.even else 4 * A_PAIRS + ODD.banks * j

        block = ctx.enter_context(nc.Block())

        @block.sync
        def _(sp):
            def load(pn):
                if pn.primed:
                    sp.wait_ge(lo_done, pn.n - 1)
                sp.dma_start(raw[pn.slot][:, :, :].rearrange("p k c -> p (k c)"),
                             panels[bass.ds(pn.n, 1), :, :].rearrange("a p n -> p (a n)")).then_inc(raw_in[pn.slot], 16)

            sp.dma_start(cols[:, :], cols_in).then_inc(cols_ok, 16)
            for c in range(4):
                if c < 2:
                    load(Panel(c))
                sp.dma_start(xs[:, 4 * c:4 * c + 4, :],
                             xT[4 * c:4 * c + 4, :, :].rearrange("k p n -> p k n")).then_inc(x_in[c], 16)
            sp.dma_start(const[:, :], const_src).then_inc(const_in, 16)
            with sp.Fori(1, NPANEL // 2) as i:
                load(Panel(0, i, 2))
                load(Panel(1, i, 2))

        @block.gpsimd
        def _(pool):
            own = OwnSteps(pool, pool_own)
            own.mark(pool.memset(epsc[:, :], EPS))
            own.mark(pool.memset(ones, 1.0))
            own.link(pool.memset(block1[:, :], 0.0))
            own.link(pool.memset(block1[0:64, 0:64], 1.0))
            pool.memset(block1[64:128, 64:128], 1.0).then_inc(setup, 1)
            pool.wait_ge(setup, 1)
            for c, sq in ((0, ss4), (1, sq4)):
                pool.wait_ge(x_in[c], 16)
                own.mark(pool.tensor_tensor(sq[:, :, :], xs[:, 4 * c:4 * c + 4, :], xs[:, 4 * c:4 * c + 4, :],
                                            ALU.mult))
            own.settle()
            pool.tensor_tensor(ss4[:, :, :], ss4[:, :, :], sq4[:, :, :], ALU.add).then_inc(x_sqp, 1)
            pool.dma_start(once[:, :], onehot_in).then_inc(tab_in, 16)
            pool.dma_start(rel_sb[:, :], rel_in).then_inc(tab_in, 16)
            own.link(pool.memset(wm[:, :], NEG))
            own.mark(pool.memset(wm[0:64, 64:192], 0.0))
            own.link(pool.memset(wm[64:128, 128:256], 0.0))
            pool.wait_ge(tab_sb, 1)
            pool.dma_start(tab_d, tab[:, :]).then_inc(tab_out, 16)
            pool.wait_ge(tab_out, 16)
            pool.dma_start(toep_d, bass.AP(tab_d.tensor, P - 1, [[NREL, 16], [-1, P], [1, T]])).then_inc(toep_out, 16)
            pool.wait_ge(toep_out, 16)

            def load_bias_a(j):
                pool.dma_start(bias_a[:, :, :], toep_d[bass.ds(2 * j, 2), :, 256:512].rearrange("a p n -> p a n"))\
                    .then_inc(bias_in, 16)

            def mask_bias_a(unit):
                pool.wait_ge(bias_in, 16 * unit)
                pool.tensor_tensor(bias_a[:, :, :], bias_a[:, :, :], wm[:, :].unsqueeze(1).to_broadcast([P, 2, 256]),
                                   ALU.add).then_inc(bias_ok, 1)

            load_bias_a(0)
            mask_bias_a(1)
            with pool.Fori(1, A_PAIRS) as j:
                pool.wait_ge(negm_ok, j)
                load_bias_a(j)
                mask_bias_a(j + 1)

            with pool.Fori(1, M_HEADS + 1) as made:
                pool.wait_ge(cat_ok, A_PAIRS)
                pool.wait_ge(m_E, made)
                for s in range(TT):
                    blk = E[:, EOFF[s]:EOFF[s] + P]
                    last = pool.affine_select(out=blk, in_=blk, pattern=[[1, P]], compare_op=ALU.is_ge, fill=0.0,
                                              base=0, channel_multiplier=-1)
                last.then_inc(m_sel, 1)
                pool.wait_ge(m_hsq, made)
                pool.tensor_tensor(Tm[:, 0:T], Tm[:, 0:T], Tm[:, T:2 * T], ALU.add).then_inc(m_hsum, 1)

            def act_lo2(phase):
                for k in POOL_TILES:
                    pool.wait_ge(h_hi, KT * phase + MIX_ORDER.index(k) + 1)
                    pool.tensor_tensor(hl[:, k, :], xs[:, k, :], hh[:, k, :].bitcast(F32), ALU.subtract)\
                        .then_inc(h_lo2, 1)

            act_lo2(1)

            def load_res(src, m, s):
                pool.dma_start(res[s][:, :], src[bass.ds(m, 1), :, :].rearrange("a p n -> p (a n)"))\
                    .then_inc(res_in[s], 16)

            pool.wait_ge(m_cat, 2 * M_HEADS)
            own.link(pool.memset(ssum[:, :], 0.0))
            load_res(xT, 0, 0)
            load_res(xT, 1, 1)

            def even_out(i, last=False):
                for s in range(2):
                    m = 2 * i + s
                    pool.wait_ge(evac_done, E0 + m + 1)
                    pool.dma_start(x1T[bass.ds(m, 1), :, :].rearrange("a p n -> p (a n)"),
                                   xs[:, bass.ds(m, 1), :].rearrange("p a n -> p (a n)")).then_inc(x1_out, 16)
                    if not last:
                        load_res(xT, m + 2, s)
                    tile = xs[:, bass.ds(m, 1), :].rearrange("p a n -> p (a n)")
                    own.link(pool.tensor_tensor(ptmp[:, :], tile, tile, ALU.mult))
                    add = pool.tensor_tensor(ssum[:, :], ssum[:, :], ptmp[:, :], ALU.add)
                    add.then_inc(x1_ss, 1) if last and s else own.link(add)

            with pool.Fori(0, KT // 2 - 1) as i:
                own.enter(i, 0, 4)
                even_out(i)
            own.leave(KT // 2 - 1)
            even_out(KT // 2 - 1, last=True)
            pool.wait_ge(x1_out, 16 * KT)
            pool.wait_ge(h_lo, LO_BEFORE[3])
            pool.dma_start(wuk[:, :, :], wuk_src).then_inc(wuk_in, 16)

            def load_bias_c(h):
                for b, t, _, w, _, _, c in ODD.blocks:
                    pool.dma_start(bias_c[:, c:c + w], toep_d[bass.ds(h, 1), :, T - w:T].rearrange("a p n -> p (a n)"))\
                        .then_inc(bias_in, 16)

            def mask_bias_c(h):
                pool.wait_ge(bias_in, 16 * A_PAIRS + 64 * h + 64)
                pool.tensor_tensor(bias_c[:, :], bias_c[:, :], mask_c[:, :], ALU.add).then_inc(bias_ok, 1)

            load_bias_c(0)
            pool.wait_ge(iw_ok, 1)
            t = TT - 1
            dst = sc[:, SC_AT[t]:SC_AT[t] + T]
            for h in range(C_IH):
                pool.wait_ge(rl_ok, C_IH * 2 + h + 1)
                r = rl[h % 4][:, :]
                if h % 2 == 0:
                    weight = iwt[:, t, h:h + 1].to_broadcast([P, T])
                    ins = pool.tensor_tensor(r if h else dst, r, weight, ALU.mult)
                if h == 0:
                    ins.then_inc(rl_used3, 1)
                else:
                    if h % 2 == 0:
                        own.link(ins)
                    pool.tensor_tensor(dst, dst, r, ALU.add).then_inc(rl_used3, 1)
                pool.wait_ge(rl_used3, h + 1)
            pool.wait_ge(lo_done, U0)
            for n in range(U0, O0 + 3):
                pool.wait_ge(hi_done, n + 1)
                pool.tensor_tensor(wl[n % 2][:, :, :], raw[n % 2][:, :, :], wh[n % 2][:, :, :].bitcast(F32),
                                   ALU.subtract).then_inc(lo_done, 1)
            pool.wait_ge(mask_ok, 1)
            mask_bias_c(0)
            with pool.Fori(1, C_HEADS) as h:
                pool.wait_ge(negm_ok, A_PAIRS + h)
                load_bias_c(h)
                mask_bias_c(h)
            act_lo2(3)

            pool.wait_ge(pv_mm, A_PAIRS + C_HEADS)
            load_res(x1T, 0, 0)
            load_res(x1T, 1, 1)

            def odd_out(i, last=False):
                for s in range(2):
                    m = 2 * i + s
                    pool.wait_ge(evac_done, F0 + m + 1)
                    pool.dma_start(outT[bass.ds(m, 1), :, :].rearrange("a p n -> p (a n)"), yt[s][:, :])\
                        .then_inc(y_out[s], 16)
                    if not last:
                        load_res(x1T, m + 2, s)

            with pool.Fori(0, KT // 2 - 1) as i:
                odd_out(i)
            odd_out(KT // 2 - 1, last=True)
            pool.wait_ge(y_out[0], 16 * KT // 2)
            pool.wait_ge(y_out[1], 16 * KT // 2)

        @block.tensor
        def _(pe):
            def mm(out, lhsT, rhs, start=True, stop=True):
                return nc.tensor.matmul(out, lhsT, rhs, start=start, stop=stop)

            def wait_low(phase, k):
                if phase in (1, 3) and k in POOL_TILES:
                    pe.wait_ge(h_lo2, len(POOL_TILES) * (phase // 2) + POOL_TILES.index(k) + 1)
                else:
                    mine = k if phase in (0, 2) or k < POOL_TILES[0] else k - len(POOL_TILES)
                    pe.wait_ge(h_lo, LO_BEFORE[phase] + mine + 1)

            def main_panel(pn, conv=None, between=None, tiles=range(KT)):
                if tiles[0] == 0:
                    pe.wait_ge(lo_done, pn.n + 1)
                    if pn.primed:
                        pe.wait_ge(evac_done, pn.n - 1)
                acc, w1, w2 = B[pn.slot], wh[pn.slot], wl[pn.slot]
                for k in tiles:
                    if between and k in between:
                        between[k]()
                    if conv is not None:
                        at = MIX_ORDER.index(k) if conv in (1, 3) else k
                        pe.wait_ge(h_hi, KT * conv + at + 1)
                    mm(acc[:, :], w1[:, k, :], hh[:, k, :], k == 0, False)
                    mm(acc[:, :], w2[:, k, :], hh[:, k, :], False, False)
                    if conv is not None:
                        wait_low(conv, k)
                    last = mm(acc[:, :], w1[:, k, :], hl[:, k, :], False, k == KT - 1)
                if tiles[-1] == KT - 1:
                    last.then_inc(mm_done, 1)

            def transpose4(bank, src, rows_=P):
                for t in range(TT):
                    last = nc.tensor.transpose(bank[:, t * P:t * P + rows_], src[:, t * P:(t + 1) * P],
                                               ident[0:rows_, 0:rows_])
                return last

            def logits(u, j):
                sq = sq_a if u.even else sq_c
                pe.wait_ge(sq_ok, u_of(u, j) + 1)
                for t in range(TT):
                    w = 2 if u.even else 1
                    last = mm(B[6][:, w * t:w * t + w], sq[:, t * P:(t + 1) * P],
                              head1 if u.even else ones[:, 0:1])
                last.then_inc(qss_mm, 1)
                pe.wait_ge(q_lo, u_of(u, j) + 1)
                for b, t, h, w, bank, c, _ in u.blocks:
                    dst = B[bank][:, c:c + w]
                    tok = slice(t * P, (t + 1) * P)
                    if u.even:
                        keys = bass.ds((j // 2) * T + (t + 1) * P - w, w)
                        mm(dst, qst[:, h, tok], kh[:, :, :].rearrange("p g n -> p (g n)")[:, keys], True, False)
                        last = mm(dst, qst[:, h, tok], kl[:, :, :].rearrange("p g n -> p (g n)")[:, keys], False, True)
                    else:
                        mm(dst, qch[:, tok], kkh[:, 0:w], True, False)
                        mm(dst, qch[:, tok], kkl[:, 0:w], False, False)
                        last = mm(dst, qcl[:, tok], kkh[:, 0:w], False, True)
                last.then_inc(lg_mm, 1)

            def transpose_weights(u, j):
                S = S_a if u.even else S_c
                pe.wait_ge(p_ok, u_of(u, j) + 1)
                n = len(u.pv)
                for i, (b, s, _) in enumerate(u.pv):
                    last = nc.tensor.transpose(B[2 + i // 4][:, (i % 4) * P:(i % 4 + 1) * P], S[:, s:s + P], ident)
                    if i % 4 == 3 or i == n - 1:
                        last.then_inc(pt_mm, 1)

            def weighted_values(u, j):
                PT, n = PT_a if u.even else PT_c, len(u.pv)
                for i, (b, _, vt) in enumerate(u.pv):
                    if i % 4 == 0:
                        pe.wait_ge(pt_ok, pt_of(u, j) + i // 4 + 1)
                    if u.even:
                        rhs = vA[:, vt, bass.ds((j // 2) * A_DIM, A_DIM)]
                    else:
                        rhs = V[:, vt, bass.ds(j * C_DIM, C_DIM)]
                    last = mm(B[6][:, b * u.ow:(b + 1) * u.ow], PT[:, i * P:(i + 1) * P], rhs,
                              i == 0 or u.pv[i - 1][0] != b, i == n - 1 or u.pv[i + 1][0] != b)
                last.then_inc(pv_mm, 1)

            def rest_of_unit(u, j):
                return {0: lambda: transpose_weights(u, j), 6: lambda: weighted_values(u, j),
                        12: lambda: outputs(u, j)}

            def outputs(u, j):
                pe.wait_ge(os_ok, u_of(u, j) + 1)
                transpose4(B[7], os_a if u.even else os_c).then_inc(oT_mm, 1)

            def bias_table():
                pe.wait_ge(tab_in, 32)
                mm(B[2][0:16, 0:512], rel_sb[:, :], once[:, 0:512])
                mm(B[3][0:16, 0:NREL - 512], rel_sb[:, :], once[:, 512:NREL]).then_inc(tab_mm, 1)

            def sum_squares():
                pe.wait_ge(const_in, 16)
                pe.wait_ge(setup, 1)
                pe.wait_ge(x_ss, 2)
                for k in range(4):
                    last = mm(B[7][:, :], ones, ss4[:, k, :], k == 0, k == 3)
                last.then_inc(ss_mm, 1)

            main_panel(Panel(0), conv=0)
            main_panel(Panel(1), between={6: sum_squares, 12: bias_table})
            main_panel(Panel(2))
            pe.wait_ge(tab_sb, 1)
            for p in range(2):
                pe.wait_ge(ksq_ok, p + 1)
                mm(B[2 + p][:, :], block1, ksq[p][:, :]).then_inc(kss_mm, 1)
            main_panel(Panel(3))
            pe.wait_ge(evac_done, 3)
            transpose4(B[4], vf[0]).then_inc(vT_mm, 1)
            main_panel(Panel(4))
            pe.wait_ge(evac_done, 4)
            transpose4(B[5], vf[1]).then_inc(vT_mm, 1)
            def gate_columns():
                pe.wait_ge(gate_a, 1)
                for t in range(TT):
                    last = nc.tensor.transpose(B[7][:, 4 * t:4 * t + 4], ga[:, t * P:(t + 1) * P], ident[0:4, 0:4])
                last.then_inc(acol_mm, 1)

            main_panel(Panel(5))
            main_panel(Panel(6), between={13: gate_columns})
            pe.wait_ge(kd_ok, 2)
            pe.wait_ge(vA_ok, 2)
            logits(EVEN, 0)

            def unit(u, base, j):
                main_panel(Panel(base, j, 2))
                main_panel(Panel(base + 1, j, 2), between=rest_of_unit(u, j - 1))
                logits(u, j)

            pe.wait_ge(acol_ok, 1)
            with pe.Fori(1, A_PAIRS) as j:
                unit(EVEN, A0, j)

            def head(h, first=False):
                pn = [Panel(M0 + u, h, 8) for u in range(8)]
                main_panel(pn[0])
                main_panel(pn[1], between=rest_of_unit(EVEN, A_PAIRS - 1) if first else None)
                main_panel(pn[2])
                pe.wait_ge(m_par, h + 1)
                if first:
                    pe.wait_ge(rows_lo, 1)
                for i in range(2):
                    mm(B[5 + i][:, :], selcur[:, :], rows_h[:, i, :], True, False)
                    last = mm(B[5 + i][:, :], selcur[:, :], rows_l[:, i, :], False, True)
                last.then_inc(m_bc, 1)
                pe.wait_ge(m_qk, 2 * h + 2)
                for s, (bank, c) in enumerate([(2, 0), (3, 0), (4, 0), (3, 384)]):
                    last = mm(B[bank][:, c:c + T - s * P], ks[:, s * P:(s + 1) * P], qs[:, s * P:T])
                last.then_inc(m_st, 1)
                main_panel(pn[3])
                if first:
                    pe.wait_ge(cat_ok, A_PAIRS)
                pe.wait_ge(evac_done, pn[2].n + 1)
                transpose4(B[7], mvf[0]).then_inc(m_vT, 1)
                main_panel(pn[4])
                pe.wait_ge(evac_done, pn[3].n + 1)
                pe.wait_ge(m_vL, 2 * h + 1)
                transpose4(B[7], mvf[1]).then_inc(m_vT, 1)
                main_panel(pn[5])
                pe.wait_ge(m_vL, 2 * h + 2)
                pe.wait_ge(m_El, h + 1)
                for v in range(2):
                    for s in range(TT):
                        e, dst, vs = slice(EOFF[s], EOFF[s] + T - s * P), B[2 + v][:, s * P:T], slice(v * P, v * P + P)
                        mm(dst, vth[:, s, vs], Eh[:, e], s == 0, False)
                        mm(dst, vth[:, s, vs], El[:, e], False, False)
                        mm(dst, vtl[:, s, vs], Eh[:, e], False, s == TT - 1)
                for s in range(TT):
                    e = slice(EOFF[s], EOFF[s] + T - s * P)
                    mm(B[4][:, s * P:T], ones_r[:, :], Eh[:, e], s == 0, False)
                    last = mm(B[4][:, s * P:T], ones_r[:, :], El[:, e], False, s == TT - 1)
                last.then_inc(m_num, 1)
                main_panel(pn[6])

                def head_squares():
                    pe.wait_ge(m_hsum, h + 1)
                    mm(B[5][:, :], ones, Tm[:, 0:T]).then_inc(m_ss, 1)

                main_panel(pn[7], between={2: head_squares})

            head(0, first=True)
            with pe.Fori(1, M_HEADS) as h:
                head(h)

            main_panel(Panel(E0), conv=1, tiles=MIX_ORDER)
            main_panel(Panel(E0 + 1))
            with pe.Fori(1, KT // 2) as i:
                main_panel(Panel(E0, i, 2))
                main_panel(Panel(E0 + 1, i, 2))

            main_panel(Panel(IKW), conv=2)
            pe.wait_ge(x1_ss, 1)
            mm(B[7][:, :], ones, ssum[:, :]).then_inc(ss_mm, 1)
            main_panel(Panel(IKW + 1))
            main_panel(Panel(IKW + 2))
            pe.wait_ge(evac_done, IKW + 1)
            pe.wait_ge(ss_rt, 2)
            for t in range(TT):
                last = nc.tensor.transpose(B[7][:, C_IH * t:C_IH * (t + 1)], iwf[:, t * P:(t + 1) * P],
                                           ident[0:C_IH, 0:C_IH])
            last.then_inc(iw_mm, 1)
            main_panel(Panel(IKW + 3))
            main_panel(Panel(IKW + 4))
            done = 0

            def index_scores(t, half):
                nonlocal done
                pe.wait_ge(iq_lo, 5)
                w = P * (t + 1)
                for h in range(4 * half, 4 * half + 4):
                    if done >= 4:
                        pe.wait_ge(rl_ok, done - 3)
                    dst, tok = B[2 + done % 4][:, 0:w], slice(t * P, (t + 1) * P)
                    mm(dst, iqst[:, h, tok], ikh[:, 0:w], True, False)
                    mm(dst, iqst[:, h, tok], ikl[:, 0:w], False, True).then_inc(isc_mm, 1)
                    done += 1

            for c in range(3):
                main_panel(Panel(CKV + c), between={9: lambda: index_scores(c + 1, 0),
                                                    14: lambda: index_scores(c + 1, 1)})
            main_panel(Panel(CKV + 3))

            def latent_squares():
                pe.wait_ge(lsq_ok, LT)
                for c in range(LT):
                    last = mm(B[6][:, :], ones, latsq[:, c, :], c == 0, c == LT - 1)
                last.then_inc(lss_mm, 1)

            main_panel(Panel(Q0), between={3: latent_squares})
            pe.wait_ge(wuk_in, 16)
            pe.wait_ge(lat_ok, LT)
            for c in range(LT):
                last = mm(B[6][:, :], wuk[:, c, :], latf[:, c, :], c == 0, c == LT - 1)
            last.then_inc(ck_mm, 1)

            for g in range(4):
                pn = Panel(U0 + g)
                pe.wait_ge(lo_done, pn.n + 1)
                if g == 0:
                    pe.wait_ge(latl_ok, LT)
                    pe.wait_ge(evac_done, U0)
                    pe.wait_ge(rl_ok, 3 * C_IH)
                if g == 1:
                    pe.wait_ge(cksq_ok, 1)
                    mm(B[7][:, :], ones, ksqc[:, :]).then_inc(ckss_mm, 1)
                if g >= 2:
                    pe.wait_ge(evac_done, pn.n - 1)
                w1 = wh[pn.slot][:, :, :].rearrange("p (c a) n -> p c (a n)", c=LT)
                w2 = wl[pn.slot][:, :, :].rearrange("p (c a) n -> p c (a n)", c=LT)
                for t in range(TT):
                    if (g, t) == (1, 3):
                        pe.wait_ge(ckrt_ok, 1)
                    dst = B[4 * (g % 2) + t][:, :]
                    tok = slice(t * P, (t + 1) * P)
                    for c in range(LT):
                        mm(dst, lath[:, c, tok], w1[:, c, :], c == 0, False)
                        mm(dst, lath[:, c, tok], w2[:, c, :], False, False)
                        last = mm(dst, latl[:, c, tok], w1[:, c, :], False, c == LT - 1)
                last.then_inc(mm_done, 1)
            main_panel(Panel(O0 + 1))
            pe.wait_ge(evac_done, O0 + 1)
            pe.wait_ge(kk_ok, 1)
            logits(ODD, 0)

            with pe.Fori(1, C_HEADS) as j:
                unit(ODD, O0, j)

            main_panel(Panel(F0), conv=3, tiles=MIX_ORDER[:-2])
            main_panel(Panel(F0 + 1), tiles=range(KT - 2), between={
                4: lambda: transpose_weights(ODD, C_HEADS - 1), 7: lambda: weighted_values(ODD, C_HEADS - 1),
                10: lambda: outputs(ODD, C_HEADS - 1), 12: lambda: main_panel(Panel(F0), conv=3, tiles=[KT - 2, KT - 1])})
            main_panel(Panel(F0 + 1), tiles=[KT - 2, KT - 1])
            with pe.Fori(1, KT // 2) as i:
                main_panel(Panel(F0, i, 2))
                main_panel(Panel(F0 + 1, i, 2))

        @block.scalar
        def _(act):
            own = OwnSteps(act, act_own)
            A = nc.scalar.activation

            def split_hi(pn):
                act.wait_ge(raw_in[pn.slot], 16 * pn.fills)
                if pn.primed:
                    act.wait_ge(mm_done, pn.n - 1)
                A(wh[pn.slot][:, :, :], raw[pn.slot][:, :, :], ACT.Copy).then_inc(hi_done, 1)

            def act_hi(k, gain=None):
                A(hh[:, k, :], xs[:, k, :], ACT.Copy, scale=col(gain + k) if gain is not None else 1.0)\
                    .then_inc(h_hi, 1)

            def after_q(u, j, first=False):
                pn = Panel(A0 if u.even else O0, j, 2)
                act.wait_ge(mm_done, pn.n + 1)
                if not first:
                    move_blocks(u, j - 1)
                split_hi(Panel((A0 if u.even else O0) + 2, j, 2))
                act.wait_ge(evac_done, pn.n + 1)
                if u.even:
                    for h in range(2):
                        r = slice(64 * h, 64 * h + 64)
                        ins = A(qst[r, h, :], qf[r, :], ACT.Copy)
                    ins.then_inc(q_hi, 1)
                    if not first:
                        act.wait_ge(pv_mm, j)
                    A(sq_a, qf[:, :], ACT.Square).then_inc(sq_ok, 1)
                else:
                    A(qch[:, :], q_c[:, :], ACT.Copy).then_inc(q_hi, 1)
                    act.wait_ge(pv_mm, u_of(u, j))
                    A(sq_c, q_c[:, :], ACT.Square).then_inc(sq_ok, 1)

            def move_blocks(u, j):
                PT = PT_a if u.even else PT_c
                for i in range(u.banks):
                    act.wait_ge(pt_mm, pt_of(u, j) + i + 1)
                    w = min(T, P * len(u.pv) - i * T)
                    A(PT[:, i * T:i * T + w], B[2 + i][:, 0:w], ACT.Copy).then_inc(pt_ok, 1)

            def after_z(u, j, last=False):
                base = (A0 if u.even else O0) + 1
                S, zf, th = (S_a, zf_a, th_a) if u.even else (S_c, zf_c, th_c)
                n = 8 if u.even else 4
                act.wait_ge(qss_mm, u_of(u, j) + 1)
                A(rtq[:, 0:n], B[6][:, 0:n], ACT.Sqrt, bias=epsc[:, :], scale=u.inv_dim).then_inc(rtq_ok, 1)
                if not last:
                    split_hi(Panel(base + 2, j, 2))
                else:
                    for i, k in enumerate(MIX_ORDER[:KT - 1]):
                        act.wait_ge(cat_ok, A_PAIRS + k + 1)
                        act_hi(k)
                        if i == 9:
                            split_hi(Panel(F0 + 1))
                act.wait_ge(evac_done, Panel(base, j, 2).n + 1)
                A(th[:, :], zf[:, :], ACT.Tanh, scale=0.5).then_inc(th_ok, 1)
                act.wait_ge(negm_ok, u_of(u, j) + 1)
                for b, t, h, w, _, _, s in u.blocks:
                    ins = A(S[:, s:s + w], S[:, s:s + w], ACT.Exp, bias=negm[:, b:b + 1],
                            accum_out=sums[:, b:b + 1])
                if u.even:
                    act.wait_ge(sk_ok, j + 1)
                    ins = A(esink[:, :], sink_arg[:, :], ACT.Exp)
                ins.then_inc(p_ok, 1)

            act.wait_ge(setup, 1)
            A(rtq[:, 0:1], epsc[:, :], ACT.Copy)
            act.wait_ge(cols_ok, 16)
            for c in range(4):
                if c == 0:
                    split_hi(Panel(0))
                act.wait_ge(x_in[c], 16)
                for k in range(4 * c, 4 * c + 4):
                    act_hi(k, G_EVEN)
                if c == 2:
                    split_hi(Panel(1))
            A(sqx[:, :, :], xs[:, 8:12, :], ACT.Square).then_inc(x_sq, 1)
            act.wait_ge(x_sqp, 1)
            A(sq4[:, :, :], xs[:, 12:16, :], ACT.Square).then_inc(x_sq, 1)
            split_hi(Panel(2))
            act.wait_ge(ss_mm, 1)
            A(krt[:, :], B[7][:, :], ACT.Sqrt, bias=epsc[:, :], scale=1.0 / D).then_inc(ss_rt, 1)
            act.wait_ge(tab_mm, 1)
            A(tab[:, 0:512], B[2][0:16, :], ACT.Copy)
            A(tab[:, 512:NREL], B[3][0:16, 0:NREL - 512], ACT.Copy).then_inc(tab_sb, 1)
            for p in range(2):
                if p:
                    split_hi(Panel(3))
                act.wait_ge(evac_done, p + 1)
                A(ksq[p][:, :], kf[p][:, :], ACT.Square).then_inc(ksq_ok, 1)
            for p in range(2):
                split_hi(Panel(4 + p))
                act.wait_ge(kss_mm, p + 1)
                A(krt[:, :], B[2 + p][:, :], ACT.Sqrt, bias=epsc[:, :], scale=1.0 / A_DIM).then_inc(krt_ok, 1)
                act.wait_ge(kn_ok, p + 1)
                for a in range(2):
                    for b in range(2):
                        ins = A(kh[64 * b:64 * b + 64, 2 * p + a, :], kn[64 * a:64 * a + 64, :], ACT.Copy)
                ins.then_inc(kh_ok, 1)
            for p in range(2):
                act.wait_ge(vT_mm, p + 1)
                A(vA[:, :, p * P:(p + 1) * P], B[4 + p][:, :].rearrange("p (t d) -> p t d", t=TT),
                  ACT.Copy).then_inc(vA_ok, 1)
            split_hi(Panel(6))
            act.wait_ge(gate_f, 1)
            own.link(A(gu[:, :], gf[:, :], ACT.Abs))
            own.link(A(gu[:, :], gu[:, :], ACT.Exp, scale=-1.0))
            A(gu[:, :], gu[:, :], ACT.Ln, bias=ones[0:4, 0:1]).then_inc(gate_u, 1)
            act.wait_ge(gate_a, 2)
            A(rows_h[:, :, :], rows[:, :, :], ACT.Copy).then_inc(rows_hi, 1)
            after_q(EVEN, 0, first=True)
            act.wait_ge(acol_mm, 1)
            A(acol[:, :].rearrange("p (h t) -> p t h", t=TT), B[7][:, 0:16].rearrange("p (t h) -> p t h", t=TT),
              ACT.Copy).then_inc(acol_ok, 1)
            after_z(EVEN, 0)

            with act.Fori(1, A_PAIRS) as j:
                after_q(EVEN, j)
                after_z(EVEN, j)

            def head(h, first=False, last=False):
                pn = [Panel(M0 + u, h, 8) for u in range(10)]

                def ahead(u):
                    act.wait_ge(mm_done, pn[u].n + 1)
                    split_hi(pn[u + 2])

                for u in range(2):
                    ahead(u)
                    if first and u == 0:
                        move_blocks(EVEN, A_PAIRS - 1)
                    act.wait_ge(m_conv, 2 * h + u + 1)
                    A(cth[:, :], cy[:, :], ACT.Tanh, scale=0.5).then_inc(m_cth, 1)
                ahead(2)
                act.wait_ge(m_bc, h + 1)
                A(em[:, :], B[6][:, :], ACT.Exp, scale=-1.0).then_inc(m_em, 1)
                act.wait_ge(m_T, h + 1)
                for s in range(TT):
                    c = slice(EOFF[s], EOFF[s] + T - s * P)
                    ins = A(E[:, c], Tm[:, c], ACT.Exp, scale=-1.0)
                ins.then_inc(m_E, 1)
                for v in range(2):
                    ahead(3 + v)
                    if v:
                        act.wait_ge(evac_done, pn[4].n + 1)
                        A(tho[0][:, :], ogf[:, :], ACT.Tanh, scale=0.5).then_inc(m_gth, 1)
                    act.wait_ge(m_vT, 2 * h + v + 1)
                    A(vth[:, :, v * P:(v + 1) * P], B[7][:, :].rearrange("p (t d) -> p t d", t=TT),
                      ACT.Copy).then_inc(m_vA, 1)
                    if v == 0:
                        act.wait_ge(m_P, h + 1)
                        A(Eh[:, :], E[:, :], ACT.Copy).then_inc(m_Eh, 1)
                ahead(5)
                act.wait_ge(evac_done, pn[5].n + 1)
                A(tho[1][:, :], ogf[:, :], ACT.Tanh, scale=0.5).then_inc(m_gth, 1)
                act.wait_ge(m_h, h + 1)
                for v in range(2):
                    ins = A(Tm[:, v * T:(v + 1) * T], hn[v][:, :], ACT.Square)
                ins.then_inc(m_hsq, 1)
                ahead(6)
                act.wait_ge(evac_done, pn[6].n + 1)
                A(m_th[:, :], ogf[:, :], ACT.Tanh, scale=0.5).then_inc(m_gth, 1)
                act.wait_ge(m_ss, h + 1)
                A(em[:, :], B[5][:, :], ACT.Sqrt, bias=epsc[:, :], scale=1.0 / M_V).then_inc(m_rtk, 1)
                if not last:
                    ahead(7)
                else:
                    act.wait_ge(mm_done, E0)
                    for k in MIX_ORDER[:KT - 2]:
                        if k >= 8:
                            act.wait_ge(m_cat, k - 7)
                        act_hi(k)
                        if k == 7:
                            act.wait_ge(evac_done, pn[7].n + 1)
                            A(m_th[:, :], ogf[:, :], ACT.Tanh, scale=0.5).then_inc(m_gth, 1)
                    return
                act.wait_ge(evac_done, pn[7].n + 1)
                A(m_th[:, :], ogf[:, :], ACT.Tanh, scale=0.5).then_inc(m_gth, 1)

            head(0, first=True)
            with act.Fori(1, M_HEADS - 1) as h:
                head(h)
            head(M_HEADS - 1, last=True)

            for k in range(KT - 2, KT):
                act.wait_ge(m_cat, k - 7)
                act_hi(k)
            split_hi(Panel(E0 + 1))
            with act.Fori(0, KT // 2 - 1) as i:
                for s in range(2):
                    act.wait_ge(mm_done, E0 + 2 * i + s + 1)
                    split_hi(Panel(E0 + 2 + s, i, 2))
            split_hi(Panel(IKW))

            act.wait_ge(mm_done, IKW)
            for k in range(KT):
                act.wait_ge(evac_done, E0 + k + 1)
                act_hi(k, G_ODD)
            split_hi(Panel(IKW + 1))

            def ahead(n):
                act.wait_ge(mm_done, n + 1)
                split_hi(Panel(n + 2))

            act.wait_ge(ss_mm, 2)
            A(rt_tmp[:, :], B[7][:, :], ACT.Sqrt, bias=epsc[:, :], scale=1.0 / D).then_inc(ss_rt, 1)

            def index_hi(n):
                act.wait_ge(evac_done, n + 1)
                if n == IKW:
                    ins = A(ikh[:, :], ik[:, :], ACT.Copy)
                else:
                    for h in range(2):
                        r = slice(64 * h, 64 * h + 64)
                        ins = A(iqst[r, 2 * (n - IQ0) + h, :], iqf[(n - IQ0) % 2][r, :], ACT.Copy)
                ins.then_inc(iq_hi, 1)

            for n in range(IKW, IKW + 3):
                ahead(n)
                index_hi(n)
            act.wait_ge(iw_mm, 1)
            A(iwt[:, :, :].rearrange("p t h -> p (t h)"), B[7][:, 0:TT * C_IH], ACT.Copy,
              scale=float(C_IH) ** -0.5).then_inc(iw_ok, 1)
            for n in range(IKW + 3, CKV):
                ahead(n)
                index_hi(n)
            done = 0

            def relu_scores(t):
                nonlocal done
                for h in range(C_IH):
                    act.wait_ge(isc_mm, done + 1)
                    if done >= 2 * C_IH + 4:
                        act.wait_ge(rl_used3, h - 3)
                    elif done >= 4:
                        act.wait_ge(rl_used, done - 3)
                    relu = A(rl[done % 4][:, 0:P * (t + 1)], B[2 + done % 4][:, 0:P * (t + 1)], ACT.Relu,
                             scale=float(C_ID) ** -0.5)
                    if t == 3 and h % 2:
                        own.link(relu)
                        relu = A(rl[done % 4][:, :], rl[done % 4][:, :], ACT.Copy, scale=iwt[:, t, h:h + 1])
                    relu.then_inc(rl_ok, 1)
                    done += 1

            relu_scores(1)
            for c in range(LT):
                ahead(CKV + c)
                act.wait_ge(evac_done, CKV + c + 1)
                A(latsq[:, c, :], latf[:, c, :], ACT.Square).then_inc(lsq_ok, 1)
                if c < 2:
                    relu_scores(c + 2)
            act.wait_ge(lss_mm, 1)
            A(latr[:, :], B[6][:, :], ACT.Sqrt, bias=epsc[:, :], scale=1.0 / C_LAT).then_inc(lrt_ok, 1)
            for c in range(LT):
                act.wait_ge(lat_ok, c + 1)
                A(lath[:, c, :], latf[:, c, :], ACT.Copy).then_inc(lath_ok, 1)
            act.wait_ge(ck_mm, 1)
            A(kfc[:, :], B[6][:, :], ACT.Copy)
            A(ksqc[:, :], B[6][:, :], ACT.Square).then_inc(cksq_ok, 1)
            ahead(Q0)
            act.wait_ge(evac_done, Q0 + 1)
            A(sq_c, q_c[:, :], ACT.Square).then_inc(sq_ok, 1)
            for g in range(4):
                if g == 1:
                    act.wait_ge(ckss_mm, 1)
                    A(krc[:, :], B[7][:, :], ACT.Sqrt, bias=epsc[:, :], scale=1.0 / C_DIM).then_inc(ckrt_ok, 1)
                ahead(U0 + g)
                if g == 0:
                    act.wait_ge(rl_used3, C_IH)
                for t in range(TT):
                    ins = A(V[:, t, g * T:(g + 1) * T], B[4 * (g % 2) + t][:, :], ACT.Copy)
                ins.then_inc(evac_done, 1)
                if g == 2:
                    act.wait_ge(kk_made, 1)
                    A(kkh[:, :], kk[:, :], ACT.Copy)
                    A(qch[:, :], q_c[:, :], ACT.Copy).then_inc(q_hi, 1)
            after_z(ODD, 0)
            with act.Fori(1, C_HEADS - 1) as j:
                after_q(ODD, j)
                after_z(ODD, j)
            after_q(ODD, C_HEADS - 1)
            after_z(ODD, C_HEADS - 1, last=True)

            move_blocks(ODD, C_HEADS - 1)
            act.wait_ge(cat_ok, A_PAIRS + KT)
            act_hi(KT - 1)
            with act.Fori(0, KT // 2 - 1) as i:
                for s in range(2):
                    act.wait_ge(mm_done, F0 + 2 * i + s + 1)
                    split_hi(Panel(F0 + 2 + s, i, 2))

        @block.vector
        def _(dve):
            own = OwnSteps(dve, dve_own)
            V_ = nc.vector

            def split_lo(pn):
                dve.wait_ge(hi_done, pn.n + 1)
                V_.tensor_tensor(wl[pn.slot][:, :, :], raw[pn.slot][:, :, :], wh[pn.slot][:, :, :].bitcast(F32),
                                 ALU.subtract).then_inc(lo_done, 1)

            def evac(pn, out, rows_=slice(0, P), out_rows=None):
                dve.wait_ge(mm_done, pn.n + 1)
                return V_.tensor_tensor(out, B[pn.slot][rows_, :], rstd[rows_, :], ALU.mult)

            def act_lo(k, phase, gain=None):
                if phase in (1, 3) and k in POOL_TILES:
                    return
                dve.wait_ge(h_hi, KT * phase + (MIX_ORDER.index(k) if phase in (1, 3) else k) + 1)
                hi = hh[:, k, :].bitcast(F32)
                if gain is None:
                    ins = V_.tensor_tensor(hl[:, k, :], xs[:, k, :], hi, ALU.subtract)
                else:
                    ins = V_.scalar_tensor_tensor(hl[:, k, :], xs[:, k, :], col(gain + k), hi, ALU.mult, ALU.subtract)
                ins.then_inc(h_lo, 1)

            def after_q(u, j, first=False):
                base = A0 if u.even else O0
                pn = Panel(base, j, 2)
                if u.even:
                    evac(pn, qf[:, :]).then_inc(evac_done, 1)
                else:
                    evac(pn, q_c[:, :]).then_inc(evac_done, 1)
                split_lo(Panel(base + 2, j, 2))
                if u.even:
                    dve.wait_ge(q_hi, j + 1)
                    for h in range(2):
                        r, o = slice(64 * h, 64 * h + 64), slice(64 - 64 * h, 128 - 64 * h)
                        ins = V_.tensor_tensor(qst[o, h, :], qf[r, :], qst[r, h, :].bitcast(F32), ALU.subtract)
                    ins.then_inc(q_lo, 1)
                else:
                    dve.wait_ge(q_hi, u_of(u, j) + 1)
                    V_.tensor_tensor(qcl[:, :], q_c[:, :], qch[:, :].bitcast(F32), ALU.subtract).then_inc(q_lo, 1)
                if not first:
                    normalise(u, j - 1)

            def normalise(u, j):
                n, OS = u.nb, os_a if u.even else os_c
                dve.wait_ge(p_ok, u_of(u, j) + 1)
                tot = sums
                if u.even:
                    own.link(V_.tensor_tensor(esink[:, 0:n], sums[:, 0:n], esink[:, 0:n], ALU.add))
                    tot = esink
                own.link(V_.reciprocal(rinv[:, 0:n], tot[:, 0:n]))
                dve.wait_ge(pv_mm, u_of(u, j) + 1)
                V_.tensor_tensor(OS[:, :].rearrange("p (b d) -> p b d", b=n),
                                 B[6][:, :].rearrange("p (b d) -> p b d", b=n),
                                 rinv[:, 0:n].unsqueeze(2).to_broadcast([P, n, u.ow]), ALU.mult).then_inc(os_ok, 1)

            def gate_out(u, j):
                dve.wait_ge(oT_mm, u_of(u, j) + 1)
                V_.scalar_tensor_tensor(xs[:, bass.ds(j, 1), :].rearrange("p a n -> p (a n)"), B[7][:, :], 0.5,
                                        (zf_a if u.even else zf_c)[:, :], ALU.mult, ALU.mult).then_inc(cat_ok, 1)

            def after_z(u, j, first=False, last=False):
                base = (A0 if u.even else O0) + 1
                S, th = (S_a, th_a) if u.even else (S_c, th_c)
                zf = zf_a if u.even else zf_c
                n = u.nb
                if not first:
                    gate_out(u, j - 1)
                    dve.wait_ge(cat_ok, u_of(u, j))
                evac(Panel(base, j, 2), zf[:, :]).then_inc(evac_done, 1)
                if last:
                    for k in range(POOL_TILES[0]):
                        act_lo(k, 3)
                    split_lo(Panel(F0 + 1))
                dve.wait_ge(rtq_ok, u_of(u, j) + 1)
                own.link(V_.reciprocal(rq[:, 0:n], rtq[:, 0:n]))
                dve.wait_ge(lg_mm, u_of(u, j) + 1)
                dve.wait_ge(bias_ok, u_of(u, j) + 1)
                for b, t, h, w, bank, c, s in u.blocks:
                    own.mark(V_.scalar_tensor_tensor(S[:, s:s + w], B[bank][:, c:c + w], rq[:, b:b + 1],
                                                     bias_a[:, h, 256 - w:256] if u.even else bias_c[:, s:s + w],
                                                     ALU.mult, ALU.add))
                own.settle()
                if u.even:
                    by_block = S[:, :].rearrange("p (b n) -> p b n", b=n)
                    own.mark(V_.tensor_reduce(negm[:, 0:2], by_block[:, 0:2, 0:P], AX, ALU.max, negate=True))
                    own.link(V_.tensor_reduce(negm[:, 2:8], by_block[:, 2:8, :], AX, ALU.max, negate=True))
                    ns = nsink[:, bass.ds(8 * j, 8)]
                    V_.tensor_tensor(negm[:, :], negm[:, :], ns, ALU.min).then_inc(negm_ok, 1)
                    dve.wait_ge(negm_ok, j + 1)
                    V_.tensor_tensor(sink_arg[:, :], negm[:, :], ns, ALU.subtract).then_inc(sk_ok, 1)
                else:
                    for b, t, h, w, bank, c, s in u.blocks:
                        ins = V_.tensor_reduce(negm[:, b:b + 1], S[:, s:s + w], AX, ALU.max, negate=True)
                    ins.then_inc(negm_ok, 1)
                if not last:
                    split_lo(Panel(base + 2, j, 2))
                dve.wait_ge(th_ok, u_of(u, j) + 1)
                own.link(V_.scalar_tensor_tensor(zf[:, :], th[:, :], 1.0, zf[:, :], ALU.add, ALU.mult))

            dve.wait_ge(cols_ok, 16)
            own.mark(V_.scalar_tensor_tensor(kgain[:, 0:1], col(G_AQ), float(A_DIM) ** -0.5, col(G_AK),
                                             ALU.mult, ALU.mult))
            own.mark(V_.scalar_tensor_tensor(kgain[:, 1:2], col(G_CQ), float(C_DIM) ** -0.5, col(G_CK),
                                             ALU.mult, ALU.mult))
            own.link(V_.tensor_scalar(nsink[:, :], col(SINKS, 8 * A_PAIRS), -1.0, None, ALU.mult))
            split_lo(Panel(0))
            for k in range(KT):
                act_lo(k, 0, G_EVEN)
                if k == 11:
                    split_lo(Panel(1))
            dve.wait_ge(x_sqp, 1)
            for c, sq in enumerate((sqx, sq4)):
                dve.wait_ge(x_sq, c + 1)
                V_.tensor_tensor(ss4[:, :, :], ss4[:, :, :], sq[:, :, :], ALU.add).then_inc(x_ss, 1)
                dve.wait_ge(x_ss, c + 1)
            split_lo(Panel(2))
            dve.wait_ge(ss_rt, 1)
            own.link(V_.reciprocal(rstd[:, :], krt[:, :]))
            for p in range(2):
                evac(Panel(p), kf[p][:, :]).then_inc(evac_done, 1)
            split_lo(Panel(3))
            for p in range(2):
                evac(Panel(2 + p), vf[p][:, :]).then_inc(evac_done, 1)
                split_lo(Panel(4 + p))
                dve.wait_ge(krt_ok, p + 1)
                own.link(V_.reciprocal(kn[:, :], krt[:, :]))
                V_.scalar_tensor_tensor(kn[:, :], kf[p][:, :], kgain[:, 0:1], kn[:, :], ALU.mult, ALU.mult)\
                    .then_inc(kn_ok, 1)
                dve.wait_ge(kh_ok, p + 1)
                for a in range(2):
                    r, g = slice(64 * a, 64 * a + 64), 2 * p + a
                    for b in range(2):
                        last = V_.tensor_tensor(kl[64 * b:64 * b + 64, g, :], kn[r, :], kh[r, g, :].bitcast(F32),
                                                ALU.subtract)
                        own.mark(last) if (a, b) != (1, 1) else last.then_inc(kd_ok, 1)
                dve.wait_ge(kd_ok, p + 1)
            dve.wait_ge(vT_mm, 2)
            own.mark(evac(Panel(GATES), gi[:, :], slice(0, 4)))
            evac(Panel(GATES), gf[:, :], slice(32, 36)).then_inc(evac_done, 1)
            split_lo(Panel(6))
            dve.wait_ge(evac_done, GATES + 1)
            own.mark(V_.memset(g1[:, :], 1.0))
            own.mark(V_.tensor_scalar(gi[:, :], gi[:, :], cols[0:4, I_BIAS:I_BIAS + 1], None, ALU.add))
            V_.tensor_scalar(gf[:, :], gf[:, :], cols[0:4, F_BIAS:F_BIAS + 1], None, ALU.add).then_inc(gate_f, 1)
            dve.wait_ge(gate_f, 1)
            dve.wait_ge(gate_u, 1)
            own.link(V_.scalar_tensor_tensor(gf[:, :], gf[:, :], 0.0, gu[:, :], ALU.min, ALU.subtract))
            own.link(V_.tensor_tensor_scan(gb[:, :], g1[:, :], gf[:, :], 0.0, ALU.mult, ALU.add))
            V_.tensor_tensor(ga[:, :], gi[:, :], gb[:, :], ALU.subtract).then_inc(gate_a, 1)
            dve.wait_ge(gate_a, 1)
            own.link(V_.tensor_tensor_scan(rows[:, 0, :], ga[:, :], ga[:, :], 0.0, ALU.max, ALU.max))
            V_.tensor_tensor(rows[:, 1, :], gb[:, :], rows[:, 0, :], ALU.add).then_inc(gate_a, 1)
            dve.wait_ge(rows_hi, 1)
            V_.tensor_tensor(rows_l[:, :, :], rows[:, :, :], rows_h[:, :, :].bitcast(F32), ALU.subtract)\
                .then_inc(rows_lo, 1)
            dve.wait_ge(tab_out, 16)
            after_q(EVEN, 0, first=True)
            dve.wait_ge(acol_mm, 1)
            after_z(EVEN, 0, first=True)

            with dve.Fori(1, A_PAIRS) as j:
                own.enter(j, 1, EVEN_STEPS)
                after_q(EVEN, j)
                after_z(EVEN, j)
            own.leave(A_PAIRS - 1)

            def head(h, first=False, last=False):
                pn = [Panel(M0 + u, h, 8) for u in range(10)]
                if first:
                    dve.wait_ge(acol_ok, 1)
                own.mark(V_.tensor_copy(hp[:, :], cols[:, bass.ds(M_PAR + 12 * h, 12)]))
                own.mark(V_.tensor_copy(acur[:, :], acol[:, bass.ds(TT * h, TT)]))
                V_.tensor_copy(selcur[:, :], const[0:4, bass.ds(IDENT + h, 1)].to_broadcast([4, P])).then_inc(m_par, 1)
                if first:
                    own.mark(V_.memset(cx[:, 0:3], 0.0))
                own.settle()
                for u, dst in ((0, qs), (1, ks)):
                    evac(pn[u], cx[:, 3:3 + T]).then_inc(evac_done, 1)
                    split_lo(pn[u + 2])
                    if first and u == 1:
                        gate_out(EVEN, A_PAIRS - 1)
                    dve.wait_ge(evac_done, pn[u].n + 1)
                    own.link(V_.tensor_scalar(cy[:, :], cx[:, 3:3 + T], hp[:, 4 * u + 3:4 * u + 4],
                                              hp[:, 8 + u:9 + u], ALU.mult, ALU.add))
                    for tap in range(3):
                        ins = V_.scalar_tensor_tensor(cy[:, :], cx[:, tap:tap + T], hp[:, 4 * u + tap:4 * u + tap + 1],
                                                      cy[:, :], ALU.mult, ALU.add)
                        own.link(ins) if tap < 2 else ins.then_inc(m_conv, 1)
                    dve.wait_ge(m_cth, 2 * h + u + 1)
                    V_.scalar_tensor_tensor(dst[:, :], cth[:, :], 1.0, cy[:, :], ALU.add, ALU.mult).then_inc(m_qk, 1)
                    if first and u == 0:
                        normalise(EVEN, A_PAIRS - 1)
                evac(pn[2], mvf[0][:, :]).then_inc(evac_done, 1)
                split_lo(pn[4])
                dve.wait_ge(m_bc, h + 1)
                for s in range(TT):
                    ins = V_.tensor_scalar(Tm[:, EOFF[s]:EOFF[s] + T - s * P], B[5][:, s * P:T], acur[:, s:s + 1], 0.0,
                                           ALU.subtract, ALU.max)
                ins.then_inc(m_T, 1)
                evac(pn[3], mvf[1][:, :]).then_inc(evac_done, 1)
                split_lo(pn[5])
                dve.wait_ge(m_st, h + 1)
                dve.wait_ge(m_sel, h + 1)
                for s, (bank, c) in enumerate([(2, 0), (3, 0), (4, 0), (3, 384)]):
                    w = T - s * P
                    e = E[:, EOFF[s]:EOFF[s] + w]
                    ins = V_.scalar_tensor_tensor(e, B[bank][:, c:c + w], 0.25 * float(M_QK) ** -0.5, e,
                                                  ALU.mult, ALU.mult)
                ins.then_inc(m_P, 1)

                def v_low(v):
                    dve.wait_ge(m_vA, 2 * h + v + 1)
                    V_.tensor_tensor(vtl[:, :, v * P:(v + 1) * P], B[7][:, :].rearrange("p (t d) -> p t d", t=TT),
                                     vth[:, :, v * P:(v + 1) * P].bitcast(F32), ALU.subtract).then_inc(m_vL, 1)

                v_low(0)
                dve.wait_ge(m_Eh, h + 1)
                V_.tensor_tensor(El[:, :], E[:, :], Eh[:, :].bitcast(F32), ALU.subtract).then_inc(m_El, 1)
                for v in range(2):
                    if v:
                        dve.wait_ge(m_gth, 4 * h + 1)
                    evac(pn[4 + v], ogf[:, :]).then_inc(evac_done, 1)
                    split_lo(pn[6 + v])
                    if v == 0:
                        v_low(1)
                dve.wait_ge(m_num, h + 1)
                dve.wait_ge(m_em, h + 1)
                own.link(V_.tensor_tensor(dd[:, :], B[4][:, :], em[:, :], ALU.max))
                own.link(V_.scalar_tensor_tensor(dd[:, :], B[4][:, :], -1.0, dd[:, :], ALU.mult, ALU.max))
                own.link(V_.reciprocal(dd[:, :], dd[:, :]))
                for w in range(2):
                    ins = V_.tensor_tensor(hn[w][:, :], B[2 + w][:, :], dd[:, :], ALU.mult)
                    own.mark(ins) if w == 0 else ins.then_inc(m_h, 1)
                for v in range(2):
                    if v == 0:
                        dve.wait_ge(m_gth, 4 * h + 2)
                    evac(pn[6 + v], ogf[:, :]).then_inc(evac_done, 1)
                    if last and v:
                        for k in range(6):
                            act_lo(k, 1)
                    else:
                        split_lo(pn[8 + v])
                    dve.wait_ge(m_gth, 4 * h + 3 + v)
                    dve.wait_ge(evac_done, pn[6 + v].n + 1)
                    own.link(V_.scalar_tensor_tensor(G[v][:, :], m_th[:, :], 1.0, ogf[:, :], ALU.add, ALU.mult))
                    own.link(V_.scalar_tensor_tensor(G[v][:, :], tho[v][:, :], 1.0, G[v][:, :], ALU.add, ALU.mult))
                    if v == 0:
                        dve.wait_ge(m_rtk, h + 1)
                        own.link(V_.reciprocal(dd[:, :], em[:, :]))
                        for w in range(2):
                            own.link(V_.scalar_tensor_tensor(hn[w][:, :], hn[w][:, :], hp[:, 10 + w:11 + w], dd[:, :],
                                                             ALU.mult, ALU.mult))
                    V_.scalar_tensor_tensor(xs[:, bass.ds(A_PAIRS + 2 * h + v, 1), :].rearrange("p a n -> p (a n)"),
                                            hn[v][:, :], 0.25, G[v][:, :], ALU.mult, ALU.mult).then_inc(m_cat, 1)

            head(0, first=True)
            with dve.Fori(1, M_HEADS - 1) as h:
                own.enter(h, 1, HEAD_STEPS)
                head(h)
            own.leave(M_HEADS - 2)
            head(M_HEADS - 1, last=True)

            for k in range(6, KT):
                act_lo(k, 1)
            split_lo(Panel(E0 + 1))

            def even_out(i, last=False):
                for s in range(2):
                    pn = Panel(E0 + s, i, 2)
                    dve.wait_ge(mm_done, pn.n + 1)
                    dve.wait_ge(res_in[s], 16 * i + 16)
                    V_.tensor_tensor(xs[:, bass.ds(2 * i + s, 1), :].rearrange("p a n -> p (a n)"), B[pn.slot][:, :],
                                     res[s][:, :], ALU.add).then_inc(evac_done, 1)
                    if not (last and s):
                        split_lo(Panel(E0 + 2 + s, i, 2))

            with dve.Fori(0, KT // 2 - 1) as i:
                even_out(i)
            even_out(KT // 2 - 1, last=True)

            for k in range(KT):
                act_lo(k, 2, G_ODD)
            split_lo(Panel(IKW + 1))
            dve.wait_ge(ss_rt, 2)
            V_.reciprocal(rstd[:, :], rt_tmp[:, :]).then_inc(rstd_ok, 1)
            dve.wait_ge(rstd_ok, 1)
            own.mark(evac(Panel(IKW), ik[0:64, :], slice(0, 64)))
            own.mark(evac(Panel(IKW), ik[64:128, :], slice(0, 64)))
            evac(Panel(IKW), iwf[:, :], slice(64, 72)).then_inc(evac_done, 1)
            split_lo(Panel(IKW + 2))
            dve.wait_ge(iq_hi, 1)
            V_.tensor_tensor(ikl[:, :], ik[:, :], ikh[:, :].bitcast(F32), ALU.subtract).then_inc(iq_lo, 1)
            for p in range(4):
                if p >= 2:
                    dve.wait_ge(iq_lo, p)
                evac(Panel(IQ0 + p), iqf[p % 2][:, :]).then_inc(evac_done, 1)
                split_lo(Panel(IQ0 + p + 2))
                dve.wait_ge(iq_hi, p + 2)
                for i in range(2):
                    r, o, h = slice(64 * i, 64 * i + 64), slice(64 - 64 * i, 128 - 64 * i), 2 * p + i
                    ins = V_.tensor_tensor(iqst[o, h, :], iqf[p % 2][r, :], iqst[r, h, :].bitcast(F32), ALU.subtract)
                ins.then_inc(iq_lo, 1)
            def add_scores(t):
                w, at = P * (t + 1), SC_AT[t]
                dst = sc[:, at:at + w]
                for h in range(C_IH):
                    done = C_IH * (t - 1) + h
                    dve.wait_ge(rl_ok, done + 1)
                    src = rl[done % 4][:, 0:w]
                    if h == 0:
                        V_.tensor_scalar(dst, src, iwt[:, t, h:h + 1], None, ALU.mult).then_inc(rl_used, 1)
                    else:
                        V_.scalar_tensor_tensor(dst, src, iwt[:, t, h:h + 1], dst, ALU.mult, ALU.add)\
                            .then_inc(rl_used, 1)
                    dve.wait_ge(rl_used, done + 1)

            def take(t, rounds):
                w, at = P * (t + 1), SC_AT[t]
                dst = sc[:, at:at + w]
                nonlocal bodies
                own.settle()
                with dve.Fori(bodies + 1, bodies + 1 + rounds // UNROLL) as n:
                    for r in range(UNROLL):
                        if r:
                            dve.wait_ge(*scored[t])
                            dve.wait_ge(taken8[r - 1], n)
                        V_.max(v8[:, :], dst).then_inc(found8[r], 1)
                        dve.wait_ge(*scored[t])
                        dve.wait_ge(found8[r], n)
                        V_.match_replace(dst, v8[:, :], dst, TAKEN).then_inc(taken8[r], 1)
                    dve.wait_ge(taken8[UNROLL - 1], n)
                bodies += rounds // UNROLL
                found_of[t] += 8 * rounds

            bodies, found_of = 0, [0] * TT
            scored = {1: (rl_used, C_IH), 2: (rl_used, 2 * C_IH), 3: (rl_used3, C_IH)}

            def hide_future(t):
                end = SC_AT[t] + P * (t + 1)
                dve.wait_ge(*scored[t])
                own.link(V_.memset(sc[0:64, end - 64:end], FUTURE))

            def make_mask(t):
                w, at = P * (t + 1), SC_AT[t]
                c = ODD.blocks[t][6]
                return V_.tensor_scalar(mask_c[:, c:c + w], sc[:, at:at + w], TAKEN * 0.9, NEG, ALU.is_gt, ALU.mult)

            dve.wait_ge(iw_ok, 1)
            dve.wait_ge(x1_out, 16 * KT)
            dve.wait_ge(h_lo, LO_BEFORE[3])
            add_scores(1)
            hide_future(1)
            for c in range(LT):
                evac(Panel(CKV + c), latf[:, c, :]).then_inc(evac_done, 1)
                if c < 3:
                    split_lo(Panel(CKV + c + 2))
                if c < 3:
                    take(1, 4)
                if c == 0:
                    add_scores(2)
                    hide_future(2)
            take(1, 4)
            dve.wait_ge(lrt_ok, 1)
            own.link(V_.reciprocal(latr[:, :], latr[:, :]))
            for c in range(LT):
                V_.scalar_tensor_tensor(latf[:, c, :], latf[:, c, :], col(G_LAT + c), latr[:, :], ALU.mult, ALU.mult)\
                    .then_inc(lat_ok, 1)
            for c in range(LT):
                dve.wait_ge(lath_ok, c + 1)
                V_.tensor_tensor(latl[:, c, :], latf[:, c, :], lath[:, c, :].bitcast(F32), ALU.subtract)\
                    .then_inc(latl_ok, 1)
            evac(Panel(Q0), q_c[:, :]).then_inc(evac_done, 1)
            take(2, 16)
            dve.wait_ge(ckrt_ok, 1)
            own.link(V_.reciprocal(krc[:, :], krc[:, :]))
            V_.scalar_tensor_tensor(kk[:, :], kfc[:, :], kgain[:, 1:2], krc[:, :], ALU.mult, ALU.mult)\
                .then_inc(kk_made, 1)
            hide_future(3)
            take(3, 12)
            dve.wait_ge(q_hi, A_PAIRS + 1)
            V_.tensor_tensor(kkl[:, :], kk[:, :], kkh[:, :].bitcast(F32), ALU.subtract).then_inc(kk_ok, 1)
            V_.tensor_tensor(qcl[:, :], q_c[:, :], qch[:, :].bitcast(F32), ALU.subtract).then_inc(q_lo, 1)
            take(3, 4)
            assert found_of[1:] == [TOPK] * (TT - 1)
            own.mark(V_.memset(mask_c[:, 0:P], 0.0))
            own.settle()
            own.mark(V_.memset(mask_c[0:64, 64:128], NEG))
            for t in range(1, TT):
                ins = make_mask(t)
                own.mark(ins) if t < TT - 1 else ins.then_inc(mask_ok, 1)
            dve.wait_ge(evac_done, O0 + 1)
            dve.wait_ge(lo_done, O0 + 3)
            after_z(ODD, 0, first=True)
            with dve.Fori(1, C_HEADS - 1) as j:
                own.enter(j, 1, ODD_STEPS)
                after_q(ODD, j)
                after_z(ODD, j)
            own.leave(C_HEADS - 2)
            after_q(ODD, C_HEADS - 1)
            after_z(ODD, C_HEADS - 1, last=True)

            act_lo(KT - 2, 3)
            normalise(ODD, C_HEADS - 1)
            gate_out(ODD, C_HEADS - 1)
            act_lo(KT - 1, 3)

            def odd_out(i, last=False):
                for s in range(2):
                    pn = Panel(F0 + s, i, 2)
                    dve.wait_ge(mm_done, pn.n + 1)
                    dve.wait_ge(res_in[s], 16 * (KT // 2) + 16 * i + 16)
                    if not isinstance(i, int) or i:
                        dve.wait_ge(y_out[s], 16 * i)
                    V_.tensor_tensor(yt[s][:, :], B[pn.slot][:, :], res[s][:, :], ALU.add).then_inc(evac_done, 1)
                    if not last:
                        split_lo(Panel(F0 + 2 + s, i, 2))

            odd_out(0)
            with dve.Fori(1, KT // 2 - 1) as i:
                odd_out(i)
            odd_out(KT // 2 - 1, last=True)


EVEN_STEPS = 2 + 1 + 8 + 2 + 1
ODD_STEPS = 1 + 1 + 4 + 1
HEAD_STEPS = 2 + 2 * 3 + 2 * 2 + 4 + 1 + 2


def buckets():
    rel = np.arange(NREL) - (T - 1)
    half, exact = NBUCKET // 2, NBUCKET // 4
    n = np.abs(rel)
    large = exact + (np.log(np.maximum(n, 1).astype(np.float32) / np.float32(exact))
                     / np.float32(np.log(1024 / exact)) * np.float32(half - exact)).astype(np.int32)
    return np.where(rel > 0, half, 0) + np.where(n < exact, n, np.minimum(large, half - 1))


def kernel(**inputs):
    import concourse.bacc as _bacc
    from concourse.bass_utils import run_bass_kernel_spmd as _run

    a = {k: np.asarray(v) for k, v in inputs.items()}
    f32 = np.float32

    def columns(w, c, n=P):
        return w[:, c:c + n].reshape(KT, P, n).transpose(1, 0, 2)

    we, wo = a["w_in_even"][0], a["w_in_odd"][0]
    panels = np.zeros((NPANEL, P, KT * P), f32)

    def put(n, block):
        panels[n].reshape(P, KT, P)[:, :, :block.shape[2]] = block

    for i in range(4):
        put(K0 + i, columns(we, 1024 + P * i))
    put(GATES, columns(we, 4608, 4))
    panels[GATES].reshape(P, KT, P)[:, :, 32:36] = columns(we, 4612, 4)
    for j in range(A_PAIRS):
        put(A0 + 2 * j, columns(we, P * j))
        put(A0 + 2 * j + 1, columns(we, 1536 + P * j))
    for h in range(M_HEADS):
        for u, c in enumerate([2560 + P * h, 3072 + P * h, 3584 + 256 * h, 3712 + 256 * h, 4616 + 256 * h,
                               4744 + 256 * h, 5640 + 256 * h, 5768 + 256 * h]):
            put(M0 + 8 * h + u, columns(we, c))
    iq_c = 2048 + 512
    ik_c = iq_c + C_IH * C_ID
    cz_c = ik_c + C_ID + C_IH
    put(IKW, columns(wo, ik_c, C_ID + C_IH))
    for i in range(4):
        put(IQ0 + i, columns(wo, iq_c + P * i))
        put(CKV + i, columns(wo, 2048 + P * i))
        uv = a["c_w_uv"][0][4 * i:4 * i + 4].reshape(4, LT, P, C_DIM)
        panels[U0 + i] = uv.transpose(2, 1, 0, 3).reshape(P, KT * P)
    for h in range(C_HEADS):
        put(O0 + 2 * h if h else Q0, columns(wo, P * h))
        put(O0 + 2 * h + 1, columns(wo, cz_c + P * h))
    for m in range(KT):
        put(E0 + m, columns(a["w_out_even"][0], P * m))
        put(F0 + m, columns(a["w_out_odd"][0], P * m))

    cols = np.zeros((P, NCOL), f32)
    cols[:, G_EVEN:G_EVEN + KT] = a["norm_even"][0].reshape(KT, P).T
    cols[:, G_ODD:G_ODD + KT] = a["norm_odd"][0].reshape(KT, P).T
    cols[:, G_AQ] = np.concatenate([a["a_q_norm"][0]] * 2)
    cols[:, G_AK] = np.concatenate([a["a_k_norm"][0]] * 2)
    cols[:, G_LAT:G_LAT + LT] = a["c_kv_norm"][0].reshape(LT, P).T
    cols[:, G_CQ] = a["c_q_norm"][0]
    cols[:, G_CK] = a["c_k_norm"][0]
    sinks = np.broadcast_to(a["a_sinks"][0].reshape(A_PAIRS, 1, 2), (A_PAIRS, TT, 2))
    cols[:, SINKS:SINKS + 8 * A_PAIRS] = sinks.reshape(1, -1)
    cols[0:4, I_BIAS] = a["b_i_bias"][0]
    cols[0:4, F_BIAS] = a["b_f_bias"][0]
    cw, cb = a["b_conv_w"][0], a["b_conv_b"][0]
    for h in range(M_HEADS):
        c = M_PAR + 12 * h
        for u in range(2):
            ch = slice(512 * u + P * h, 512 * u + P * h + P)
            cols[:, c + 4 * u:c + 4 * u + 4] = cw[:, ch].T
            cols[:, c + 8 + u] = cb[ch]
            cols[:, c + 10 + u] = a["b_out_norm"][0][256 * h + P * u:256 * h + P * u + P]

    const = np.zeros((P, NCONST), f32)
    const[:, IDENT:IDENT + P] = np.eye(P)
    const[0:64, HEAD1] = 1
    const[64:128, HEAD1 + 1] = 1
    onehot = np.zeros((NBUCKET, NREL), f32)
    onehot[buckets()[:NREL - 1], np.arange(NREL - 1)] = 1

    arrays = {
        "panels": panels,
        "xT": np.ascontiguousarray(a["x"][0].T).reshape(KT, P, T),
        "cols_in": cols, "const_src": const, "onehot_in": onehot, "rel_in": np.ascontiguousarray(a["rel_bias"]),
        "wuk_src": np.ascontiguousarray(a["c_w_uk"][0].reshape(LT, P, C_DIM).transpose(1, 0, 2)),
    }
    nc = _bacc.Bacc("TRN2", target_bir_lowering=False, num_devices=1)
    t = {k: nc.dram_tensor(k, v.shape, F32, kind="ExternalInput").ap() for k, v in arrays.items()}
    outT = nc.dram_tensor("outT", (KT, P, T), F32, kind="ExternalOutput").ap()
    trunk_program(nc, t["panels"], t["xT"], t["cols_in"], t["const_src"], t["onehot_in"], t["rel_in"], t["wuk_src"],
                  outT)
    r = _run(nc, [arrays], core_ids=[0])
    got = r.results[0]["outT"].reshape(D, T)
    return np.ascontiguousarray(got.T).reshape(1, T, D)
```
